# Optimizing a Trainium2 kernel written in Bass

```python
import math
import jax, jax.numpy as jnp
from jax import lax
import numpy as np

D_MODEL = 1024
BATCH = 1
SEQ = 2048
DEPTH = 1

MIX_WIDTH = D_MODEL
CONV_WIDTH = MIX_WIDTH // 2
SSM_WIDTH = MIX_WIDTH - CONV_WIDTH
CONV_KERNEL = 31
SSM_GROUP = 16
SSM_GROUPS = SSM_WIDTH // SSM_GROUP
SSM_STATE = 64
IN_COLS = 2 * CONV_WIDTH + SSM_WIDTH
FFN_HIDDEN = ((8 * D_MODEL + 3 * 256 - 1) // (3 * 256)) * 256
DT_MIN = 1e-3
DT_MAX = 1e-1
NORM_EPS = 1e-6

kernel_name = "hybrid_conformer_s5_parallel_encoder"

def rms_norm(x, g):
    xf = x.astype(jnp.float32)
    y = xf * lax.rsqrt(jnp.mean(xf * xf, axis=-1, keepdims=True) + NORM_EPS)
    return (y * g.astype(jnp.float32)).astype(x.dtype)

def layer_norm(x, g, b):
    xf = x.astype(jnp.float32)
    mu = jnp.mean(xf, axis=-1, keepdims=True)
    var = jnp.mean(jnp.square(xf - mu), axis=-1, keepdims=True)
    y = (xf - mu) * lax.rsqrt(var + NORM_EPS)
    return (y * g.astype(jnp.float32) + b.astype(jnp.float32)).astype(x.dtype)

def depthwise_conv(h, w, b):
    c = h.shape[-1]
    y = lax.conv_general_dilated(
        h, w[:, None, :].astype(h.dtype), window_strides=(1,),
        padding=[(CONV_KERNEL // 2, CONV_KERNEL // 2)],
        dimension_numbers=("NWC", "WIO", "NWC"), feature_group_count=c)
    return y + b.astype(h.dtype)

def _linear_combine(e1, e2):
    a1, b1 = e1
    a2, b2 = e2
    return a2 * a1, a2 * b1 + b2

def s5_direction(u_c, a_re, a_im, log_dt, b_re, b_im, c_re, c_im, reverse):
    f32 = jnp.float32
    lam = lax.complex(a_re.astype(f32), a_im.astype(f32))
    dt = jnp.exp(log_dt.astype(f32))[:, None]
    a_bar = jnp.exp(lam * dt)
    b_bar = ((a_bar - 1.0) / lam)[:, :, None] * lax.complex(b_re.astype(f32), b_im.astype(f32))
    bu = jnp.einsum("blgh,gph->blgp", u_c, b_bar)
    a_seq = jnp.broadcast_to(a_bar, (1, u_c.shape[1]) + a_bar.shape)
    _, states = lax.associative_scan(_linear_combine, (a_seq, bu), reverse=reverse, axis=1)
    c_mat = lax.complex(c_re.astype(f32), c_im.astype(f32))
    return jnp.real(jnp.einsum("blgp,ghp->blgh", states, c_mat))

def s5_mixer(u, a_re, a_im, log_dt, b_re, b_im, c_re, c_im, d_skip, glu_w, glu_b):
    bsz, length, _ = u.shape
    uf = u.astype(jnp.float32).reshape(bsz, length, SSM_GROUPS, SSM_GROUP)
    u_c = uf.astype(jnp.complex64)
    y_fwd = s5_direction(u_c, a_re[0], a_im[0], log_dt[0], b_re[0], b_im[0], c_re[0], c_im[0], False)
    y_bwd = s5_direction(u_c, a_re[1], a_im[1], log_dt[1], b_re[1], b_im[1], c_re[1], c_im[1], True)
    y = (y_fwd + y_bwd).reshape(bsz, length, SSM_WIDTH) + d_skip.astype(jnp.float32) * uf.reshape(bsz, length, SSM_WIDTH)
    z = jax.nn.gelu(y)
    z = z * jax.nn.sigmoid(z @ glu_w.astype(jnp.float32) + glu_b.astype(jnp.float32))
    return z.astype(u.dtype)

def setup_inputs(seed: int = 0) -> dict:
    key = jax.random.key(seed)
    ks = jax.random.split(key, 24)
    f32 = jnp.float32
    L2 = (DEPTH, 2)

    def nrm(k, shape, scale):
        return jax.random.normal(k, shape, f32) * scale

    def gain(k, shape):
        return 1.0 + 0.05 * jax.random.normal(k, shape, f32)

    n_idx = jnp.arange(SSM_STATE, dtype=f32)
    a_im_base = jnp.broadcast_to(math.pi * n_idx, L2 + (SSM_GROUPS, SSM_STATE))
    return {
        "x": jax.random.normal(ks[0], (BATCH, SEQ, D_MODEL), f32),
        "mix_norm_pre": gain(ks[1], (DEPTH, D_MODEL)),
        "mix_norm_post": gain(ks[2], (DEPTH, D_MODEL)),
        "w_in": nrm(ks[3], (DEPTH, D_MODEL, IN_COLS), D_MODEL ** -0.5),
        "conv_dw_w": nrm(ks[4], (DEPTH, CONV_KERNEL, CONV_WIDTH), CONV_KERNEL ** -0.5),
        "conv_dw_b": nrm(ks[5], (DEPTH, CONV_WIDTH), 0.02),
        "conv_ln_g": gain(ks[6], (DEPTH, CONV_WIDTH)),
        "conv_ln_b": nrm(ks[7], (DEPTH, CONV_WIDTH), 0.02),
        "ssm_a_re": -0.5 + 0.01 * jax.random.normal(ks[8], L2 + (SSM_GROUPS, SSM_STATE), f32),
        "ssm_a_im": a_im_base + 0.01 * jax.random.normal(ks[9], L2 + (SSM_GROUPS, SSM_STATE), f32),
        "ssm_log_dt": jax.random.uniform(ks[10], L2 + (SSM_GROUPS,), f32, math.log(DT_MIN), math.log(DT_MAX)),
        "ssm_b_re": nrm(ks[11], L2 + (SSM_GROUPS, SSM_STATE, SSM_GROUP), (2 * SSM_GROUP) ** -0.5),
        "ssm_b_im": nrm(ks[12], L2 + (SSM_GROUPS, SSM_STATE, SSM_GROUP), (2 * SSM_GROUP) ** -0.5),
        "ssm_c_re": nrm(ks[13], L2 + (SSM_GROUPS, SSM_GROUP, SSM_STATE), (2 * SSM_STATE) ** -0.5),
        "ssm_c_im": nrm(ks[14], L2 + (SSM_GROUPS, SSM_GROUP, SSM_STATE), (2 * SSM_STATE) ** -0.5),
        "ssm_d": nrm(ks[15], (DEPTH, SSM_WIDTH), 1.0),
        "ssm_glu_w": nrm(ks[16], (DEPTH, SSM_WIDTH, SSM_WIDTH), SSM_WIDTH ** -0.5),
        "ssm_glu_b": nrm(ks[17], (DEPTH, SSM_WIDTH), 0.02),
        "w_out": nrm(ks[18], (DEPTH, MIX_WIDTH, D_MODEL), MIX_WIDTH ** -0.5),
        "ffn_norm_pre": gain(ks[19], (DEPTH, D_MODEL)),
        "ffn_norm_post": gain(ks[20], (DEPTH, D_MODEL)),
        "ffn_w_gate": nrm(ks[21], (DEPTH, D_MODEL, FFN_HIDDEN), D_MODEL ** -0.5),
        "ffn_w_up": nrm(ks[22], (DEPTH, D_MODEL, FFN_HIDDEN), D_MODEL ** -0.5),
        "ffn_w_down": nrm(ks[23], (DEPTH, FFN_HIDDEN, D_MODEL), FFN_HIDDEN ** -0.5),
    }

def reference(x, mix_norm_pre, mix_norm_post, w_in, conv_dw_w, conv_dw_b, conv_ln_g, conv_ln_b,
              ssm_a_re, ssm_a_im, ssm_log_dt, ssm_b_re, ssm_b_im, ssm_c_re, ssm_c_im, ssm_d,
              ssm_glu_w, ssm_glu_b, w_out, ffn_norm_pre, ffn_norm_post, ffn_w_gate, ffn_w_up,
              ffn_w_down):
    for layer in range(DEPTH):
        h = rms_norm(x, mix_norm_pre[layer])
        proj = h @ w_in[layer]
        conv_val = proj[..., :CONV_WIDTH]
        conv_gate = proj[..., CONV_WIDTH:2 * CONV_WIDTH]
        u = proj[..., 2 * CONV_WIDTH:]
        c = conv_val * jax.nn.sigmoid(conv_gate)
        c = depthwise_conv(c, conv_dw_w[layer], conv_dw_b[layer])
        c = jax.nn.silu(layer_norm(c, conv_ln_g[layer], conv_ln_b[layer]))
        s = s5_mixer(u, ssm_a_re[layer], ssm_a_im[layer], ssm_log_dt[layer], ssm_b_re[layer],
                     ssm_b_im[layer], ssm_c_re[layer], ssm_c_im[layer], ssm_d[layer],
                     ssm_glu_w[layer], ssm_glu_b[layer])
        mixed = jnp.concatenate([c, s.astype(c.dtype)], axis=-1) @ w_out[layer]
        x = x + rms_norm(mixed, mix_norm_post[layer])
        h = rms_norm(x, ffn_norm_pre[layer])
        f = (jax.nn.silu(h @ ffn_w_gate[layer]) * (h @ ffn_w_up[layer])) @ ffn_w_down[layer]
        x = x + rms_norm(f, ffn_norm_post[layer])
    return x


_drawn_inputs = setup_inputs


def setup_inputs(seed=0):
    import zlib

    import numpy as np

    out = dict(_drawn_inputs(seed))
    spreads = {}
    factors = {'conv_ln_b': 4.017,
     'ssm_a_re': 200.0,
     'ssm_glu_b': 8.0,
     'ssm_a_im': 34.608,
     'ssm_log_dt': 37.296,
     'ssm_b_re': 48.248,
     'ssm_b_im': 48.28,
     'ssm_c_re': 47.488,
     'ssm_c_im': 48.432}
    for name, (base, spread) in spreads.items():
        noise = np.random.default_rng([zlib.crc32(name.encode()), seed]).standard_normal(out[name].shape)
        drawn = base * np.exp(spread * noise) if base else spread * noise
        out[name] = __import__('jax').numpy.asarray(drawn.astype(out[name].dtype))
    for name, factor in factors.items():
        out[name] = (out[name] * factor).astype(out[name].dtype)
    return out
```

```python
import math
from contextlib import ExitStack

import concourse.bass as bass
from concourse import mybir

F32 = mybir.dt.float32
F32R = mybir.dt.float32r
I32 = mybir.dt.int32
ALU = mybir.AluOpType
ACT = mybir.ActivationFunctionType

P = 128
TB = 512
EPS = 1e-6
N_CONSTS = 19
HALF, HSIN, HABS, HCOS = 6, 7, 8, 18
START, START_DMA = 1, 16
SQ0 = 32
RING = 4
CH = 8
SUP = 16
GQ = 8
MAGIC = 12582912.0


def hybrid_encoder(nc, x, mix_norm_pre, mix_norm_post, w_in, conv_dw_w, conv_dw_b, conv_ln_g,
                   conv_ln_b, ssm_a_re, ssm_a_im, ssm_log_dt, ssm_b_re, ssm_b_im, ssm_c_re,
                   ssm_c_im, ssm_d, ssm_glu_w, ssm_glu_b, w_out, ffn_norm_pre, ffn_norm_post,
                   ffn_w_gate, ffn_w_up, ffn_w_down, out):
    _, T, D = x.shape
    KD = D // P
    NB = T // TB
    NT = TB // P
    CW = conv_dw_w.shape[2]
    CT = CW // P
    TAPS = conv_dw_w.shape[1]
    HALO = TAPS // 2
    CPAD = T + 2 * HALO
    CIN = TB + 2 * HALO
    _, _, G, NP_, H = ssm_b_re.shape
    NC = T // CH
    ND = NC // SUP
    CB = TB // CH
    FT = ffn_w_gate.shape[2] // P
    assert CH * H == P and 2 * NP_ == P and G == 4 * GQ and NB == 4 and KD == 8

    UNITS_U, UNITS_VG = CT, 2 * CT
    GLU_UNITS = 2
    USE_VG = NB * UNITS_U // RING
    USE_BLK = USE_VG + NB * UNITS_VG // RING
    UNITS_BLK = GLU_UNITS + KD + 2 * FT + FT
    PER_BLK = UNITS_BLK // RING
    assert UNITS_BLK % RING == 0 and UNITS_U == RING

    def scratch(name, shape):
        return nc.dram_tensor(name, shape, F32, kind="Internal").ap()

    u_d = scratch("u_scratch", [G, H, CH, NC])
    z_d = scratch("z_scratch", [G, H, CH, NC])
    c_d = scratch("c_scratch", [CT, P, CPAD])
    e_d = scratch("e_scratch", [4, P, 2 * GQ * P])
    f_d = scratch("f_scratch", [4, P, 2 * GQ * P])
    m_d = scratch("m_scratch", [P, CH, G, H])

    with ExitStack() as ctx:
        def sb(name, shape, dt=F32, scope=ctx):
            return scope.enter_context(nc.sbuf_tensor(name, shape, dt))

        def sem(name):
            return ctx.enter_context(nc.semaphore(name))

        def sems(name, n):
            return [sem(f"{name}{i}") for i in range(n)]

        ident = sb("ident", [P, P])
        mean_w = sb("mean_w", [P, P])
        xb = sb("xb", [P, NT, D])
        raw = sb("raw", [P, RING, D])
        w_hi = sb("w_hi", [P, RING, D], F32R)
        w_lo = sb("w_lo", [P, RING, D], F32R)
        t_hi = sb("t_hi", [P, KD, TB], F32R)
        t_lo = sb("t_lo", [P, KD, TB], F32R)
        g_mix = sb("g_mix", [P, KD])
        g_ffn = sb("g_ffn", [P, KD])
        ln_g = sb("ln_g", [P, CT])
        ln_b = sb("ln_b", [P, CT])
        glu_b = sb("glu_b", [P, CT])
        conv_b = sb("conv_b", [P, CT])
        conv_w = sb("conv_w", [P, CT, TAPS])
        ssq = sb("ssq", [P, 3, NT])
        std = sb("std", [P, 3, NT])
        rstd = sb("rstd", [P, 3, NT])
        epsc = sb("epsc", [P, 1])
        halfpi = sb("halfpi", [P, 1])

        pscope = ExitStack()
        psb = lambda name, shape, dt=F32: sb(name, shape, dt, pscope)
        sq_junk = psb("sq_junk", [P, D])
        u_st = psb("u_st", [P, CT, TB])
        sig_st = psb("sig_st", [P, 2, TB])
        c_st = psb("c_st", [P, 2, TB])
        e_sb = psb("e_sb", [P, 2, GQ, P])
        f_sb = psb("f_sb", [P, 2, GQ, P])
        qr_t = psb("qr_t", [P, SUP + 3, G])
        qi_t = psb("qi_t", [P, SUP + 3, 2, G])
        lscope = ExitStack()
        lsb = lambda name, shape, dt=F32: sb(name, shape, dt, lscope)
        u_sb = lsb("u_sb", [P, GQ, NC])
        m_in = lsb("m_in", [P, CH, GQ, H])
        m_sb = lsb("m_sb", [P, GQ, CH * H])
        s_sb = lsb("s_sb", [P, 2, GQ, NC])
        x_sb = lsb("x_sb", [P, 2, GQ, NC + 2])
        bnd = lsb("bnd", [P, 2, GQ, ND])
        sc1 = lsb("sc1", [P, 2, GQ, ND])
        sc2 = lsb("sc2", [P, 2, GQ, ND])
        fx1 = lsb("fx1", [P, 4, SUP, ND - 1])
        fx2 = lsb("fx2", [P, 4, SUP, ND - 1])
        z_st = lsb("z_st", [P, 2, 2, NC])
        lscope.close()
        rscope = ExitStack()
        rsb = lambda name, shape, dt=F32: sb(name, shape, dt, rscope)
        zeros = rsb("zeros", [P, CT, HALO])
        cw_raw = rsb("cw_raw", [TAPS, CW])
        prm = rsb("prm", [G, 3, 2, NP_])
        ldt_raw = rsb("ldt_raw", [G, 2])
        c_raw = rsb("c_raw", [P, 2, 4, 2, NP_])
        b_in = rsb("b_in", [P, 2, G, H])
        lam = rsb("lam", [P, 3, G])
        pv = rsb("pv", [P, 24, G])
        pvi = rsb("pvi", [P, G], I32)
        bb = rsb("bb", [P, 2, G, H])
        cc = rsb("cc", [P, 3, G, H])
        pw = rsb("pw", [P, 2, CH + 1, G])
        pe = rsb("pe", [P, 2, CH, G])
        pf = rsb("pf", [P, 2, CH, G])
        gg = rsb("gg", [P, 2, GQ, CH, H])
        ccq = rsb("ccq", [P, 2, GQ, 2, H])
        g1 = rsb("g1", [P, GQ * CH * H])
        g2 = rsb("g2", [P, GQ * CH * H])
        lf = rsb("lf", [P, 2, G, H])
        kx = rsb("kx", [P, G, H])
        d_b = rsb("d_b", [P, G, H])
        rscope.close()
        pscope.close()

        fscope = ExitStack()
        fsb = lambda name, shape, dt=F32: sb(name, shape, dt, fscope)
        cin = fsb("cin", [P, CT, CIN + 2])
        cv = fsb("cv", [P, CT, TB])
        gp_mix = fsb("gp_mix", [P, D])
        gp_ffn = fsb("gp_ffn", [P, D])
        tmp = fsb("tmp", [P, D])
        act_t = fsb("act_t", [P, 2, TB])
        junk = fsb("junk", [P, D])
        hscope = ExitStack()
        hid_hi = sb("hid_hi", [P, FT, TB], F32R, hscope)
        hid_lo = sb("hid_lo", [P, FT, TB], F32R, hscope)
        hscope.close()
        mscope = ExitStack()
        msb = lambda name, shape, dt=F32: sb(name, shape, dt, mscope)
        z_sb = msb("z_sb", [P, CT, TB])
        sg = msb("sg", [P, CT, TB])
        sq = msb("sq", [P, CT, TB])
        cn = msb("cn", [P, CT, TB])
        ln_std = msb("ln_std", [P, TB])
        ln_rstd = msb("ln_rstd", [P, TB])
        xn = msb("xn", [P, NT, D])
        mscope.close()
        fscope.close()

        ps = ctx.enter_context(nc.psum_tensor("ps", [P, 8, TB], F32))

        raw_landed = sems("raw_landed", RING)
        whi_done = sems("whi_done", RING)
        split_done = sems("split_done", RING)
        used = sems("used", RING)
        consts_in = sem("consts_in")
        s5_in = sem("s5_in")
        gp_in = sem("gp_in")
        pads_out = sem("pads_out")
        ident_zero = sem("ident_zero")
        ident_ready = sem("ident_ready")
        pool_consts = sem("pool_consts")
        zeros_ready = sem("zeros_ready")
        x_landed = sems("x_landed", NT)
        squares = sem("squares")
        std_ready = sem("std_ready")
        rstd_ready = sem("rstd_ready")
        rows_ready = sem("rows_ready")
        tp_ready = sem("tp_ready")
        hi_done = sem("hi_done")
        lo_done = sem("lo_done")
        u_evac = sems("u_evac", CT)
        u_stored = sems("u_stored", CT)
        dve = sem("dve_chain")
        act_chain = sem("act_chain")
        prm_t = sem("prm_t")
        prm_in = sem("prm_in")
        angle_ready = sem("angle_ready")
        trig_ready = sem("trig_ready")
        g_ready = sem("g_ready")
        f_ready = sem("f_ready")
        et_ready = sem("et_ready")
        e_evac = sem("e_evac")
        l_ready = sem("l_ready")
        l_evac = sem("l_evac")
        ef_stored = sem("ef_stored")
        k0_moved = sem("k0_moved")
        lf_full = sem("lf_full")
        m_stored = sem("m_stored")
        s5_landed = sem("s5_landed")
        m_laid = sem("m_laid")
        st_ready = sem("st_ready")
        st_fwd = sem("st_fwd")
        st_bwd = sem("st_bwd")
        fixed = sem("fixed")
        sig_done = sem("sig_done")
        c_done = sems("c_done", 2)
        c_stored = sems("c_stored", 2)
        y_ready = sem("y_ready")
        z_done = sem("z_done")
        z_stored = sems("z_stored", 2)
        cin_landed = sem("cin_landed")
        conv_done = sem("conv_done")
        z_landed = sem("z_landed")
        zhi_done = sem("zhi_done")
        zlo_done = sem("zlo_done")
        gate_done = sem("gate_done")
        s_split = sem("s_split")
        mean_ready = sem("mean_ready")
        dev_done = sem("dev_done")
        sq_done = sem("sq_done")
        var_ready = sem("var_ready")
        lstd_ready = sem("lstd_ready")
        norm_done = sem("norm_done")
        silu_done = sem("silu_done")
        c_split = sem("c_split")
        mixed_ready = sem("mixed_ready")
        silu_h = sem("silu_h")
        hid_done = sems("hid_done", 2)
        out_stored = sem("out_stored")
        conv_chain = sems("conv_chain", CT)
        ln_chain = sem("ln_chain")
        chi_done = sem("chi_done")
        shi_done = sem("shi_done")
        s_done = sem("s_done")
        tmp_made = sem("tmp_made")
        rows_added = sem("rows_added")
        hid_made = sems("hid_made", 2)
        hid_hi_done = sems("hid_hi_done", 2)
        down_tile = sem("down_tile")

        block = ctx.enter_context(nc.Block())


        @block.sync
        def _(sp):
            def load(slot, n, src):
                sp.wait_ge(split_done[slot], START + n)
                sp.dma_start(raw[:, slot, :].rearrange("p (k m) -> p k m", k=src.shape[1]), src)\
                    .then_inc(raw_landed[slot], 16)

            w_in_v = w_in[0].rearrange("(k p) n -> p k n", p=P)
            with sp.Fori(0, NB) as i:
                for m in range(CT):
                    load(m, i, w_in_v[:, :, 2 * CW + m * P:2 * CW + (m + 1) * P])
            with sp.Fori(0, NB) as i:
                for m in range(CT):
                    for v in range(2):
                        u = 2 * m + v
                        load(u % RING, USE_VG + 2 * i + u // RING,
                             w_in_v[:, :, v * CW + m * P:v * CW + (m + 1) * P])
            glu_v = ssm_glu_w[0].rearrange("(k p) n -> p k n", p=P)
            w_out_v = w_out[0].rearrange("(k p) (a n) -> p k a n", p=P, a=1)
            gate_v = ffn_w_gate[0].rearrange("(k p) n -> p k n", p=P)
            up_v = ffn_w_up[0].rearrange("(k p) n -> p k n", p=P)
            down_v = ffn_w_down[0].rearrange("(k p) (a n) -> p k a n", p=P, a=1)
            with sp.Fori(0, NB) as b:
                use = USE_BLK + PER_BLK * b
                for u in range(GLU_UNITS):
                    load(u, use, glu_v[:, :, u * 2 * P:(u + 1) * 2 * P])
                for k in range(KD):
                    u = GLU_UNITS + k
                    load(u % RING, use + u // RING, w_out_v[:, k])
                at = GLU_UNITS + KD
                with sp.Fori(0, FT // 2) as t:
                    for v in range(4):
                        src = (gate_v, up_v)[v % 2]
                        load((at + v) % RING, use + (at + v) // RING + t,
                             src[:, :, bass.ds((2 * t + v // 2) * P, P)])
                at += 2 * FT
                for k in range(FT):
                    load((at + k) % RING, use + (at + k) // RING, down_v[:, k])

        @block.gpsimd
        def _(pool):
            for s in split_done:
                pool.sem_inc(s, START)
            pool.memset(ident[:], 0.0).then_inc(ident_zero, 1)
            pool.wait_ge(ident_zero, 1)
            pool.affine_select(out=ident[:], in_=ident[:], compare_op=ALU.not_equal, fill=1.0, base=0,
                               pattern=[[-1, P]], channel_multiplier=1).then_inc(ident_ready, 1)
            pool.memset(zeros[:], 0.0).then_inc(zeros_ready, 1)
            pool.memset(mean_w[:], 1.0 / CW).then_inc(pool_consts, 1)
            pool.memset(epsc[:], EPS).then_inc(pool_consts, 1)
            pool.memset(halfpi[:], math.pi / 2).then_inc(pool_consts, 1)
            pool.memset(kx[:], 0.0).then_inc(pool_consts, 1)

            with pool.Fori(0, NB * (UNITS_U + UNITS_VG) // RING + NB * PER_BLK) as n:
                for slot in range(RING):
                    pool.wait_ge(whi_done[slot], n + 1)
                    pool.tensor_tensor(w_lo[:, slot, :], raw[:, slot, :],
                                       w_hi[:, slot, :].bitcast(F32), ALU.subtract)\
                        .then_inc(split_done[slot], 1)

        W_IN_X = x[0].rearrange("(b t p) d -> p b t d", t=NT, p=P)
        W_OUT_X = out[0].rearrange("(b t p) d -> p b t d", t=NT, p=P)

        @block.scalar
        def _(act):
            for s in (*u_evac, e_evac, l_evac, squares, z_done):
                act.sem_inc(s, START)
            for s in (*u_stored, *c_stored, *z_stored, ef_stored, out_stored):
                act.sem_inc(s, START_DMA)
            loads = [(prm[:, 0], ssm_a_re[0].rearrange("d g p -> g d p")),
                     (prm[:, 1], ssm_a_im[0].rearrange("d g p -> g d p")),
                     (ldt_raw[:], ssm_log_dt[0].rearrange("d g -> g d")),
                     (cw_raw[:], conv_dw_w[0])]
            for ri, c_in in enumerate((ssm_c_re, ssm_c_im)):
                for d in range(2):
                    loads.append((c_raw[:, ri, :, d, :],
                                  c_in[0, d].rearrange("(o g) h p -> (g h) o p", o=4)))
            for ri, b_x in enumerate((ssm_b_re, ssm_b_im)):
                for d in range(2):
                    loads.append((b_in[d * NP_:(d + 1) * NP_, ri], b_x[0, d].rearrange("g p h -> p g h")))
            for dst, src in ((g_mix, mix_norm_pre), (g_ffn, ffn_norm_pre), (ln_g, conv_ln_g),
                             (ln_b, conv_ln_b), (glu_b, ssm_glu_b), (conv_b, conv_dw_b)):
                loads.append((dst[:], src[0].rearrange("(k p) -> p k", p=P)))
            loads.append((d_b[96:P].rearrange("p g h -> p (g h)"), ssm_d[0].partition_broadcast(32)))
            assert len(loads) == N_CONSTS
            for tt in range(NT):
                act.dma_start(xb[:, tt, :], W_IN_X[:, 0, tt, :]).then_inc(x_landed[tt], 16)
            for dst, src in loads:
                act.dma_start(dst, src, allow_slow_non_contiguous=True).then_inc(consts_in, 16)
            act.wait_ge(zeros_ready, 1)
            for at in (0, HALO + T):
                act.dma_start(c_d[:, :, at:at + HALO].rearrange("c p t -> p c t"), zeros[:])\
                    .then_inc(pads_out, 16)

            act.wait_ge(angle_ready, 1)
            act.wait_ge(pool_consts, 4)
            act.activation(pv[:, HSIN], pv[:, HALF], ACT.Sin).then_inc(trig_ready, 1)
            act.activation(pv[:, HABS], pv[:, HALF], ACT.Abs).then_inc(act_chain, 1)
            act.wait_ge(act_chain, 1)
            act.activation(pv[:, HCOS], pv[:, HABS], ACT.Sin, bias=halfpi[:, 0:1], scale=-1.0)\
                .then_inc(trig_ready, 1)

            def split_hi(slot, n):
                act.wait_ge(raw_landed[slot], 16 * (n + 1))
                act.wait_ge(used[slot], START + n)
                act.activation(w_hi[:, slot, :], raw[:, slot, :], ACT.Copy).then_inc(whi_done[slot], 1)

            def row_stats(it):
                for tt in range(NT):
                    act.wait_ge(x_landed[tt], 16 * it + 16)
                    if tt:
                        act.wait_ge(squares, START + 4 * it + tt)
                    else:
                        act.wait_ge(squares, START + 4 * it)
                    act.activation(sq_junk[:], xb[:, tt, :], ACT.Square, accum_out=ssq[:, 0, tt:tt + 1])\
                        .then_inc(squares, 1)
                act.wait_ge(squares, START + 4 * it + 4)
                act.activation(std[:, 0, :], ssq[:, 0, :], ACT.Sqrt, bias=epsc[:, 0:1], scale=1.0 / D)\
                    .then_inc(std_ready, 1)

            def evacuate_hi(it, gain):
                for k in range(KD):
                    act.wait_ge(tp_ready, KD * it + k + 1)
                    act.activation(t_hi[:, k, :], ps[:, 4 + k % 2, :], ACT.Copy, scale=gain[:, k:k + 1])\
                        .then_inc(hi_done, 1)

            def load_rows(it, nxt):
                for tt in range(NT):
                    act.dma_start(xb[:, tt, :], W_IN_X[:, nxt, tt, :]).then_inc(x_landed[tt], 16)

            act.wait_ge(consts_in, 16 * N_CONSTS)
            with act.Fori(0, NB) as i:
                for u in range(RING):
                    split_hi(u, i)
                row_stats(i)
                act.wait_ge(used[RING - 1], START + i)
                evacuate_hi(i, g_mix)
                load_rows(i, (i + 1) % NB)
                for m in range(CT):
                    act.wait_ge(used[m], START + i + 1)
                    act.wait_ge(u_stored[m], START_DMA + 16 * i)
                    act.activation(u_st[:, m, :].rearrange("p (j c) -> p j c", j=CH),
                                   ps[:, m, :].rearrange("p (c j) -> p j c", j=CH), ACT.Copy)\
                        .then_inc(u_evac[m], 1)
                    act.wait_ge(u_evac[m], START + i + 1)
                    act.dma_start(
                        u_d[m * GQ:(m + 1) * GQ, :, :, bass.ds(CB * i, CB)].rearrange("g h j c -> (g h) j c"),
                        u_st[:, m, :].rearrange("p (j c) -> p j c", j=CH)).then_inc(u_stored[m], 16)
                act.wait_ge(ef_stored, START_DMA + 32 * i)
                for r in range(4):
                    act.wait_ge(et_ready, 4 * i + r + 1)
                    act.activation(e_sb[:, r // 2, 4 * (r % 2):4 * (r % 2) + 4, :],
                                   ps[:, 6, :].rearrange("p (g q) -> p g q", g=4), ACT.Copy).then_inc(e_evac, 1)
                act.wait_ge(l_ready, START + i + 1)
                act.activation(lf[:, :, bass.ds(GQ * i, GQ), :],
                               ps[:, 7, 0:2 * GQ * H].rearrange("p (g f h) -> p f g h", g=GQ, f=2),
                               ACT.Copy).then_inc(l_evac, 1)
                act.wait_ge(e_evac, START + 4 * i + 4)
                act.dma_start(e_d[i], e_sb[:].rearrange("p r g q -> p (r g q)")).then_inc(ef_stored, 16)
                act.wait_ge(f_ready, i + 1)
                act.dma_start(f_d[i], f_sb[:].rearrange("p r g q -> p (r g q)")).then_inc(ef_stored, 16)

            act.wait_ge(l_evac, START + NB)
            act.dma_start(kx[P - H:P], lf[0:H, 1]).then_inc(k0_moved, 16)
            act.wait_ge(lf_full, 1)
            for j in range(CH):
                act.dma_start(m_d[0:H * (j + 1), j], lf[H * (CH - 1 - j):P, 0]).then_inc(m_stored, 16)
                if j < CH - 1:
                    act.dma_start(m_d[H * (j + 1):P, j], lf[H:H * (CH - j), 1]).then_inc(m_stored, 16)
            for m in range(CT):
                act.wait_ge(u_stored[m], START_DMA + 16 * NB)
            act.wait_ge(ef_stored, START_DMA + 32 * NB)
            act.wait_ge(m_stored, 16 * (2 * CH - 1))

            with act.Fori(0, NB) as i:
                act.wait_ge(y_ready, START + 4 * i)
                for j in range(CH):
                    act.dma_start(u_sb[j * H:(j + 1) * H],
                                  u_d[bass.ds(GQ * i, GQ), :, j, :].rearrange("g h c -> h g c"))\
                        .then_inc(s5_landed, 16)
                act.dma_start(e_sb[:].rearrange("p r g q -> p (r g q)"), e_d[i]).then_inc(s5_landed, 16)
                act.dma_start(f_sb[:].rearrange("p r g q -> p (r g q)"), f_d[i]).then_inc(s5_landed, 16)
                act.dma_start(m_in[:], m_d[:, :, bass.ds(GQ * i, GQ), :]).then_inc(s5_landed, 16)
                for u in range(RING):
                    split_hi(u, USE_VG + 2 * i)
                row_stats(NB + i)
                act.wait_ge(used[RING - 1], START + USE_VG + 2 * i)
                evacuate_hi(NB + i, g_mix)
                load_rows(NB + i, (i + 1) % NB)
                act.wait_ge(fixed, START + i)
                for r in range(4):
                    for ri in range(2):
                        act.wait_ge(st_ready, 8 * i + 2 * r + ri + 1)
                        act.activation(s_sb[0:NP_, ri, 2 * r:2 * r + 2, :],
                                       ps[0:NP_, 6 + ri, :].rearrange("p (g c) -> p g c", g=2), ACT.Copy)\
                            .then_inc(st_fwd, 1)

                act.wait_ge(s5_landed, 16 * (CH + 3) * (i + 1))
                act.activation(m_sb[:].rearrange("p g (j h) -> p g j h", j=CH),
                               m_in[:].rearrange("p j g h -> p g j h"), ACT.Copy).then_inc(m_laid, 1)

                def store_c(m):
                    act.wait_ge(c_done[m % 2], START + 2 * i + m // 2 + 1)
                    act.dma_start(c_d[m, :, bass.ds(TB * i + HALO, TB)], c_st[:, m % 2, :])\
                        .then_inc(c_stored[m % 2], 16)

                for m in range(CT):
                    gate = 2 * m + 1
                    act.wait_ge(used[gate % RING], START + USE_VG + 2 * i + gate // RING + 1)
                    act.wait_ge(c_done[m % 2], START + 2 * i + m // 2)
                    act.activation(sig_st[:, m % 2, :], ps[:, 2 * (m % 2) + 1, :], ACT.Sigmoid)\
                        .then_inc(sig_done, 1)
                    if m < 2:
                        for u in (2 * m, 2 * m + 1):
                            split_hi(u, USE_VG + 2 * i + 1)
                    if m:
                        store_c(m - 1)
                store_c(CT - 1)
                for r in range(4):
                    act.wait_ge(y_ready, START + 4 * i + r + 1)
                    act.wait_ge(z_stored[r % 2], START_DMA + 16 * CH * (2 * i + r // 2))
                    act.activation(z_st[:, r % 2], ps[:, 6 + r % 2, :].rearrange("p (g c) -> p g c", g=2),
                                   ACT.Gelu_apprx_tanh).then_inc(z_done, 1)
                    act.wait_ge(z_done, START + 4 * i + r + 1)
                    for j in range(CH):
                        act.dma_start(
                            z_d[bass.ds(GQ * i + 2 * r, 2), :, j, :].rearrange("g h c -> h g c"),
                            z_st[j * H:(j + 1) * H, r % 2]).then_inc(z_stored[r % 2], 16)

            act.wait_ge(pads_out, 32)
            for n in range(2):
                act.wait_ge(c_stored[n], START_DMA + 16 * 2 * NB)
                act.wait_ge(z_stored[n], START_DMA + 16 * CH * 2 * NB)
            act.wait_ge(fixed, START + NB)
            cin_src = lambda b: c_d[:, :, bass.ds(TB * b, CIN)].rearrange("c p t -> p c t")
            act.dma_start(cin[:, :, 0:CIN], cin_src(0)).then_inc(cin_landed, 16)
            act.dma_start(gp_mix[:], mix_norm_post[0].partition_broadcast(P)).then_inc(gp_in, 16)
            act.dma_start(gp_ffn[:], ffn_norm_post[0].partition_broadcast(P)).then_inc(gp_in, 16)
            with act.Fori(0, NB) as b:
                it = 2 * NB + b
                act.wait_ge(out_stored, START_DMA + 16 * NT * b)
                load_rows(it + 1, b)

                def split_blk(u):
                    split_hi(u % RING, USE_BLK + PER_BLK * b + u // RING)

                for u in range(RING):
                    split_blk(u)
                act.wait_ge(used[RING - 1], START + USE_BLK + PER_BLK * b)
                for k in range(CT):
                    act.dma_start(z_sb[:, k, :].rearrange("p (j c) -> p j c", j=CH),
                                  z_d[k * GQ:(k + 1) * GQ, :, :, bass.ds(CB * b, CB)]
                                  .rearrange("g h j c -> (g h) j c")).then_inc(z_landed, 16)
                act.wait_ge(z_landed, 16 * CT * (b + 1))
                for k in range(CT):
                    act.activation(t_hi[:, CT + k, :], z_sb[:, k, :], ACT.Copy).then_inc(zhi_done, 1)
                for k in range(CT):
                    act.wait_ge(dev_done, CT * b + k + 1)
                    act.activation(sq[:, k, :], cv[:, k, :], ACT.Square).then_inc(sq_done, 1)
                for k in range(CT):
                    act.wait_ge(used[k // 2], START + USE_BLK + PER_BLK * b + 1)
                    act.activation(sg[:, k, :], ps[:, k, :], ACT.Sigmoid, bias=glu_b[:, k:k + 1])\
                        .then_inc(gate_done, 1)
                    if k % 2:
                        split_blk(RING + k // 2)
                act.wait_ge(var_ready, b + 1)
                act.activation(ln_std[:], ps[:, 5, :], ACT.Sqrt, bias=epsc[:, 0:1]).then_inc(lstd_ready, 1)
                for k in range(CT):
                    act.wait_ge(norm_done, CT * b + k + 1)
                    act.activation(cn[:, k, :], cv[:, k, :], ACT.Silu, scale=ln_g[:, k:k + 1],
                                   bias=ln_b[:, k:k + 1]).then_inc(silu_done, 1)

                def tile_stats(which, ready, rows):
                    for tt in range(NT):
                        ready(tt)
                        act.wait_ge(squares, START + SQ0 + 12 * b + 4 * which + tt)
                        act.activation(junk[:], rows(tt), ACT.Square,
                                       accum_out=ssq[:, which, tt:tt + 1]).then_inc(squares, 1)
                    act.wait_ge(squares, START + SQ0 + 12 * b + 4 * which + 4)
                    act.activation(std[:, which, :], ssq[:, which, :], ACT.Sqrt, bias=epsc[:, 0:1],
                                   scale=1.0 / D).then_inc(std_ready, 1)

                act.wait_ge(conv_done, b + 1)
                act.dma_start(cin[:, :, 0:CIN], cin_src((b + 1) % NB)).then_inc(cin_landed, 16)
                bank2 = lambda tt: ps[:, 2 * tt:2 * tt + 2, :].rearrange("p a n -> p (a n)")
                for u in range(RING + 2, GLU_UNITS + KD + 2):
                    split_blk(u)

                def tile_done(tile_ready, last_unit, tt):
                    if tt < NT - 1:
                        act.wait_ge(tile_ready, (NT - 1) * b + tt + 1)
                    else:
                        act.wait_ge(used[last_unit % RING], START + USE_BLK + PER_BLK * b + last_unit // RING + 1)

                tile_stats(0, lambda tt: tile_done(mixed_ready, GLU_UNITS + KD - 1, tt), bank2)
                tile_stats(1, lambda tt: act.wait_ge(rows_added, START + 2 * NT * b + tt + 1), lambda tt: xb[:, tt, :])
                evacuate_hi(it, g_ffn)
                for u in range(GLU_UNITS + KD + 2, GLU_UNITS + KD + 4):
                    split_blk(u)
                with act.Fori(0, FT // 2) as t:
                    for v in range(2):
                        up = GLU_UNITS + KD + 2 * v + 1
                        act.wait_ge(used[up % RING], START + USE_BLK + PER_BLK * b + up // RING + t + 1)
                        act.wait_ge(hid_done[v], START + FT // 2 * b + t)
                        act.activation(act_t[:, v, :], ps[:, 2 * v, :], ACT.Silu).then_inc(silu_h, 1)
                        for u in (up + 3, up + 4):
                            split_hi(u % RING, USE_BLK + PER_BLK * b + u // RING + t)
                for u in range(GLU_UNITS + KD + 2 * FT + 4, UNITS_BLK):
                    split_blk(u)
                tile_stats(2, lambda tt: tile_done(down_tile, UNITS_BLK - 1, tt), bank2)
                for tt in range(NT):
                    act.wait_ge(rows_added, START + 2 * NT * b + NT + tt + 1)
                    act.dma_start(W_OUT_X[:, b, tt, :], xb[:, tt, :]).then_inc(out_stored, 16)
            act.wait_ge(out_stored, START_DMA + 16 * NT * NB)

        @block.vector
        def _(v):
            for s in (lo_done, fixed, *c_done, *hid_done, rows_added):
                v.sem_inc(s, START)
            made = [0]

            def link(ins):
                made[0] += 1
                ins.then_inc(dve, 1)
                v.wait_ge(dve, made[0])

            def tt(o, a, b, op):
                link(v.tensor_tensor(o, a, b, op))

            def ts(o, a, s1, s2=None, op0=ALU.mult, op1=None):
                if op1 is None:
                    link(v.tensor_scalar(o, a, s1, None, op0))
                else:
                    link(v.tensor_scalar(o, a, s1, s2, op0, op1))

            def stt(o, a, s1, b, op0, op1):
                link(v.scalar_tensor_tensor(out=o, in0=a, scalar=s1, in1=b, op0=op0, op1=op1))

            def cmul(out_re, out_im, ar, ai, br, bi, shape, o=0):
                n = math.prod(shape[1:])
                pat = {2: "p (a) -> p a", 3: "p (a b) -> p a b", 4: "p (a b c) -> p a b c"}[len(shape)]
                sizes = dict(zip("abc", shape[1:]))
                t1 = g1[:, 0:n].rearrange(pat, **sizes)
                t2 = g2[:, 0:n].rearrange(pat, **sizes)
                tt(t1, ar, br, ALU.mult)
                tt(t2, ai, bi, ALU.mult)
                tt(out_re, t1, t2, ALU.subtract)
                tt(t1, ar, bi, ALU.mult)
                tt(t2, ai, br, ALU.mult)
                tt(out_im, t1, t2, ALU.add)

            v.wait_ge(consts_in, 16 * N_CONSTS)
            link(v.tensor_copy(prm[:, 2], ldt_raw[:].unsqueeze(2).broadcast_to([G, 2, NP_])))
            v.nop().then_inc(prm_in, 1)
            v.wait_ge(pool_consts, 4)
            v.wait_ge(prm_t, 1)
            link(v.tensor_copy(lam[:], ps[:, 0, 0:3 * G].rearrange("p (a g) -> p a g", a=3)))
            for ri in range(2):
                link(v.tensor_copy(cc[:, ri], ps[:, 1 + ri, :].rearrange("p (g h) -> p g h", g=G)))
            link(v.tensor_copy(conv_w[:], ps[:, 3, 0:CT * TAPS].rearrange("p (c k) -> p c k", c=CT)))
            ts(cc[:, 2], cc[:, 1], -1.0)

            def expm1(out, out_pow, t):
                ts(t, t, 88.0, -87.0, ALU.min, ALU.max)
                kk, r, pol = pv[:, 20], pv[:, 21], pv[:, 22]
                ts(kk, t, 1.0 / math.log(2.0), MAGIC, ALU.mult, ALU.add)
                ts(kk, kk, MAGIC, None, ALU.subtract)
                stt(r, kk, -0.693359375, t, ALU.mult, ALU.add)
                stt(r, kk, 2.12194440e-4, r, ALU.mult, ALU.add)
                ts(pol, r, 1.0 / 5040)
                for c in (1.0 / 720, 1.0 / 120, 1.0 / 24, 1.0 / 6, 0.5, 1.0):
                    stt(pol, pol, c, r, ALU.add, ALU.mult)
                ts(pvi[:], kk, 127.0, None, ALU.add)
                link(v.tensor_scalar(pvi[:], pvi[:], 23, None, ALU.logical_shift_left))
                link(v.tensor_copy(out_pow, pvi[:].bitcast(F32)))
                tt(pol, pol, out_pow, ALU.mult)
                stt(out, out_pow, -1.0, pol, ALU.add, ALU.add)

            dt_, xr, th, em, pow2, kk, hs, c1, sn, ar1, ai, den, qr, qi, t1, ar = (pv[:, n] for n in
                (0, 1, 2, 3, 4, 5, HSIN, 9, 10, 11, 12, 13, 14, 15, 16, 17))
            lr, li, ldt = lam[:, 0], lam[:, 1], lam[:, 2]
            expm1(em, pow2, ldt)
            ts(dt_, em, 1.0, None, ALU.add)
            tt(dt_, pv[:, 22], pow2, ALU.add)
            tt(xr, lr, dt_, ALU.mult)
            tt(th, li, dt_, ALU.mult)
            expm1(em, pow2, xr)
            ts(kk, th, 1.0 / (2 * math.pi), MAGIC, ALU.mult, ALU.add)
            ts(kk, kk, MAGIC, None, ALU.subtract)
            for part in (6.28125, 0.0019350051879882812, 3.019915981956752e-07):
                stt(th, kk, -part, th, ALU.mult, ALU.add)
            ts(pv[:, HALF], th, 0.5)
            link(v.tensor_scalar(pv[:, HALF], pv[:, HALF], 1.5707964, -1.5707964, ALU.min, ALU.max))
            v.nop().then_inc(angle_ready, 1)
            v.wait_ge(trig_ready, 2)
            stt(c1, hs, -2.0, hs, ALU.mult, ALU.mult)
            stt(sn, hs, 2.0, pv[:, HCOS], ALU.mult, ALU.mult)
            tt(ar1, em, c1, ALU.mult)
            tt(ar1, ar1, em, ALU.add)
            tt(ar1, ar1, c1, ALU.add)
            stt(ai, em, 1.0, sn, ALU.add, ALU.mult)
            ts(ar, ar1, 1.0, None, ALU.add)
            tt(den, lr, lr, ALU.mult)
            tt(t1, li, li, ALU.mult)
            tt(den, den, t1, ALU.add)
            link(v.reciprocal(den, den))
            tt(qr, ar1, lr, ALU.mult)
            tt(t1, ai, li, ALU.mult)
            tt(qr, qr, t1, ALU.add)
            tt(qr, qr, den, ALU.mult)
            tt(qi, ai, lr, ALU.mult)
            tt(t1, ar1, li, ALU.mult)
            tt(qi, qi, t1, ALU.subtract)
            tt(qi, qi, den, ALU.mult)
            over_h = lambda a: a.unsqueeze(2).broadcast_to([P, G, H])
            cmul(bb[:, 0], bb[:, 1], over_h(qr), over_h(qi), b_in[:, 0], b_in[:, 1], [P, G, H])
            link(v.memset(pw[:, 0, 0], 1.0))
            link(v.memset(pw[:, 1, 0], 0.0))
            link(v.tensor_copy(pw[:, 0, 1], ar))
            link(v.tensor_copy(pw[:, 1, 1], ai))
            n = 1
            while n < CH:
                last = lambda ri: pw[:, ri, n:n + 1].broadcast_to([P, n, G])
                cmul(pw[:, 0, n + 1:2 * n + 1], pw[:, 1, n + 1:2 * n + 1], pw[:, 0, 1:n + 1],
                     pw[:, 1, 1:n + 1], last(0), last(1), [P, n, G])
                n *= 2
            for ri in range(2):
                link(v.tensor_copy(pe[0:NP_, ri], pw[0:NP_, ri, CH - 1::-1]))
                link(v.tensor_copy(pe[NP_:P, ri], pw[NP_:P, ri, 0:CH]))
                link(v.tensor_copy(pf[0:NP_, ri], pw[0:NP_, ri, 1:CH + 1]))
                link(v.tensor_copy(pf[NP_:P, ri], pw[NP_:P, ri, CH:0:-1]))
            q_re, q_im = qr_t, qi_t[:, :, 1]
            link(v.tensor_copy(q_re[:, 0], pw[:, 0, CH]))
            link(v.tensor_copy(q_im[:, 0], pw[:, 1, CH]))
            n = 1
            while n < SUP:
                last = lambda a: a[:, n - 1:n].broadcast_to([P, n, G])
                cmul(q_re[:, n:2 * n], q_im[:, n:2 * n], q_re[:, 0:n], q_im[:, 0:n], last(q_re), last(q_im),
                     [P, n, G])
                n *= 2
            for n in range(SUP, SUP + 3):
                cmul(q_re[:, n], q_im[:, n], q_re[:, n - 1], q_im[:, n - 1], q_re[:, n - 1], q_im[:, n - 1],
                     [P, G])
            ts(qi_t[:, :, 0], q_im, -1.0)
            tt(d_b[96:P], d_b[96:P], ident[96:P, P - H:P].unsqueeze(1).broadcast_to([32, G, H]), ALU.mult)
            link(v.memset(ccq[:], 0.0))

            def scale_rows(it, k):
                v.wait_ge(std_ready, k)
                v.reciprocal(rstd[:, 0, :], std[:, 0, :]).then_inc(rstd_ready, 1)
                v.wait_ge(rstd_ready, k)
                for n in range(NT):
                    v.tensor_scalar(xb[:, n, :], xb[:, n, :], rstd[:, 0, n:n + 1], None, ALU.mult)\
                        .then_inc(rows_ready, 1)

            def evacuate_lo(it, gain):
                for k in range(KD):
                    v.wait_ge(hi_done, KD * it + k + 1)
                    v.scalar_tensor_tensor(out=t_lo[:, k, :], in0=ps[:, 4 + k % 2, :], scalar=gain[:, k:k + 1],
                                           in1=t_hi[:, k, :].bitcast(F32), op0=ALU.mult, op1=ALU.subtract)\
                        .then_inc(lo_done, 1)

            before = made[0]
            STEPS = 16
            with v.Fori(0, NB) as i:
                scale_rows(i, i + 1)
                evacuate_lo(i, g_mix)
                count = [0]

                def step(ins):
                    count[0] += 1
                    ins.then_inc(dve, 1)
                    v.wait_ge(dve, before + STEPS * i + count[0])

                qg = bass.ds(GQ * i, GQ)
                powers = lambda t, ri: t[:, ri, :, qg].rearrange("p j g -> p g j").unsqueeze(3)\
                    .broadcast_to([P, GQ, CH, H])
                coeffs = lambda t, ri: t[:, ri, qg, :].unsqueeze(2).broadcast_to([P, GQ, CH, H])
                t1 = g1[:].rearrange("p (g j h) -> p g j h", g=GQ, j=CH)
                t2 = g2[:].rearrange("p (g j h) -> p g j h", g=GQ, j=CH)
                v.wait_ge(l_ready, START + i)
                for half, d in ((slice(0, NP_), 0), (slice(NP_, P), 1)):
                    step(v.tensor_copy(ccq[half, 0, :, d], cc[half, 0, qg]))
                    step(v.tensor_copy(ccq[half, 1, :, d], cc[half, 2, qg]))
                step(v.tensor_tensor(t1, powers(pe, 0), coeffs(bb, 0), ALU.mult))
                step(v.tensor_tensor(t2, powers(pe, 1), coeffs(bb, 1), ALU.mult))
                step(v.tensor_tensor(gg[:, 0], t1, t2, ALU.subtract))
                step(v.tensor_tensor(t1, powers(pe, 0), coeffs(bb, 1), ALU.mult))
                step(v.tensor_tensor(t2, powers(pe, 1), coeffs(bb, 0), ALU.mult))
                step(v.tensor_tensor(gg[:, 1], t1, t2, ALU.add))
                v.nop().then_inc(g_ready, 1)
                v.wait_ge(ef_stored, START_DMA + 32 * i)
                fv = [f_sb[:, ri].rearrange("p g (j h) -> p g j h", j=CH) for ri in range(2)]
                step(v.tensor_tensor(t1, powers(pf, 0), coeffs(cc, 0), ALU.mult))
                step(v.tensor_tensor(t2, powers(pf, 1), coeffs(cc, 1), ALU.mult))
                step(v.tensor_tensor(fv[0], t1, t2, ALU.subtract))
                step(v.tensor_tensor(t1, powers(pf, 0), coeffs(cc, 2), ALU.mult))
                step(v.tensor_tensor(t2, powers(pf, 1), coeffs(cc, 0), ALU.mult))
                step(v.tensor_tensor(fv[1], t1, t2, ALU.subtract))
                v.nop().then_inc(f_ready, 1)
                assert count[0] == STEPS
            made[0] = before + STEPS * NB
            v.wait_ge(dve, made[0])
            v.wait_ge(l_evac, START + NB)
            v.wait_ge(k0_moved, 16)
            tt(lf[96:P, 0], lf[96:P, 0], kx[96:P], ALU.add)
            tt(lf[96:P, 0], lf[96:P, 0], d_b[96:P], ALU.add)
            v.nop().then_inc(lf_full, 1)

            v.wait_ge(m_stored, 16 * (2 * CH - 1))
            v.wait_ge(ef_stored, START_DMA + 32 * NB)
            link(v.memset(x_sb[:], 0.0))
            before2 = made[0]
            STEPS2 = 4 * (SUP - 1) + 1 + 16 + 4 + 4 * 5
            with v.Fori(0, NB) as i:
                count = [0]

                def step(ins, wait=True):
                    count[0] += 1
                    ins.then_inc(dve, 1)
                    if wait:
                        v.wait_ge(dve, before2 + STEPS2 * i + count[0])

                scale_rows(NB + i, NB + i + 1)
                evacuate_lo(NB + i, g_mix)
                qg = bass.ds(GQ * i, GQ)
                for r in range(4):
                    for ri in range(2):
                        v.wait_ge(st_ready, 8 * i + 2 * r + ri + 1)
                        v.tensor_copy(s_sb[NP_:P, ri, 2 * r:2 * r + 2, ::-1],
                                      ps[NP_:P, 6 + ri, :].rearrange("p (g c) -> p g c", g=2))\
                            .then_inc(st_bwd, 1)
                v.wait_ge(st_fwd, 8 * i + 8)
                v.wait_ge(st_bwd, 8 * i + 8)
                sv = s_sb[:].rearrange("p r g (d e) -> p r g d e", e=SUP)

                def local(e):
                    prev = sv[:, :, :, :, e - 1]
                    shape = [P, 2, GQ, ND]
                    step(v.tensor_tensor(sc1[:], prev, qr_t[:, 0:1, qg].unsqueeze(3).broadcast_to(shape), ALU.mult),
                         False)
                    step(v.tensor_tensor(sc2[:], prev[:, ::-1],
                                         qi_t[:, 0, :, qg].unsqueeze(3).broadcast_to(shape), ALU.mult))
                    step(v.tensor_tensor(sc1[:], sc1[:], sc2[:], ALU.add))
                    step(v.tensor_tensor(sv[:, :, :, :, e], sv[:, :, :, :, e], sc1[:], ALU.add))

                def super_scan():
                    step(v.tensor_copy(bnd[:], sv[:, :, :, :, SUP - 1]))
                    for lev in range(4):
                        sh = 1 << lev
                        w = ND - sh
                        shape = [P, 2, GQ, w]
                        prev = bnd[:, :, :, 0:w]
                        pr = qr_t[:, SUP - 1 + lev:SUP + lev, qg].unsqueeze(3).broadcast_to(shape)
                        pi = qi_t[:, SUP - 1 + lev, :, qg].unsqueeze(3).broadcast_to(shape)
                        step(v.tensor_tensor(sc1[:, :, :, 0:w], prev, pr, ALU.mult), False)
                        step(v.tensor_tensor(sc2[:, :, :, 0:w], prev[:, ::-1], pi, ALU.mult))
                        step(v.tensor_tensor(sc1[:, :, :, 0:w], sc1[:, :, :, 0:w], sc2[:, :, :, 0:w], ALU.add))
                        step(v.tensor_tensor(bnd[:, :, :, sh:], bnd[:, :, :, sh:], sc1[:, :, :, 0:w], ALU.add))

                def fix_up():
                    v.wait_ge(y_ready, START + 4 * i)
                    for ri in range(2):
                        step(v.tensor_copy(x_sb[0:NP_, ri, :, 2:2 + SUP], s_sb[0:NP_, ri, :, 0:SUP]), False)
                        step(v.tensor_copy(x_sb[NP_:P, ri, :, NC - 1:NC - 1 - SUP:-1], s_sb[NP_:P, ri, :, 0:SUP]),
                             False)
                    for g0 in (0, 4):
                        shape = [P, 4, SUP, ND - 1]
                        qs = bass.ds(GQ * i + g0, 4)
                        for ri in range(2):
                            over = lambda t: t.rearrange("p e g -> p g e").unsqueeze(3).broadcast_to(shape)
                            b_ = lambda r: bnd[:, r, g0:g0 + 4, 0:ND - 1].unsqueeze(2).broadcast_to(shape)
                            step(v.tensor_tensor(fx1[:], b_(ri), over(qr_t[:, 0:SUP, qs]), ALU.mult), False)
                            step(v.tensor_tensor(fx2[:], b_(1 - ri), over(qi_t[:, 0:SUP, ri, qs]), ALU.mult))
                            step(v.tensor_tensor(fx1[:], fx1[:], fx2[:], ALU.add))
                            view = lambda t: t.rearrange("p g (d e) -> p g e d", e=SUP)
                            step(v.tensor_tensor(view(x_sb[0:NP_, ri, g0:g0 + 4, 2 + SUP:2 + NC]),
                                                 view(s_sb[0:NP_, ri, g0:g0 + 4, SUP:NC]), fx1[0:NP_], ALU.add),
                                 False)
                            step(v.tensor_tensor(view(x_sb[NP_:P, ri, g0:g0 + 4, NC - 1 - SUP::-1]),
                                                 view(s_sb[NP_:P, ri, g0:g0 + 4, SUP:NC]), fx1[NP_:P], ALU.add))
                    v.nop().then_inc(fixed, 1)

                pieces = (lambda: [local(e) for e in range(1, 6)], lambda: [local(e) for e in range(6, 11)],
                          lambda: [*(local(e) for e in range(11, SUP)), super_scan()], fix_up)
                for m in range(CT):
                    pieces[m]()
                    v.wait_ge(sig_done, CT * i + m + 1)
                    v.wait_ge(c_stored[m % 2], START_DMA + 16 * (2 * i + m // 2))
                    v.tensor_tensor(c_st[:, m % 2, :], ps[:, 2 * (m % 2), :], sig_st[:, m % 2, :], ALU.mult)\
                        .then_inc(c_done[m % 2], 1)
                assert count[0] == STEPS2, count[0]

            def conv_start():
                for c in range(CT):
                    v.tensor_scalar(cv[:, c, :], cin[:, c, 0:TB], conv_w[:, c, 0:1], conv_b[:, c:c + 1],
                                    ALU.mult, ALU.add).then_inc(conv_chain[c], 1)

            def conv_tap(k, n):
                for c in range(CT):
                    v.wait_ge(conv_chain[c], n)
                    v.scalar_tensor_tensor(out=cv[:, c, :], in0=cin[:, c, bass.ds(k, TB)],
                                           scalar=conv_w[:, c, bass.ds(k, 1)], in1=cv[:, c, :],
                                           op0=ALU.mult, op1=ALU.add).then_inc(conv_chain[c], 1)

            v.wait_ge(cin_landed, 16)
            for n in range(2):
                v.wait_ge(c_stored[n], START_DMA + 16 * 2 * NB)
            v.wait_ge(y_ready, START + 4 * NB)
            conv_start()
            with v.Fori(1, TAPS) as k:
                conv_tap(k, k)
            for c in range(CT):
                v.wait_ge(conv_chain[c], TAPS)
            v.nop().then_inc(conv_done, 1)
            v.wait_ge(gp_in, 32)
            with v.Fori(0, NB) as b:
                it = 2 * NB + b
                for k in range(CT):
                    v.wait_ge(zhi_done, CT * b + k + 1)
                    v.tensor_tensor(t_lo[:, CT + k, :], z_sb[:, k, :], t_hi[:, CT + k, :].bitcast(F32),
                                    ALU.subtract).then_inc(zlo_done, 1)
                v.wait_ge(mean_ready, b + 1)
                for k in range(CT):
                    v.tensor_tensor(cv[:, k, :], cv[:, k, :], ps[:, 4, :], ALU.subtract).then_inc(dev_done, 1)
                v.wait_ge(lstd_ready, b + 1)
                v.reciprocal(ln_rstd[:], ln_std[:]).then_inc(ln_chain, 1)
                v.wait_ge(ln_chain, b + 1)
                v.wait_ge(sq_done, CT * b + CT)
                for k in range(CT):
                    v.tensor_tensor(cv[:, k, :], cv[:, k, :], ln_rstd[:], ALU.mult).then_inc(norm_done, 1)
                for k in range(CT):
                    v.wait_ge(silu_done, CT * b + k + 1)
                    v.tensor_copy(t_hi[:, k, :], cn[:, k, :]).then_inc(chi_done, 1)
                for k in range(CT):
                    v.wait_ge(chi_done, CT * b + k + 1)
                    v.tensor_tensor(t_lo[:, k, :], cn[:, k, :], t_hi[:, k, :].bitcast(F32), ALU.subtract)\
                        .then_inc(c_split, 1)
                natural = lambda t: t.rearrange("p (c j) -> p j c", j=CH)
                steps = lambda t: t.rearrange("p (j c) -> p j c", j=CH)
                for k in range(CT):
                    v.wait_ge(gate_done, CT * b + k + 1)
                    v.tensor_tensor(sg[:, k, :], sg[:, k, :], z_sb[:, k, :], ALU.mult).then_inc(s_done, 1)
                v.wait_ge(used[1], START + USE_BLK + PER_BLK * b + 1)
                for k in range(CT):
                    v.wait_ge(s_done, CT * b + k + 1)
                    v.tensor_copy(natural(t_hi[:, CT + k, :]), steps(sg[:, k, :])).then_inc(shi_done, 1)
                for k in range(CT):
                    v.wait_ge(shi_done, CT * b + k + 1)
                    v.tensor_tensor(natural(t_lo[:, CT + k, :]), steps(sg[:, k, :]),
                                    natural(t_hi[:, CT + k, :].bitcast(F32)), ALU.subtract)\
                        .then_inc(s_split, 1)
                bank2 = lambda n: ps[:, 2 * n:2 * n + 2, :].rearrange("p a n -> p (a n)")

                def residual(which, gain):
                    v.wait_ge(std_ready, 2 * NB + 3 * b + which + 1)
                    v.reciprocal(rstd[:, which, :], std[:, which, :]).then_inc(rstd_ready, 1)
                    v.wait_ge(rstd_ready, 2 * NB + 3 * b + which + 1)
                    for n in range(NT):
                        v.wait_ge(rows_added, START + 2 * NT * b + NT * (which // 2) + n)
                        v.scalar_tensor_tensor(out=tmp[:], in0=bank2(n), scalar=rstd[:, which, n:n + 1],
                                               in1=gain[:], op0=ALU.mult, op1=ALU.mult).then_inc(tmp_made, 1)
                        v.wait_ge(tmp_made, 2 * NT * b + NT * (which // 2) + n + 1)
                        if which == 0:
                            v.wait_ge(x_landed[n], 16 * (it + 2))
                        v.tensor_tensor(xb[:, n, :], xb[:, n, :], tmp[:], ALU.add)\
                            .then_inc(rows_added, 1)

                residual(0, gp_mix)
                v.wait_ge(std_ready, 2 * NB + 3 * b + 2)
                v.reciprocal(rstd[:, 1, :], std[:, 1, :]).then_inc(rstd_ready, 1)
                v.wait_ge(rstd_ready, 2 * NB + 3 * b + 2)
                for n in range(NT):
                    v.tensor_scalar(xn[:, n, :], xb[:, n, :], rstd[:, 1, n:n + 1], None, ALU.mult)\
                        .then_inc(rows_ready, 1)
                evacuate_lo(it, g_ffn)

                def hidden(m, w, n):
                    v.wait_ge(silu_h, FT * b + m + 1)
                    v.tensor_tensor(act_t[:, w, :], act_t[:, w, :], ps[:, 2 * w + 1, :], ALU.mult)\
                        .then_inc(hid_made[w], 1)
                    v.wait_ge(hid_made[w], n + 1)
                    v.tensor_copy(hid_hi[:, bass.ds(m, 1), :].rearrange("p a n -> p (a n)"), act_t[:, w, :])\
                        .then_inc(hid_hi_done[w], 1)
                    v.wait_ge(hid_hi_done[w], n + 1)
                    v.tensor_tensor(hid_lo[:, bass.ds(m, 1), :].rearrange("p a n -> p (a n)"), act_t[:, w, :],
                                    hid_hi[:, bass.ds(m, 1), :].bitcast(F32).rearrange("p a n -> p (a n)"),
                                    ALU.subtract).then_inc(hid_done[w], 1)

                v.wait_ge(cin_landed, 16 * (b + 2))
                v.wait_ge(silu_done, CT * b + CT)
                conv_start()
                with v.Fori(0, (TAPS - 1) // 3) as t:
                    for w in range(2):
                        hidden(2 * t + w, w, FT // 2 * b + t)
                        for k in ((1, 2), (3,))[w]:
                            conv_tap(3 * t + k, TAPS * (b + 1) + 3 * t + k)
                for w in range(2):
                    hidden(FT - 2 + w, w, FT // 2 * b + FT // 2 - 1)
                for c in range(CT):
                    v.wait_ge(conv_chain[c], TAPS * (b + 2))
                v.nop().then_inc(conv_done, 1)
                residual(2, gp_ffn)

        @block.tensor
        def _(pe_):
            for s in (*used, l_ready, y_ready):
                pe_.sem_inc(s, START)
            def split_product(o, slot_w, act_hi, act_lo, weights_first, start, stop):
                whi, wlo = slot_w
                if weights_first:
                    parts = ((whi, act_hi), (whi, act_lo), (wlo, act_hi))
                else:
                    parts = ((act_hi, whi), (act_hi, wlo), (act_lo, whi))
                for n, (l, r) in enumerate(parts):
                    last = pe_.matmul(o, l, r, start=start and n == 0, stop=stop and n == 2)
                return last

            pe_.wait_ge(ident_ready, 1)
            pe_.wait_ge(prm_in, 1)
            for n in range(3):
                pe_.transpose(ps[:, 0, n * G:(n + 1) * G], prm[:, n].rearrange("g d p -> g (d p)"),
                              ident[0:G, 0:G])
            for ri in range(2):
                for o in range(4):
                    pe_.transpose(ps[:, 1 + ri, o * P:(o + 1) * P],
                                  c_raw[:, ri, o].rearrange("q d p -> q (d p)"), ident[:])
            for c in range(CT):
                last = pe_.transpose(ps[:, 3, c * TAPS:(c + 1) * TAPS], cw_raw[:, c * P:(c + 1) * P],
                                     ident[0:TAPS, 0:TAPS])
            last.then_inc(prm_t, 1)

            def transpose_rows(it, rows):
                pe_.wait_ge(rows_ready, NT * (it + 1))
                for k in range(KD):
                    if k < 2:
                        pe_.wait_ge(lo_done, START + KD * it)
                    else:
                        pe_.wait_ge(lo_done, START + KD * it + k - 1)
                    for n in range(NT):
                        last = pe_.transpose(ps[:, 4 + k % 2, n * P:(n + 1) * P], rows[:, n, k * P:(k + 1) * P],
                                             ident[:])
                    last.then_inc(tp_ready, 1)

            def project(slot, n, bank, it, first):
                pe_.wait_ge(split_done[slot], START + n + 1)
                wh = w_hi[:, slot, :].rearrange("p (k m) -> p k m", k=KD)
                wl = w_lo[:, slot, :].rearrange("p (k m) -> p k m", k=KD)
                for k in range(KD):
                    if first:
                        pe_.wait_ge(lo_done, START + KD * it + k + 1)
                    last = split_product(ps[:, bank, :], (wh[:, k], wl[:, k]), t_hi[:, k, :], t_lo[:, k, :], True,
                                         k == 0, k == KD - 1)
                return last.then_inc(used[slot], 1)

            pe_.wait_ge(dve, 6)
            with pe_.Fori(0, NB) as i:
                transpose_rows(i, xb)
                for m in range(CT):
                    pe_.wait_ge(u_evac[m], START + i)
                    project(m, i, m, i, m == 0)
                pe_.wait_ge(g_ready, i + 1)
                for r in range(4):
                    pe_.wait_ge(e_evac, START + 4 * i + r)
                    for n in range(4):
                        last = pe_.transpose(ps[:, 6, n * P:(n + 1) * P],
                                             gg[:, r // 2, 4 * (r % 2) + n].rearrange("p j h -> p (j h)"), ident[:])
                    last.then_inc(et_ready, 1)
                pe_.wait_ge(l_evac, START + i)
                for g in range(GQ):
                    for ri in range(2):
                        last = pe_.matmul(ps[:, 7, 2 * H * g:2 * H * (g + 1)],
                                          gg[:, ri, g].rearrange("p j h -> p (j h)"),
                                          ccq[:, ri, g].rearrange("p f h -> p (f h)"), start=ri == 0, stop=ri == 1)
                last.then_inc(l_ready, 1)

            pe_.wait_ge(l_evac, START + NB)
            with pe_.Fori(0, NB) as i:
                transpose_rows(NB + i, xb)
                pe_.wait_ge(s5_landed, 16 * (CH + 3) * (i + 1))
                for r in range(4):
                    for ri in range(2):
                        if r == 0:
                            pe_.wait_ge(z_done, START + 4 * i)
                        else:
                            pe_.wait_ge(st_fwd, 8 * i + 2 * (r - 1) + ri + 1)
                            pe_.wait_ge(st_bwd, 8 * i + 2 * (r - 1) + ri + 1)
                        for n in range(2):
                            last = pe_.matmul(ps[:, 6 + ri, n * NC:(n + 1) * NC], e_sb[:, ri, 2 * r + n],
                                              u_sb[:, 2 * r + n], start=True, stop=True)
                        last.then_inc(st_ready, 1)
                for m in range(CT):
                    if m < 2:
                        pe_.wait_ge(c_done[m % 2], START + 2 * i)
                    else:
                        pe_.wait_ge(c_done[m % 2], START + 2 * i + 1)
                    for w in range(2):
                        u = 2 * m + w
                        project(u % RING, USE_VG + 2 * i + u // RING, 2 * (m % 2) + w, NB + i, u == 0)
                pe_.wait_ge(m_laid, i + 1)
                pe_.wait_ge(fixed, START + i + 1)
                for r in range(4):
                    if r < 2:
                        pe_.wait_ge(st_fwd, 8 * i + 8)
                        pe_.wait_ge(st_bwd, 8 * i + 8)
                    else:
                        pe_.wait_ge(z_done, START + 4 * i + r - 1)
                    for n in range(2):
                        g = 2 * r + n
                        o = ps[:, 6 + r % 2, n * NC:(n + 1) * NC]
                        pe_.matmul(o, m_sb[:, g], u_sb[:, g], start=True, stop=False)
                        for ri in range(2):
                            last = pe_.matmul(o, f_sb[:, ri, g], x_sb[:, ri, g, 1:NC + 1], start=False, stop=ri == 1)
                    last.then_inc(y_ready, 1)

            for m in range(2):
                pe_.wait_ge(c_done[m], START + 2 * NB)
            pe_.wait_ge(z_done, START + 4 * NB)
            pe_.wait_ge(pool_consts, 4)
            with pe_.Fori(0, NB) as b:
                it = 2 * NB + b
                use = USE_BLK + PER_BLK * b
                pe_.wait_ge(rows_added, START + 2 * NT * b)
                for u in range(GLU_UNITS):
                    pe_.wait_ge(split_done[u], START + use + 1)
                    wh = w_hi[:, u, :].rearrange("p (k m) -> p k m", k=CT)
                    wl = w_lo[:, u, :].rearrange("p (k m) -> p k m", k=CT)
                    for mm in range(2):
                        m = 2 * u + mm
                        cols = slice(mm * P, (mm + 1) * P)
                        for k in range(CT):
                            if m == 0:
                                pe_.wait_ge(zlo_done, CT * b + k + 1)
                            last = split_product(ps[:, m, :], (wh[:, k, cols], wl[:, k, cols]), t_hi[:, CT + k, :],
                                                 t_lo[:, CT + k, :], True, k == 0, k == CT - 1)
                    last.then_inc(used[u], 1)
                pe_.wait_ge(conv_done, b + 1)
                for k in range(CT):
                    last = pe_.matmul(ps[:, 4, :], mean_w[:], cv[:, k, :], start=k == 0, stop=k == CT - 1)
                last.then_inc(mean_ready, 1)
                for k in range(CT):
                    pe_.wait_ge(sq_done, CT * b + k + 1)
                    last = pe_.matmul(ps[:, 5, :], mean_w[:], sq[:, k, :], start=k == 0, stop=k == CT - 1)
                last.then_inc(var_ready, 1)

                def rows_product(units, at, act_of, ready, done):
                    total = sum(len(x_) for x_ in units)
                    n0 = 0
                    for group in units:
                        for tt_ in range(NT):
                            for j, k in enumerate(group):
                                u = at + k
                                slot = u % RING
                                if tt_ == 0:
                                    pe_.wait_ge(split_done[slot], START + use + u // RING + 1)
                                    ready(k)
                                toks = slice(tt_ * P, (tt_ + 1) * P)
                                hi_, lo_ = act_of(k)
                                for a in range(2):
                                    cols = slice(a * TB, (a + 1) * TB)
                                    last = split_product(ps[:, 2 * tt_ + a, :],
                                                         (w_hi[:, slot, cols], w_lo[:, slot, cols]),
                                                         hi_[:, toks], lo_[:, toks], False, n0 + j == 0,
                                                         n0 + j == total - 1)
                                if tt_ == NT - 1:
                                    last.then_inc(used[slot], 1)
                            if group is units[-1] and tt_ < NT - 1:
                                last.then_inc(done, 1)
                        n0 += len(group)

                def mixed_in(k):
                    if k < CT:
                        pe_.wait_ge(c_split, CT * b + k + 1)
                    else:
                        pe_.wait_ge(s_split, CT * b + k - CT + 1)
                    if k == 0:
                        pe_.wait_ge(gate_done, CT * b + CT)
                        pe_.wait_ge(lstd_ready, b + 1)

                rows_product([[k] for k in range(KD - 2)] + [[KD - 2, KD - 1]], GLU_UNITS,
                             lambda k: (t_hi[:, k, :], t_lo[:, k, :]), mixed_in, mixed_ready)
                pe_.wait_ge(rows_added, START + 2 * NT * b + NT)
                transpose_rows(it, xn)
                at = GLU_UNITS + KD
                with pe_.Fori(0, FT // 2) as t:
                    pe_.wait_ge(lo_done, START + KD * (it + 1))
                    for w in range(2):
                        pe_.wait_ge(hid_done[w], START + FT // 2 * b + t)
                        for a in range(2):
                            u = at + 2 * w + a
                            project(u % RING, use + u // RING + t, 2 * w + a, it, False)
                at += 2 * FT
                for w in range(2):
                    pe_.wait_ge(hid_done[w], START + FT // 2 * (b + 1))
                rows_product([[k] for k in range(FT - 2)] + [[FT - 2, FT - 1]], at,
                             lambda k: (hid_hi[:, k, :], hid_lo[:, k, :]), lambda k: None, down_tile)


_INS = ["x", "mix_norm_pre", "mix_norm_post", "w_in", "conv_dw_w", "conv_dw_b", "conv_ln_g", "conv_ln_b",
        "ssm_a_re", "ssm_a_im", "ssm_log_dt", "ssm_b_re", "ssm_b_im", "ssm_c_re", "ssm_c_im", "ssm_d",
        "ssm_glu_w", "ssm_glu_b", "w_out", "ffn_norm_pre", "ffn_norm_post", "ffn_w_gate", "ffn_w_up",
        "ffn_w_down"]


def kernel(**inputs):
    import numpy as _np
    import concourse.bacc as _bacc
    from concourse import mybir as _mybir
    from concourse.bass_utils import run_bass_kernel_spmd as _run

    nc = _bacc.Bacc("TRN2", target_bir_lowering=False, num_devices=1, dynamic_dma_scratch_size=1024)
    arrays, args = {}, []
    for name in _INS:
        a = _np.ascontiguousarray(inputs[name])
        arrays[f"in_{name}_dram"] = a
        args.append(nc.dram_tensor(f"in_{name}_dram", a.shape, _mybir.dt.from_np(a.dtype), kind="ExternalInput").ap())
    shape = inputs["x"].shape
    args.append(nc.dram_tensor("out_dram", shape, _mybir.dt.float32, kind="ExternalOutput").ap())
    hybrid_encoder(nc, *args)
    r = _run(nc, [arrays], core_ids=[0])
    return r.results[0]["out_dram"]
```

```python
import math
from contextlib import ExitStack

import concourse.bass as bass
from concourse import mybir

F32 = mybir.dt.float32
F32R = mybir.dt.float32r
I32 = mybir.dt.int32
ALU = mybir.AluOpType
ACT = mybir.ActivationFunctionType

P = 128
TB = 512
EPS = 1e-6
N_CONSTS = 19
HALF, HSIN, HABS, HCOS = 6, 7, 8, 18
START, START_DMA = 1, 16
SQ0 = 32
RING = 4
CH = 8
SUP = 16
GQ = 8
MAGIC = 12582912.0


def hybrid_encoder(nc, x, mix_norm_pre, mix_norm_post, w_in, conv_dw_w, conv_dw_b, conv_ln_g,
                   conv_ln_b, ssm_a_re, ssm_a_im, ssm_log_dt, ssm_b_re, ssm_b_im, ssm_c_re,
                   ssm_c_im, ssm_d, ssm_glu_w, ssm_glu_b, w_out, ffn_norm_pre, ffn_norm_post,
                   ffn_w_gate, ffn_w_up, ffn_w_down, out):
    _, T, D = x.shape
    KD = D // P
    NB = T // TB
    NT = TB // P
    CW = conv_dw_w.shape[2]
    CT = CW // P
    TAPS = conv_dw_w.shape[1]
    HALO = TAPS // 2
    CPAD = T + 2 * HALO
    CIN = TB + 2 * HALO
    _, _, G, NP_, H = ssm_b_re.shape
    NC = T // CH
    ND = NC // SUP
    CB = TB // CH
    FT = ffn_w_gate.shape[2] // P
    assert CH * H == P and 2 * NP_ == P and G == 4 * GQ and NB == 4 and KD == 8

    UNITS_U, UNITS_VG = CT, 2 * CT
    GLU_UNITS = 2
    USE_VG = NB * UNITS_U // RING
    USE_BLK = USE_VG + NB * UNITS_VG // RING
    UNITS_BLK = GLU_UNITS + KD + 2 * FT + FT
    PER_BLK = UNITS_BLK // RING
    assert UNITS_BLK % RING == 0 and UNITS_U == RING

    def scratch(name, shape):
        return nc.dram_tensor(name, shape, F32, kind="Internal").ap()

    u_d = scratch("u_scratch", [G, H, CH, NC])
    z_d = scratch("z_scratch", [G, H, CH, NC])
    c_d = scratch("c_scratch", [CT, P, CPAD])
    t_d = scratch("t_scratch", [NB, H, 2 * CH, GQ * H])

    with ExitStack() as ctx:
        def sb(name, shape, dt=F32, scope=ctx):
            return scope.enter_context(nc.sbuf_tensor(name, shape, dt))

        def sem(name):
            return ctx.enter_context(nc.semaphore(name))

        def sems(name, n):
            return [sem(f"{name}{i}") for i in range(n)]

        ident = sb("ident", [P, P])
        mean_w = sb("mean_w", [P, P])
        xb = sb("xb", [P, NT, D])
        raw = sb("raw", [P, RING, D])
        w_hi = sb("w_hi", [P, RING, D], F32R)
        w_lo = sb("w_lo", [P, RING, D], F32R)
        t_hi = sb("t_hi", [P, KD, TB], F32R)
        t_lo = sb("t_lo", [P, KD, TB], F32R)
        g_mix = sb("g_mix", [P, KD])
        g_ffn = sb("g_ffn", [P, KD])
        ln_g = sb("ln_g", [P, CT])
        ln_b = sb("ln_b", [P, CT])
        glu_b = sb("glu_b", [P, CT])
        conv_b = sb("conv_b", [P, CT])
        conv_w = sb("conv_w", [P, CT, TAPS])
        ssq = sb("ssq", [P, 3, NT])
        std = sb("std", [P, 3, NT])
        rstd = sb("rstd", [P, 3, NT])
        epsc = sb("epsc", [P, 1])
        halfpi = sb("halfpi", [P, 1])

        pscope = ExitStack()
        psb = lambda name, shape, dt=F32: sb(name, shape, dt, pscope)
        shared = psb("shared", [P, D])
        sig_st = psb("sig_st", [P, 2, TB])
        c_st = psb("c_st", [P, 2, TB])
        e_sb = psb("e_sb", [P, 2, GQ, P])
        f_sb = psb("f_sb", [P, 2, GQ, H, CH])
        gg = psb("gg", [P, 2, GQ, H, CH])
        bbq = psb("bbq", [P, 2, GQ, H])
        ccq = psb("ccq", [P, 2, GQ, 2, H])
        bb = psb("bb", [P, 2, G, H])
        cc = psb("cc", [P, 3, G, H])
        pe = psb("pe", [P, 2, CH, G])
        pf = psb("pf", [P, 2, CH, G])
        dd = psb("dd", [H, G, H])
        lf = psb("lf", [P, 2, GQ, H])
        l0 = psb("l0", [H, GQ, H])
        qr_t = psb("qr_t", [P, SUP + 3, G])
        qi_t = psb("qi_t", [P, SUP + 3, 2, G])
        pt = psb("pt", [P, GQ, H, CH])
        lscope = ExitStack()
        lsb = lambda name, shape, dt=F32: sb(name, shape, dt, lscope)
        u_sb = lsb("u_sb", [P, GQ, NC])
        m_sb = lsb("m_sb", [P, GQ, CH * H])
        s_sb = lsb("s_sb", [P, 2, GQ, NC])
        x_sb = lsb("x_sb", [P, 2, GQ, NC + 2])
        bnd = lsb("bnd", [P, 2, GQ, ND])
        fx1 = lsb("fx1", [P, 4, SUP, ND - 1])
        fx2 = lsb("fx2", [P, 4, SUP, ND - 1])
        sc1, sc2 = (t[:].rearrange("p a b c -> p (a b c)")[:, 0:2 * GQ * ND]
                    .rearrange("p (a g d) -> p a g d", a=2, g=GQ) for t in (fx1, fx2))
        sq_junk = shared[:]
        m_in = shared[:].rearrange("p (j n) -> p j n", j=CH)
        z_st = shared[:].rearrange("p (a g c) -> p a g c", a=2, g=2)
        lscope.close()
        rscope = ExitStack()
        rsb = lambda name, shape, dt=F32: sb(name, shape, dt, rscope)
        u_st = rsb("u_st", [P, CT, TB])
        zeros = rsb("zeros", [P, CT, HALO])
        cw_raw = rsb("cw_raw", [TAPS, CW])
        prm = rsb("prm", [G, 3, 2, NP_])
        ldt_raw = rsb("ldt_raw", [G, 2])
        c_raw = rsb("c_raw", [P, 2, 4, 2, NP_])
        b_in = rsb("b_in", [P, 2, G, H])
        lam = rsb("lam", [P, 3, G])
        pv = rsb("pv", [P, 24, G])
        pvi = rsb("pvi", [P, G], I32)
        pw = rsb("pw", [P, 2, CH + 1, G])
        g1 = rsb("g1", [P, G * H])
        g2 = rsb("g2", [P, G * H])
        rscope.close()
        pscope.close()

        fscope = ExitStack()
        fsb = lambda name, shape, dt=F32: sb(name, shape, dt, fscope)
        cin = fsb("cin", [P, CT, CIN + 2])
        cv = fsb("cv", [P, CT, TB])
        gp_mix = fsb("gp_mix", [P, D])
        gp_ffn = fsb("gp_ffn", [P, D])
        tmp = fsb("tmp", [P, D])
        act_t = fsb("act_t", [P, 2, TB])
        junk = fsb("junk", [P, D])
        hscope = ExitStack()
        hid_hi = sb("hid_hi", [P, FT, TB], F32R, hscope)
        hid_lo = sb("hid_lo", [P, FT, TB], F32R, hscope)
        hscope.close()
        mscope = ExitStack()
        msb = lambda name, shape, dt=F32: sb(name, shape, dt, mscope)
        z_sb = msb("z_sb", [P, CT, TB])
        sg = msb("sg", [P, CT, TB])
        sq = msb("sq", [P, CT, TB])
        cn = msb("cn", [P, CT, TB])
        ln_std = msb("ln_std", [P, TB])
        ln_rstd = msb("ln_rstd", [P, TB])
        xn = msb("xn", [P, NT, D])
        mscope.close()
        fscope.close()

        ps = ctx.enter_context(nc.psum_tensor("ps", [P, 8, TB], F32))

        raw_landed = sems("raw_landed", RING)
        whi_done = sems("whi_done", RING)
        split_done = sems("split_done", RING)
        used = sems("used", RING)
        consts_in = sem("consts_in")
        s5_in = sem("s5_in")
        gp_in = sem("gp_in")
        pads_out = sem("pads_out")
        ident_zero = sem("ident_zero")
        ident_ready = sem("ident_ready")
        pool_consts = sem("pool_consts")
        zeros_ready = sem("zeros_ready")
        x_landed = sems("x_landed", NT)
        squares = sem("squares")
        std_ready = sem("std_ready")
        rstd_ready = sem("rstd_ready")
        rows_ready = sem("rows_ready")
        tp_ready = sem("tp_ready")
        hi_done = sem("hi_done")
        lo_done = sem("lo_done")
        u_evac = sems("u_evac", CT)
        u_stored = sems("u_stored", CT)
        dve = sem("dve_chain")
        act_chain = sem("act_chain")
        prm_t = sem("prm_t")
        prm_in = sem("prm_in")
        angle_ready = sem("angle_ready")
        trig_ready = sem("trig_ready")
        et_ready = sem("et_ready")
        e_evac = sem("e_evac")
        l_ready = sem("l_ready")
        l_evac = sem("l_evac")
        l_half = sem("l_half")
        disc_ready = sem("disc_ready")
        pool_p = sem("pool_products")
        pool_pause = sem("pool_pause")
        gg_ready = sem("gg_ready")
        f_ready = sem("f_ready")
        cq_ready = sem("cq_ready")
        t_stored = sem("t_stored")
        m_landed = sem("m_landed")
        u_landed = sem("u_landed")
        m_laid = sem("m_laid")
        st_ready = sem("st_ready")
        st_fwd = sem("st_fwd")
        st_bwd = sem("st_bwd")
        fixed = sem("fixed")
        sig_done = sem("sig_done")
        c_done = sems("c_done", 2)
        c_stored = sems("c_stored", 2)
        y_ready = sem("y_ready")
        z_done = sem("z_done")
        z_stored = sems("z_stored", 2)
        cin_landed = sem("cin_landed")
        conv_done = sem("conv_done")
        z_landed = sem("z_landed")
        zhi_done = sem("zhi_done")
        zlo_done = sem("zlo_done")
        gate_done = sem("gate_done")
        s_split = sem("s_split")
        mean_ready = sem("mean_ready")
        dev_done = sem("dev_done")
        sq_done = sem("sq_done")
        var_ready = sem("var_ready")
        lstd_ready = sem("lstd_ready")
        norm_done = sem("norm_done")
        silu_done = sem("silu_done")
        c_split = sem("c_split")
        mixed_ready = sem("mixed_ready")
        silu_h = sem("silu_h")
        hid_done = sems("hid_done", 2)
        out_stored = sem("out_stored")
        conv_chain = sems("conv_chain", CT)
        ln_chain = sem("ln_chain")
        chi_done = sem("chi_done")
        shi_done = sem("shi_done")
        s_done = sem("s_done")
        tmp_made = sem("tmp_made")
        rows_added = sem("rows_added")
        hid_made = sems("hid_made", 2)
        hid_hi_done = sems("hid_hi_done", 2)
        down_tile = sem("down_tile")

        block = ctx.enter_context(nc.Block())


        @block.sync
        def _(sp):
            def load(slot, n, src):
                sp.wait_ge(split_done[slot], START + n)
                sp.dma_start(raw[:, slot, :].rearrange("p (k m) -> p k m", k=src.shape[1]), src)\
                    .then_inc(raw_landed[slot], 16)

            w_in_v = w_in[0].rearrange("(k p) n -> p k n", p=P)
            with sp.Fori(0, NB) as i:
                for m in range(CT):
                    load(m, i, w_in_v[:, :, 2 * CW + m * P:2 * CW + (m + 1) * P])
            with sp.Fori(0, NB) as i:
                for m in range(CT):
                    for v in range(2):
                        u = 2 * m + v
                        load(u % RING, USE_VG + 2 * i + u // RING,
                             w_in_v[:, :, v * CW + m * P:v * CW + (m + 1) * P])
            glu_v = ssm_glu_w[0].rearrange("(k p) n -> p k n", p=P)
            w_out_v = w_out[0].rearrange("(k p) (a n) -> p k a n", p=P, a=1)
            gate_v = ffn_w_gate[0].rearrange("(k p) n -> p k n", p=P)
            up_v = ffn_w_up[0].rearrange("(k p) n -> p k n", p=P)
            down_v = ffn_w_down[0].rearrange("(k p) (a n) -> p k a n", p=P, a=1)
            with sp.Fori(0, NB) as b:
                use = USE_BLK + PER_BLK * b
                for u in range(GLU_UNITS):
                    load(u, use, glu_v[:, :, u * 2 * P:(u + 1) * 2 * P])
                for k in range(KD):
                    u = GLU_UNITS + k
                    load(u % RING, use + u // RING, w_out_v[:, k])
                at = GLU_UNITS + KD
                with sp.Fori(0, FT // 2) as t:
                    for v in range(4):
                        src = (gate_v, up_v)[v % 2]
                        load((at + v) % RING, use + (at + v) // RING + t,
                             src[:, :, bass.ds((2 * t + v // 2) * P, P)])
                at += 2 * FT
                for k in range(FT):
                    load((at + k) % RING, use + (at + k) // RING, down_v[:, k])

        @block.gpsimd
        def _(pool):
            for s in (*split_done, pool_p):
                pool.sem_inc(s, START)
            pool.memset(ident[:], 0.0).then_inc(ident_zero, 1)
            pool.wait_ge(ident_zero, 1)
            pool.affine_select(out=ident[:], in_=ident[:], compare_op=ALU.not_equal, fill=1.0, base=0,
                               pattern=[[-1, P]], channel_multiplier=1).then_inc(ident_ready, 1)
            pool.memset(zeros[:], 0.0).then_inc(zeros_ready, 1)
            pool.memset(mean_w[:], 1.0 / CW).then_inc(pool_consts, 1)
            pool.memset(epsc[:], EPS).then_inc(pool_consts, 1)
            pool.memset(halfpi[:], math.pi / 2).then_inc(pool_consts, 1)

            def split_lo(slot, n):
                pool.wait_ge(whi_done[slot], n + 1)
                pool.tensor_tensor(w_lo[:, slot, :], raw[:, slot, :], w_hi[:, slot, :].bitcast(F32),
                                   ALU.subtract).then_inc(split_done[slot], 1)

            shape = [P, GQ, H, CH]

            def product(part, q, out, powers, coeffs, im, made):
                pa = lambda ri: powers[:, ri, :, q].rearrange("p j g -> p g j").unsqueeze(2).broadcast_to(shape)
                co = lambda c: coeffs[:, c, q, :].unsqueeze(3).broadcast_to(shape)
                ri, k = divmod(part, 3)
                if k == 0:
                    pool.wait_ge(pool_p, START + made)
                    pool.nop().then_inc(pool_pause, 1)
                    pool.tensor_tensor(out[:, ri], pa(0), co((0, im)[ri]), ALU.mult).then_inc(pool_p, 1)
                elif k == 1:
                    pool.wait_ge(pool_p, START + made)
                    pool.nop().then_inc(pool_pause, 1)
                    pool.tensor_tensor(pt[:], pa(1), co((1, 0)[ri]), ALU.mult).then_inc(pool_p, 1)
                else:
                    pool.wait_ge(pool_p, START + made)
                    pool.nop().then_inc(pool_pause, 1)
                    pool.tensor_tensor(out[:, ri], out[:, ri], pt[:], (ALU.subtract, ALU.add)[ri] if im == 1
                                       else ALU.subtract).then_inc(pool_p, 1)

            quarter = lambda q: bass.ds(GQ * q, GQ)

            def gg_part(part, q):
                product(part, quarter(q), gg, pe, bb, 1, 12 * q + part)
                if part == 5:
                    pool.wait_ge(pool_p, START + 12 * q + 6)
                    pool.sem_inc(gg_ready, 1)

            def f_part(part, q):
                if part == 0:
                    pool.wait_ge(y_ready, START + 4 * q)
                product(part, quarter(q), f_sb, pf, cc, 2, 12 * q + 6 + part)
                if part == 5:
                    pool.wait_ge(pool_p, START + 12 * q + 12)
                    pool.sem_inc(f_ready, 1)

            with pool.Fori(0, NB - 1) as n:
                for slot in range(RING):
                    split_lo(slot, n)
            pool.wait_ge(disc_ready, 1)
            for part in range(6):
                gg_part(part, 0)
            for slot in range(RING):
                split_lo(slot, NB - 1)

            def beside_vg(i, last):
                for u in range(2 * RING):
                    split_lo(u % RING, USE_VG + 2 * i + u // RING)
                    if u < 3:
                        f_part(2 * u, i)
                        f_part(2 * u + 1, i)
                    elif u < 2 * RING - 2 and not last:
                        if u == 3:
                            pool.wait_ge(l_ready, START + i + 1)
                        gg_part(2 * (u - 3), i + 1)
                        gg_part(2 * (u - 3) + 1, i + 1)

            with pool.Fori(0, NB - 1) as i:
                beside_vg(i, False)
            beside_vg(NB - 1, True)
            with pool.Fori(USE_BLK, USE_BLK + NB * PER_BLK) as n:
                for slot in range(RING):
                    split_lo(slot, n)

        W_IN_X = x[0].rearrange("(b t p) d -> p b t d", t=NT, p=P)
        W_OUT_X = out[0].rearrange("(b t p) d -> p b t d", t=NT, p=P)

        @block.scalar
        def _(act):
            for s in (*u_evac, e_evac, squares, z_done):
                act.sem_inc(s, START)
            for s in (*u_stored, *c_stored, *z_stored, out_stored):
                act.sem_inc(s, START_DMA)
            loads = [(prm[:, 0], ssm_a_re[0].rearrange("d g p -> g d p")),
                     (prm[:, 1], ssm_a_im[0].rearrange("d g p -> g d p")),
                     (ldt_raw[:], ssm_log_dt[0].rearrange("d g -> g d")),
                     (cw_raw[:], conv_dw_w[0])]
            for ri, c_in in enumerate((ssm_c_re, ssm_c_im)):
                for d in range(2):
                    loads.append((c_raw[:, ri, :, d, :],
                                  c_in[0, d].rearrange("(o g) h p -> (g h) o p", o=4)))
            for ri, b_x in enumerate((ssm_b_re, ssm_b_im)):
                for d in range(2):
                    loads.append((b_in[d * NP_:(d + 1) * NP_, ri], b_x[0, d].rearrange("g p h -> p g h")))
            for dst, src in ((g_mix, mix_norm_pre), (g_ffn, ffn_norm_pre), (ln_g, conv_ln_g),
                             (ln_b, conv_ln_b), (glu_b, ssm_glu_b), (conv_b, conv_dw_b)):
                loads.append((dst[:], src[0].rearrange("(k p) -> p k", p=P)))
            loads.append((dd[:].rearrange("p g h -> p (g h)"), ssm_d[0].partition_broadcast(H)))
            assert len(loads) == N_CONSTS
            for tt in range(NT):
                act.dma_start(xb[:, tt, :], W_IN_X[:, 0, tt, :]).then_inc(x_landed[tt], 16)
            for dst, src in loads:
                act.dma_start(dst, src, allow_slow_non_contiguous=True).then_inc(consts_in, 16)
            act.wait_ge(zeros_ready, 1)
            for at in (0, HALO + T):
                act.dma_start(c_d[:, :, at:at + HALO].rearrange("c p t -> p c t"), zeros[:])\
                    .then_inc(pads_out, 16)

            def split_hi(slot, n):
                act.wait_ge(raw_landed[slot], 16 * (n + 1))
                act.wait_ge(used[slot], START + n)
                act.activation(w_hi[:, slot, :], raw[:, slot, :], ACT.Copy).then_inc(whi_done[slot], 1)

            def row_stats(it):
                for tt in range(NT):
                    act.wait_ge(x_landed[tt], 16 * it + 16)
                    if tt:
                        act.wait_ge(squares, START + 4 * it + tt)
                    else:
                        act.wait_ge(squares, START + 4 * it)
                    act.activation(sq_junk[:], xb[:, tt, :], ACT.Square, accum_out=ssq[:, 0, tt:tt + 1])\
                        .then_inc(squares, 1)
                act.wait_ge(squares, START + 4 * it + 4)
                act.activation(std[:, 0, :], ssq[:, 0, :], ACT.Sqrt, bias=epsc[:, 0:1], scale=1.0 / D)\
                    .then_inc(std_ready, 1)

            def evacuate_hi(it, gain):
                for k in range(KD):
                    act.wait_ge(tp_ready, KD * it + k + 1)
                    act.activation(t_hi[:, k, :], ps[:, 4 + k % 2, :], ACT.Copy, scale=gain[:, k:k + 1])\
                        .then_inc(hi_done, 1)

            def load_rows(it, nxt):
                for tt in range(NT):
                    act.dma_start(xb[:, tt, :], W_IN_X[:, nxt, tt, :]).then_inc(x_landed[tt], 16)

            act.wait_ge(pool_consts, 3)
            row_stats(0)
            def project_u(i):
                for u in range(RING):
                    split_hi(u, i)
                act.wait_ge(used[RING - 1], START + i)
                evacuate_hi(i, g_mix)
                load_rows(i + 1, (i + 1) % NB)

            def evacuate_u(i, m):
                act.wait_ge(used[m], START + i + 1)
                act.wait_ge(u_stored[m], START_DMA + 16 * i)
                act.activation(u_st[:, m, :].rearrange("p (j c) -> p j c", j=CH),
                               ps[:, m, :].rearrange("p (c j) -> p j c", j=CH), ACT.Copy).then_inc(u_evac[m], 1)
                act.wait_ge(u_evac[m], START + i + 1)
                act.dma_start(
                    u_d[m * GQ:(m + 1) * GQ, :, :, bass.ds(CB * i, CB)].rearrange("g h j c -> (g h) j c"),
                    u_st[:, m, :].rearrange("p (j c) -> p j c", j=CH)).then_inc(u_stored[m], 16)

            act.wait_ge(consts_in, 16 * N_CONSTS)
            project_u(0)
            evacuate_u(0, 0)
            evacuate_u(0, 1)
            row_stats(1)
            evacuate_u(0, 2)
            evacuate_u(0, 3)
            act.wait_ge(angle_ready, 1)
            act.activation(pv[:, HSIN], pv[:, HALF], ACT.Sin).then_inc(trig_ready, 1)
            act.activation(pv[:, HABS], pv[:, HALF], ACT.Abs).then_inc(act_chain, 1)
            act.wait_ge(act_chain, 1)
            act.activation(pv[:, HCOS], pv[:, HABS], ACT.Sin, bias=halfpi[:, 0:1], scale=-1.0)\
                .then_inc(trig_ready, 1)

            with act.Fori(1, NB) as i:
                project_u(i)
                evacuate_u(i, 0)
                evacuate_u(i, 1)
                row_stats(i + 1)
                evacuate_u(i, 2)
                evacuate_u(i, 3)

            def s5_matrices(q):
                for r in range(4):
                    act.wait_ge(et_ready, 4 * q + r + 1)
                    act.activation(e_sb[:, r // 2, 4 * (r % 2):4 * (r % 2) + 4, :],
                                   ps[:, 6, :].rearrange("p (g q) -> p g q", g=4), ACT.Copy).then_inc(e_evac, 1)
                act.wait_ge(l_half, q + 1)
                act.wait_ge(l_evac, START + q + 1)
                for f in range(2):
                    act.dma_start(t_d[q, :, f * CH:(f + 1) * CH], lf[:, f].rearrange("p g h -> p (g h)"))\
                        .then_inc(t_stored, 16)

            def store_lag0(q):
                act.wait_ge(t_stored, 48 * q + 32)
                act.dma_start(t_d[q, :, CH - 1], l0[:].rearrange("p g n -> p (g n)")).then_inc(t_stored, 16)

            s5_matrices(0)
            store_lag0(0)
            for m in range(CT):
                act.wait_ge(u_stored[m], START_DMA + 16 * NB)

            def beside_vg(i, last):
                act.wait_ge(y_ready, START + 4 * i)
                act.dma_start(u_sb[:], u_d[bass.ds(GQ * i, GQ)].rearrange("g h j c -> (h j) g c"))\
                    .then_inc(u_landed, 16)
                for u in range(RING):
                    split_hi(u, USE_VG + 2 * i)
                act.wait_ge(t_stored, 48 * (i + 1))
                for n in range(2):
                    act.wait_ge(z_stored[n], START_DMA + 32 * i)
                for j in range(CH):
                    act.dma_start(m_in[:, j], t_d[i, :, CH - 1 - j:2 * CH - 1 - j].rearrange("h j n -> h j n"))\
                        .then_inc(m_landed, 16)
                act.wait_ge(used[RING - 1], START + USE_VG + 2 * i)
                evacuate_hi(NB + i, g_mix)
                if not last:
                    load_rows(NB + i + 1, i + 1)
                act.wait_ge(fixed, START + i)
                for r in range(4):
                    for ri in range(2):
                        act.wait_ge(st_ready, 8 * i + 2 * r + ri + 1)
                        act.activation(s_sb[0:NP_, ri, 2 * r:2 * r + 2, :],
                                       ps[0:NP_, 6 + ri, :].rearrange("p (g c) -> p g c", g=2), ACT.Copy)\
                            .then_inc(st_fwd, 1)
                act.wait_ge(m_landed, 16 * CH * (i + 1))
                act.activation(m_sb[:].rearrange("p g (h j) -> p g h j", j=CH),
                               m_in[:].rearrange("p j (g h) -> p g h j", g=GQ), ACT.Copy).then_inc(m_laid, 1)

                def store_c(m):
                    act.wait_ge(c_done[m % 2], START + 2 * i + m // 2 + 1)
                    act.dma_start(c_d[m, :, bass.ds(TB * i + HALO, TB)], c_st[:, m % 2, :])\
                        .then_inc(c_stored[m % 2], 16)

                for m in range(CT):
                    gate = 2 * m + 1
                    act.wait_ge(used[gate % RING], START + USE_VG + 2 * i + gate // RING + 1)
                    act.wait_ge(c_done[m % 2], START + 2 * i + m // 2)
                    act.activation(sig_st[:, m % 2, :], ps[:, 2 * (m % 2) + 1, :], ACT.Sigmoid)\
                        .then_inc(sig_done, 1)
                    if m < 2:
                        for u in (2 * m, 2 * m + 1):
                            split_hi(u, USE_VG + 2 * i + 1)
                    if m:
                        store_c(m - 1)
                if not last:
                    row_stats(NB + i + 1)
                    s5_matrices(i + 1)
                store_c(CT - 1)
                if not last:
                    store_lag0(i + 1)
                for r in range(4):
                    act.wait_ge(y_ready, START + 4 * i + r + 1)
                    act.wait_ge(z_stored[r % 2], START_DMA + 16 * (2 * i + r // 2))
                    act.activation(z_st[:, r % 2], ps[:, 6 + r % 2, :].rearrange("p (g c) -> p g c", g=2),
                                   ACT.Gelu_apprx_tanh).then_inc(z_done, 1)
                    act.wait_ge(z_done, START + 4 * i + r + 1)
                    act.dma_start(z_d[bass.ds(GQ * i + 2 * r, 2)].rearrange("g h j c -> (h j) g c"),
                                  z_st[:, r % 2]).then_inc(z_stored[r % 2], 16)

            with act.Fori(0, NB - 1) as i:
                beside_vg(i, False)
            beside_vg(NB - 1, True)

            act.wait_ge(pads_out, 32)
            for n in range(2):
                act.wait_ge(c_stored[n], START_DMA + 16 * 2 * NB)
                act.wait_ge(z_stored[n], START_DMA + 16 * 2 * NB)
            act.wait_ge(fixed, START + NB)
            cin_src = lambda b: c_d[:, :, bass.ds(TB * b, CIN)].rearrange("c p t -> p c t")
            act.dma_start(cin[:, :, 0:CIN], cin_src(0)).then_inc(cin_landed, 16)
            act.dma_start(gp_mix[:], mix_norm_post[0].partition_broadcast(P)).then_inc(gp_in, 16)
            act.dma_start(gp_ffn[:], ffn_norm_post[0].partition_broadcast(P)).then_inc(gp_in, 16)
            with act.Fori(0, NB) as b:
                it = 2 * NB + b
                act.wait_ge(out_stored, START_DMA + 16 * NT * b)
                load_rows(it, b)

                def split_blk(u):
                    split_hi(u % RING, USE_BLK + PER_BLK * b + u // RING)

                for u in range(RING):
                    split_blk(u)
                act.wait_ge(used[RING - 1], START + USE_BLK + PER_BLK * b)
                for k in range(CT):
                    act.dma_start(z_sb[:, k, :].rearrange("p (j c) -> p j c", j=CH),
                                  z_d[k * GQ:(k + 1) * GQ, :, :, bass.ds(CB * b, CB)]
                                  .rearrange("g h j c -> (g h) j c")).then_inc(z_landed, 16)
                act.wait_ge(z_landed, 16 * CT * (b + 1))
                for k in range(CT):
                    act.activation(t_hi[:, CT + k, :], z_sb[:, k, :], ACT.Copy).then_inc(zhi_done, 1)
                for k in range(CT):
                    act.wait_ge(dev_done, CT * b + k + 1)
                    act.activation(sq[:, k, :], cv[:, k, :], ACT.Square).then_inc(sq_done, 1)
                for k in range(CT):
                    act.wait_ge(used[k // 2], START + USE_BLK + PER_BLK * b + 1)
                    act.activation(sg[:, k, :], ps[:, k, :], ACT.Sigmoid, bias=glu_b[:, k:k + 1])\
                        .then_inc(gate_done, 1)
                    if k % 2:
                        split_blk(RING + k // 2)
                act.wait_ge(var_ready, b + 1)
                act.activation(ln_std[:], ps[:, 5, :], ACT.Sqrt, bias=epsc[:, 0:1]).then_inc(lstd_ready, 1)
                for k in range(CT):
                    act.wait_ge(norm_done, CT * b + k + 1)
                    act.activation(cn[:, k, :], cv[:, k, :], ACT.Silu, scale=ln_g[:, k:k + 1],
                                   bias=ln_b[:, k:k + 1]).then_inc(silu_done, 1)

                def tile_stats(which, ready, rows):
                    for tt in range(NT):
                        ready(tt)
                        act.wait_ge(squares, START + SQ0 + 12 * b + 4 * which + tt)
                        act.activation(junk[:], rows(tt), ACT.Square,
                                       accum_out=ssq[:, which, tt:tt + 1]).then_inc(squares, 1)
                    act.wait_ge(squares, START + SQ0 + 12 * b + 4 * which + 4)
                    act.activation(std[:, which, :], ssq[:, which, :], ACT.Sqrt, bias=epsc[:, 0:1],
                                   scale=1.0 / D).then_inc(std_ready, 1)

                act.wait_ge(conv_done, b + 1)
                act.dma_start(cin[:, :, 0:CIN], cin_src((b + 1) % NB)).then_inc(cin_landed, 16)
                bank2 = lambda tt: ps[:, 2 * tt:2 * tt + 2, :].rearrange("p a n -> p (a n)")
                for u in range(RING + 2, GLU_UNITS + KD + 2):
                    split_blk(u)

                def tile_done(tile_ready, last_unit, tt):
                    if tt < NT - 1:
                        act.wait_ge(tile_ready, (NT - 1) * b + tt + 1)
                    else:
                        act.wait_ge(used[last_unit % RING], START + USE_BLK + PER_BLK * b + last_unit // RING + 1)

                tile_stats(0, lambda tt: tile_done(mixed_ready, GLU_UNITS + KD - 1, tt), bank2)
                tile_stats(1, lambda tt: act.wait_ge(rows_added, START + 2 * NT * b + tt + 1), lambda tt: xb[:, tt, :])
                evacuate_hi(it, g_ffn)
                for u in range(GLU_UNITS + KD + 2, GLU_UNITS + KD + 4):
                    split_blk(u)
                with act.Fori(0, FT // 2) as t:
                    for v in range(2):
                        up = GLU_UNITS + KD + 2 * v + 1
                        act.wait_ge(used[up % RING], START + USE_BLK + PER_BLK * b + up // RING + t + 1)
                        act.wait_ge(hid_done[v], START + FT // 2 * b + t)
                        act.activation(act_t[:, v, :], ps[:, 2 * v, :], ACT.Silu).then_inc(silu_h, 1)
                        for u in (up + 3, up + 4):
                            split_hi(u % RING, USE_BLK + PER_BLK * b + u // RING + t)
                for u in range(GLU_UNITS + KD + 2 * FT + 4, UNITS_BLK):
                    split_blk(u)
                tile_stats(2, lambda tt: tile_done(down_tile, UNITS_BLK - 1, tt), bank2)
                for tt in range(NT):
                    act.wait_ge(rows_added, START + 2 * NT * b + NT + tt + 1)
                    act.dma_start(W_OUT_X[:, b, tt, :], xb[:, tt, :]).then_inc(out_stored, 16)
            act.wait_ge(out_stored, START_DMA + 16 * NT * NB)

        @block.vector
        def _(v):
            for s in (lo_done, l_evac, fixed, *c_done, *hid_done, rows_added):
                v.sem_inc(s, START)
            made = [0]

            def link(ins):
                made[0] += 1
                ins.then_inc(dve, 1)
                v.wait_ge(dve, made[0])

            def tt(o, a, b, op):
                link(v.tensor_tensor(o, a, b, op))

            def ts(o, a, s1, s2=None, op0=ALU.mult, op1=None):
                if op1 is None:
                    link(v.tensor_scalar(o, a, s1, None, op0))
                else:
                    link(v.tensor_scalar(o, a, s1, s2, op0, op1))

            def stt(o, a, s1, b, op0, op1):
                link(v.scalar_tensor_tensor(out=o, in0=a, scalar=s1, in1=b, op0=op0, op1=op1))

            def cmul(out_re, out_im, ar, ai, br, bi, shape, o=0):
                n = math.prod(shape[1:])
                pat = {2: "p (a) -> p a", 3: "p (a b) -> p a b", 4: "p (a b c) -> p a b c"}[len(shape)]
                sizes = dict(zip("abc", shape[1:]))
                t1 = g1[:, 0:n].rearrange(pat, **sizes)
                t2 = g2[:, 0:n].rearrange(pat, **sizes)
                tt(t1, ar, br, ALU.mult)
                tt(t2, ai, bi, ALU.mult)
                tt(out_re, t1, t2, ALU.subtract)
                tt(t1, ar, bi, ALU.mult)
                tt(t2, ai, br, ALU.mult)
                tt(out_im, t1, t2, ALU.add)

            v.wait_ge(consts_in, 16 * N_CONSTS)
            link(v.tensor_copy(prm[:, 2], ldt_raw[:].unsqueeze(2).broadcast_to([G, 2, NP_])))
            v.nop().then_inc(prm_in, 1)
            def expm1(out, out_pow, t):
                ts(t, t, 88.0, -87.0, ALU.min, ALU.max)
                kk, r, pol = pv[:, 20], pv[:, 21], pv[:, 22]
                ts(kk, t, 1.0 / math.log(2.0), MAGIC, ALU.mult, ALU.add)
                ts(kk, kk, MAGIC, None, ALU.subtract)
                stt(r, kk, -0.693359375, t, ALU.mult, ALU.add)
                stt(r, kk, 2.12194440e-4, r, ALU.mult, ALU.add)
                ts(pol, r, 1.0 / 5040)
                for c in (1.0 / 720, 1.0 / 120, 1.0 / 24, 1.0 / 6, 0.5, 1.0):
                    stt(pol, pol, c, r, ALU.add, ALU.mult)
                ts(pvi[:], kk, 127.0, None, ALU.add)
                link(v.tensor_scalar(pvi[:], pvi[:], 23, None, ALU.logical_shift_left))
                link(v.tensor_copy(out_pow, pvi[:].bitcast(F32)))
                tt(pol, pol, out_pow, ALU.mult)
                stt(out, out_pow, -1.0, pol, ALU.add, ALU.add)

            dt_, xr, th, em, pow2, kk, hs, c1, sn, ar1, ai, den, qr, qi, t1, ar = (pv[:, n] for n in
                (0, 1, 2, 3, 4, 5, HSIN, 9, 10, 11, 12, 13, 14, 15, 16, 17))
            lr, li, ldt = lam[:, 0], lam[:, 1], lam[:, 2]
            def scale_rows(it, k):
                v.wait_ge(std_ready, k)
                v.reciprocal(rstd[:, 0, :], std[:, 0, :]).then_inc(rstd_ready, 1)
                v.wait_ge(rstd_ready, k)
                for n in range(NT):
                    v.tensor_scalar(xb[:, n, :], xb[:, n, :], rstd[:, 0, n:n + 1], None, ALU.mult)\
                        .then_inc(rows_ready, 1)

            def evacuate_lo(it, gain):
                for k in range(KD):
                    v.wait_ge(hi_done, KD * it + k + 1)
                    v.scalar_tensor_tensor(out=t_lo[:, k, :], in0=ps[:, 4 + k % 2, :], scalar=gain[:, k:k + 1],
                                           in1=t_hi[:, k, :].bitcast(F32), op0=ALU.mult, op1=ALU.subtract)\
                        .then_inc(lo_done, 1)

            def discretise_1():
                expm1(em, pow2, ldt)
                ts(dt_, em, 1.0, None, ALU.add)
                tt(dt_, pv[:, 22], pow2, ALU.add)
                tt(xr, lr, dt_, ALU.mult)
                tt(th, li, dt_, ALU.mult)
                expm1(em, pow2, xr)
                ts(kk, th, 1.0 / (2 * math.pi), MAGIC, ALU.mult, ALU.add)
                ts(kk, kk, MAGIC, None, ALU.subtract)
                for part in (6.28125, 0.0019350051879882812, 3.019915981956752e-07):
                    stt(th, kk, -part, th, ALU.mult, ALU.add)
                ts(pv[:, HALF], th, 0.5)
                link(v.tensor_scalar(pv[:, HALF], pv[:, HALF], 1.5707964, -1.5707964, ALU.min, ALU.max))
                v.nop().then_inc(angle_ready, 1)
            def discretise_2():
                v.wait_ge(trig_ready, 2)
                stt(c1, hs, -2.0, hs, ALU.mult, ALU.mult)
                stt(sn, hs, 2.0, pv[:, HCOS], ALU.mult, ALU.mult)
                tt(ar1, em, c1, ALU.mult)
                tt(ar1, ar1, em, ALU.add)
                tt(ar1, ar1, c1, ALU.add)
                stt(ai, em, 1.0, sn, ALU.add, ALU.mult)
                ts(ar, ar1, 1.0, None, ALU.add)
                tt(den, lr, lr, ALU.mult)
                tt(t1, li, li, ALU.mult)
                tt(den, den, t1, ALU.add)
                link(v.reciprocal(den, den))
                tt(qr, ar1, lr, ALU.mult)
                tt(t1, ai, li, ALU.mult)
                tt(qr, qr, t1, ALU.add)
                tt(qr, qr, den, ALU.mult)
                tt(qi, ai, lr, ALU.mult)
                tt(t1, ar1, li, ALU.mult)
                tt(qi, qi, t1, ALU.subtract)
                tt(qi, qi, den, ALU.mult)
                over_h = lambda a: a.unsqueeze(2).broadcast_to([P, G, H])
                cmul(bb[:, 0], bb[:, 1], over_h(qr), over_h(qi), b_in[:, 0], b_in[:, 1], [P, G, H])
            def discretise_3():
                link(v.memset(pw[:, 0, 0], 1.0))
                link(v.memset(pw[:, 1, 0], 0.0))
                link(v.tensor_copy(pw[:, 0, 1], ar))
                link(v.tensor_copy(pw[:, 1, 1], ai))
                n = 1
                while n < CH:
                    last = lambda ri: pw[:, ri, n:n + 1].broadcast_to([P, n, G])
                    cmul(pw[:, 0, n + 1:2 * n + 1], pw[:, 1, n + 1:2 * n + 1], pw[:, 0, 1:n + 1],
                         pw[:, 1, 1:n + 1], last(0), last(1), [P, n, G])
                    n *= 2
                for ri in range(2):
                    link(v.tensor_copy(pe[0:NP_, ri], pw[0:NP_, ri, CH - 1::-1]))
                    link(v.tensor_copy(pe[NP_:P, ri], pw[NP_:P, ri, 1:CH + 1]))
                    link(v.tensor_copy(pf[0:NP_, ri], pw[0:NP_, ri, 1:CH + 1]))
                    link(v.tensor_copy(pf[NP_:P, ri], pw[NP_:P, ri, CH - 1::-1]))
                q_re, q_im = qr_t, qi_t[:, :, 1]
                link(v.tensor_copy(q_re[:, 0], pw[:, 0, CH]))
                link(v.tensor_copy(q_im[:, 0], pw[:, 1, CH]))
                n = 1
                while n < SUP:
                    last = lambda a: a[:, n - 1:n].broadcast_to([P, n, G])
                    cmul(q_re[:, n:2 * n], q_im[:, n:2 * n], q_re[:, 0:n], q_im[:, 0:n], last(q_re), last(q_im),
                         [P, n, G])
                    n *= 2
                for n in range(SUP, SUP + 3):
                    cmul(q_re[:, n], q_im[:, n], q_re[:, n - 1], q_im[:, n - 1], q_re[:, n - 1], q_im[:, n - 1],
                         [P, G])
                ts(qi_t[:, :, 0], q_im, -1.0)
                tt(dd[:], dd[:], ident[0:H, 0:H].unsqueeze(1).broadcast_to([H, G, H]), ALU.mult)
                v.sem_inc(disc_ready, 1)

            def small_matrices(q, step):
                qg = bass.ds(GQ * q, GQ)
                for half, d in ((slice(0, NP_), 0), (slice(NP_, P), 1)):
                    step(v.tensor_copy(ccq[half, 0, :, d], cc[half, 0, qg]))
                    step(v.tensor_copy(ccq[half, 1, :, d], cc[half, 2, qg]))
                step(v.tensor_copy(bbq[:], bb[:, :, qg, :]))
                v.sem_inc(cq_ready, 1)

            def add_d(q):
                v.wait_ge(l_ready, START + q + 1)
                if not isinstance(q, int):
                    v.wait_ge(t_stored, 48 * q)
                v.tensor_copy(lf[:], ps[:, 7, 0:2 * GQ * H].rearrange("p (g f h) -> p f g h", g=GQ, f=2))\
                    .then_inc(l_half, 1)
                v.tensor_tensor(l0[:], ps[0:H, 7, 2 * GQ * H:3 * GQ * H].rearrange("p (g h) -> p g h", g=GQ),
                                dd[:, bass.ds(GQ * q, GQ), :], ALU.add).then_inc(l_evac, 1)

            link(v.memset(ccq[:], 0.0))
            scale_rows(0, 1)
            v.wait_ge(pool_consts, 3)
            v.wait_ge(prm_t, 1)
            link(v.tensor_copy(lam[:], ps[:, 0, 0:3 * G].rearrange("p (a g) -> p a g", a=3)))
            for ri in range(2):
                link(v.tensor_copy(cc[:, ri], ps[:, 1 + ri, :].rearrange("p (g h) -> p g h", g=G)))
            link(v.tensor_copy(conv_w[:], ps[:, 3, 0:CT * TAPS].rearrange("p (c k) -> p c k", c=CT)))
            ts(cc[:, 2], cc[:, 1], -1.0)
            pieces = (discretise_1, discretise_2, discretise_3, lambda: small_matrices(0, link))
            for i in range(NB):
                evacuate_lo(i, g_mix)
                pieces[i]()
                scale_rows(i + 1, i + 2)
            v.wait_ge(gg_ready, 1)
            v.wait_ge(pads_out, 32)
            v.wait_ge(prm_t, 1)
            add_d(0)
            for edge in (slice(0, 2), slice(NC, NC + 2)):
                link(v.memset(x_sb[:, :, :, edge], 0.0))

            before2 = made[0]
            STEPS2 = 4 * (SUP - 1) + 1 + 16 + 4 + 4 * 5 + 5

            def beside_vg(i, last):
                count = [0]

                def step(ins, wait=True):
                    count[0] += 1
                    ins.then_inc(dve, 1)
                    if wait:
                        v.wait_ge(dve, before2 + STEPS2 * i + count[0])

                evacuate_lo(NB + i, g_mix)
                qg = bass.ds(GQ * i, GQ)
                for r in range(4):
                    for ri in range(2):
                        v.wait_ge(st_ready, 8 * i + 2 * r + ri + 1)
                        v.tensor_copy(s_sb[NP_:P, ri, 2 * r:2 * r + 2, ::-1],
                                      ps[NP_:P, 6 + ri, :].rearrange("p (g c) -> p g c", g=2))\
                            .then_inc(st_bwd, 1)
                v.wait_ge(st_fwd, 8 * i + 8)
                v.wait_ge(st_bwd, 8 * i + 8)
                sv = s_sb[:].rearrange("p r g (d e) -> p r g d e", e=SUP)

                def local(e):
                    prev = sv[:, :, :, :, e - 1]
                    shape = [P, 2, GQ, ND]
                    step(v.tensor_tensor(sc1[:], prev, qr_t[:, 0:1, qg].unsqueeze(3).broadcast_to(shape), ALU.mult),
                         False)
                    step(v.tensor_tensor(sc2[:], prev[:, ::-1],
                                         qi_t[:, 0, :, qg].unsqueeze(3).broadcast_to(shape), ALU.mult))
                    step(v.tensor_tensor(sc1[:], sc1[:], sc2[:], ALU.add))
                    step(v.tensor_tensor(sv[:, :, :, :, e], sv[:, :, :, :, e], sc1[:], ALU.add))

                def super_scan():
                    step(v.tensor_copy(bnd[:], sv[:, :, :, :, SUP - 1]))
                    for lev in range(4):
                        sh = 1 << lev
                        w = ND - sh
                        shape = [P, 2, GQ, w]
                        prev = bnd[:, :, :, 0:w]
                        pr = qr_t[:, SUP - 1 + lev:SUP + lev, qg].unsqueeze(3).broadcast_to(shape)
                        pi = qi_t[:, SUP - 1 + lev, :, qg].unsqueeze(3).broadcast_to(shape)
                        step(v.tensor_tensor(sc1[:, :, :, 0:w], prev, pr, ALU.mult), False)
                        step(v.tensor_tensor(sc2[:, :, :, 0:w], prev[:, ::-1], pi, ALU.mult))
                        step(v.tensor_tensor(sc1[:, :, :, 0:w], sc1[:, :, :, 0:w], sc2[:, :, :, 0:w], ALU.add))
                        step(v.tensor_tensor(bnd[:, :, :, sh:], bnd[:, :, :, sh:], sc1[:, :, :, 0:w], ALU.add))

                def fix_up():
                    v.wait_ge(y_ready, START + 4 * i)
                    for ri in range(2):
                        step(v.tensor_copy(x_sb[0:NP_, ri, :, 2:2 + SUP], s_sb[0:NP_, ri, :, 0:SUP]), False)
                        step(v.tensor_copy(x_sb[NP_:P, ri, :, NC - 1:NC - 1 - SUP:-1], s_sb[NP_:P, ri, :, 0:SUP]),
                             False)
                    for g0 in (0, 4):
                        shape = [P, 4, SUP, ND - 1]
                        qs = bass.ds(GQ * i + g0, 4)
                        for ri in range(2):
                            over = lambda t: t.rearrange("p e g -> p g e").unsqueeze(3).broadcast_to(shape)
                            b_ = lambda r: bnd[:, r, g0:g0 + 4, 0:ND - 1].unsqueeze(2).broadcast_to(shape)
                            step(v.tensor_tensor(fx1[:], b_(ri), over(qr_t[:, 0:SUP, qs]), ALU.mult), False)
                            step(v.tensor_tensor(fx2[:], b_(1 - ri), over(qi_t[:, 0:SUP, ri, qs]), ALU.mult))
                            step(v.tensor_tensor(fx1[:], fx1[:], fx2[:], ALU.add))
                            view = lambda t: t.rearrange("p g (d e) -> p g e d", e=SUP)
                            step(v.tensor_tensor(view(x_sb[0:NP_, ri, g0:g0 + 4, 2 + SUP:2 + NC]),
                                                 view(s_sb[0:NP_, ri, g0:g0 + 4, SUP:NC]), fx1[0:NP_], ALU.add),
                                 False)
                            step(v.tensor_tensor(view(x_sb[NP_:P, ri, g0:g0 + 4, NC - 1 - SUP::-1]),
                                                 view(s_sb[NP_:P, ri, g0:g0 + 4, SUP:NC]), fx1[NP_:P], ALU.add))
                    v.nop().then_inc(fixed, 1)

                pieces = (lambda: [local(e) for e in range(1, 6)], lambda: [local(e) for e in range(6, 11)],
                          lambda: [*(local(e) for e in range(11, SUP)), super_scan()], fix_up)
                for m in range(CT):
                    pieces[m]()
                    v.wait_ge(sig_done, CT * i + m + 1)
                    v.wait_ge(c_stored[m % 2], START_DMA + 16 * (2 * i + m // 2))
                    v.tensor_tensor(c_st[:, m % 2, :], ps[:, 2 * (m % 2), :], sig_st[:, m % 2, :], ALU.mult)\
                        .then_inc(c_done[m % 2], 1)
                    if m == 0 and not last:
                        v.wait_ge(l_ready, START + i + 1)
                        small_matrices(i + 1, step)
                assert count[0] == STEPS2 - (5 if last else 0), count[0]
                if not last:
                    scale_rows(NB + i + 1, NB + i + 2)
                    add_d(i + 1)

            with v.Fori(0, NB - 1) as i:
                beside_vg(i, False)
            beside_vg(NB - 1, True)

            def conv_start():
                for c in range(CT):
                    v.tensor_scalar(cv[:, c, :], cin[:, c, 0:TB], conv_w[:, c, 0:1], conv_b[:, c:c + 1],
                                    ALU.mult, ALU.add).then_inc(conv_chain[c], 1)

            def conv_tap(k, n):
                for c in range(CT):
                    v.wait_ge(conv_chain[c], n)
                    v.scalar_tensor_tensor(out=cv[:, c, :], in0=cin[:, c, bass.ds(k, TB)],
                                           scalar=conv_w[:, c, bass.ds(k, 1)], in1=cv[:, c, :],
                                           op0=ALU.mult, op1=ALU.add).then_inc(conv_chain[c], 1)

            v.wait_ge(cin_landed, 16)
            for n in range(2):
                v.wait_ge(c_stored[n], START_DMA + 16 * 2 * NB)
            v.wait_ge(y_ready, START + 4 * NB)
            conv_start()
            with v.Fori(1, TAPS) as k:
                conv_tap(k, k)
            for c in range(CT):
                v.wait_ge(conv_chain[c], TAPS)
            v.nop().then_inc(conv_done, 1)
            v.wait_ge(gp_in, 32)
            with v.Fori(0, NB) as b:
                it = 2 * NB + b
                for k in range(CT):
                    v.wait_ge(zhi_done, CT * b + k + 1)
                    v.tensor_tensor(t_lo[:, CT + k, :], z_sb[:, k, :], t_hi[:, CT + k, :].bitcast(F32),
                                    ALU.subtract).then_inc(zlo_done, 1)
                v.wait_ge(mean_ready, b + 1)
                for k in range(CT):
                    v.tensor_tensor(cv[:, k, :], cv[:, k, :], ps[:, 4, :], ALU.subtract).then_inc(dev_done, 1)
                v.wait_ge(lstd_ready, b + 1)
                v.reciprocal(ln_rstd[:], ln_std[:]).then_inc(ln_chain, 1)
                v.wait_ge(ln_chain, b + 1)
                v.wait_ge(sq_done, CT * b + CT)
                for k in range(CT):
                    v.tensor_tensor(cv[:, k, :], cv[:, k, :], ln_rstd[:], ALU.mult).then_inc(norm_done, 1)
                for k in range(CT):
                    v.wait_ge(silu_done, CT * b + k + 1)
                    v.tensor_copy(t_hi[:, k, :], cn[:, k, :]).then_inc(chi_done, 1)
                for k in range(CT):
                    v.wait_ge(chi_done, CT * b + k + 1)
                    v.tensor_tensor(t_lo[:, k, :], cn[:, k, :], t_hi[:, k, :].bitcast(F32), ALU.subtract)\
                        .then_inc(c_split, 1)
                natural = lambda t: t.rearrange("p (c j) -> p j c", j=CH)
                steps = lambda t: t.rearrange("p (j c) -> p j c", j=CH)
                for k in range(CT):
                    v.wait_ge(gate_done, CT * b + k + 1)
                    v.tensor_tensor(sg[:, k, :], sg[:, k, :], z_sb[:, k, :], ALU.mult).then_inc(s_done, 1)
                v.wait_ge(used[1], START + USE_BLK + PER_BLK * b + 1)
                for k in range(CT):
                    v.wait_ge(s_done, CT * b + k + 1)
                    v.tensor_copy(natural(t_hi[:, CT + k, :]), steps(sg[:, k, :])).then_inc(shi_done, 1)
                for k in range(CT):
                    v.wait_ge(shi_done, CT * b + k + 1)
                    v.tensor_tensor(natural(t_lo[:, CT + k, :]), steps(sg[:, k, :]),
                                    natural(t_hi[:, CT + k, :].bitcast(F32)), ALU.subtract)\
                        .then_inc(s_split, 1)
                bank2 = lambda n: ps[:, 2 * n:2 * n + 2, :].rearrange("p a n -> p (a n)")

                def residual(which, gain):
                    v.wait_ge(std_ready, 2 * NB + 3 * b + which + 1)
                    v.reciprocal(rstd[:, which, :], std[:, which, :]).then_inc(rstd_ready, 1)
                    v.wait_ge(rstd_ready, 2 * NB + 3 * b + which + 1)
                    for n in range(NT):
                        v.wait_ge(rows_added, START + 2 * NT * b + NT * (which // 2) + n)
                        v.scalar_tensor_tensor(out=tmp[:], in0=bank2(n), scalar=rstd[:, which, n:n + 1],
                                               in1=gain[:], op0=ALU.mult, op1=ALU.mult).then_inc(tmp_made, 1)
                        v.wait_ge(tmp_made, 2 * NT * b + NT * (which // 2) + n + 1)
                        if which == 0:
                            v.wait_ge(x_landed[n], 16 * (it + 1))
                        v.tensor_tensor(xb[:, n, :], xb[:, n, :], tmp[:], ALU.add)\
                            .then_inc(rows_added, 1)

                residual(0, gp_mix)
                v.wait_ge(std_ready, 2 * NB + 3 * b + 2)
                v.reciprocal(rstd[:, 1, :], std[:, 1, :]).then_inc(rstd_ready, 1)
                v.wait_ge(rstd_ready, 2 * NB + 3 * b + 2)
                for n in range(NT):
                    v.tensor_scalar(xn[:, n, :], xb[:, n, :], rstd[:, 1, n:n + 1], None, ALU.mult)\
                        .then_inc(rows_ready, 1)
                evacuate_lo(it, g_ffn)

                def hidden(m, w, n):
                    v.wait_ge(silu_h, FT * b + m + 1)
                    v.tensor_tensor(act_t[:, w, :], act_t[:, w, :], ps[:, 2 * w + 1, :], ALU.mult)\
                        .then_inc(hid_made[w], 1)
                    v.wait_ge(hid_made[w], n + 1)
                    v.tensor_copy(hid_hi[:, bass.ds(m, 1), :].rearrange("p a n -> p (a n)"), act_t[:, w, :])\
                        .then_inc(hid_hi_done[w], 1)
                    v.wait_ge(hid_hi_done[w], n + 1)
                    v.tensor_tensor(hid_lo[:, bass.ds(m, 1), :].rearrange("p a n -> p (a n)"), act_t[:, w, :],
                                    hid_hi[:, bass.ds(m, 1), :].bitcast(F32).rearrange("p a n -> p (a n)"),
                                    ALU.subtract).then_inc(hid_done[w], 1)

                v.wait_ge(cin_landed, 16 * (b + 2))
                v.wait_ge(silu_done, CT * b + CT)
                conv_start()
                with v.Fori(0, (TAPS - 1) // 3) as t:
                    for w in range(2):
                        hidden(2 * t + w, w, FT // 2 * b + t)
                        for k in ((1, 2), (3,))[w]:
                            conv_tap(3 * t + k, TAPS * (b + 1) + 3 * t + k)
                for w in range(2):
                    hidden(FT - 2 + w, w, FT // 2 * b + FT // 2 - 1)
                for c in range(CT):
                    v.wait_ge(conv_chain[c], TAPS * (b + 2))
                v.nop().then_inc(conv_done, 1)
                residual(2, gp_ffn)

        @block.tensor
        def _(pe_):
            for s in (*used, l_ready, y_ready):
                pe_.sem_inc(s, START)
            def split_product(o, slot_w, act_hi, act_lo, weights_first, start, stop):
                whi, wlo = slot_w
                if weights_first:
                    parts = ((whi, act_hi), (whi, act_lo), (wlo, act_hi))
                else:
                    parts = ((act_hi, whi), (act_hi, wlo), (act_lo, whi))
                for n, (l, r) in enumerate(parts):
                    last = pe_.matmul(o, l, r, start=start and n == 0, stop=stop and n == 2)
                return last

            pe_.wait_ge(ident_ready, 1)
            pe_.wait_ge(prm_in, 1)
            for n in range(3):
                pe_.transpose(ps[:, 0, n * G:(n + 1) * G], prm[:, n].rearrange("g d p -> g (d p)"),
                              ident[0:G, 0:G])
            for ri in range(2):
                for o in range(4):
                    pe_.transpose(ps[:, 1 + ri, o * P:(o + 1) * P],
                                  c_raw[:, ri, o].rearrange("q d p -> q (d p)"), ident[:])
            for c in range(CT):
                last = pe_.transpose(ps[:, 3, c * TAPS:(c + 1) * TAPS], cw_raw[:, c * P:(c + 1) * P],
                                     ident[0:TAPS, 0:TAPS])
            last.then_inc(prm_t, 1)

            def transpose_rows(it, rows):
                pe_.wait_ge(rows_ready, NT * (it + 1))
                for k in range(KD):
                    if k < 2:
                        pe_.wait_ge(lo_done, START + KD * it)
                    else:
                        pe_.wait_ge(lo_done, START + KD * it + k - 1)
                    for n in range(NT):
                        last = pe_.transpose(ps[:, 4 + k % 2, n * P:(n + 1) * P], rows[:, n, k * P:(k + 1) * P],
                                             ident[:])
                    last.then_inc(tp_ready, 1)

            def project(slot, n, bank, it, first):
                pe_.wait_ge(split_done[slot], START + n + 1)
                wh = w_hi[:, slot, :].rearrange("p (k m) -> p k m", k=KD)
                wl = w_lo[:, slot, :].rearrange("p (k m) -> p k m", k=KD)
                for k in range(KD):
                    if first:
                        pe_.wait_ge(lo_done, START + KD * it + k + 1)
                    last = split_product(ps[:, bank, :], (wh[:, k], wl[:, k]), t_hi[:, k, :], t_lo[:, k, :], True,
                                         k == 0, k == KD - 1)
                return last.then_inc(used[slot], 1)

            with pe_.Fori(0, NB) as i:
                transpose_rows(i, xb)
                for m in range(CT):
                    pe_.wait_ge(u_evac[m], START + i)
                    project(m, i, m, i, m == 0)

            def s5_matrices(q):
                pe_.wait_ge(gg_ready, q + 1)
                for r in range(4):
                    pe_.wait_ge(e_evac, START + 4 * q + r)
                    for n in range(4):
                        last = pe_.transpose(ps[:, 6, n * P:(n + 1) * P],
                                             gg[:, r // 2, 4 * (r % 2) + n].rearrange("p h j -> p (h j)"), ident[:])
                    last.then_inc(et_ready, 1)
                pe_.wait_ge(l_evac, START + q)
                if not isinstance(q, int):
                    pe_.wait_ge(l_half, q)
                pe_.wait_ge(cq_ready, q + 1)
                flat = lambda t: t.rearrange("p a b -> p (a b)")
                for g in range(GQ):
                    at = 2 * H * g
                    for ri in range(2):
                        pe_.matmul(ps[:, 7, at:at + 2 * H], flat(gg[:, ri, g]), flat(ccq[:, ri, g]), start=ri == 0,
                                   stop=ri == 1)
                    at = 2 * H * GQ + H * g
                    for ri in range(2):
                        last = pe_.matmul(ps[0:H, 7, at:at + H], bbq[:, ri, g],
                                          cc[:, 2 * ri, bass.ds(GQ * q + g, 1)].rearrange("p a h -> p (a h)"),
                                          start=ri == 0, stop=ri == 1)
                last.then_inc(l_ready, 1)

            s5_matrices(0)

            def beside_vg(i, last_one):
                transpose_rows(NB + i, xb)
                pe_.wait_ge(u_landed, 16 * (i + 1))
                for r in range(4):
                    for ri in range(2):
                        if r == 0:
                            pe_.wait_ge(z_done, START + 4 * i)
                            pe_.wait_ge(e_evac, START + 4 * i + 4)
                            pe_.wait_ge(l_half, i + 1)
                            pe_.wait_ge(l_evac, START + i + 1)
                        else:
                            pe_.wait_ge(st_fwd, 8 * i + 2 * (r - 1) + ri + 1)
                            pe_.wait_ge(st_bwd, 8 * i + 2 * (r - 1) + ri + 1)
                        for n in range(2):
                            last = pe_.matmul(ps[:, 6 + ri, n * NC:(n + 1) * NC], e_sb[:, ri, 2 * r + n],
                                              u_sb[:, 2 * r + n], start=True, stop=True)
                        last.then_inc(st_ready, 1)
                for m in range(CT):
                    if m < 2:
                        pe_.wait_ge(c_done[m % 2], START + 2 * i)
                    else:
                        pe_.wait_ge(c_done[m % 2], START + 2 * i + 1)
                    for w in range(2):
                        u = 2 * m + w
                        project(u % RING, USE_VG + 2 * i + u // RING, 2 * (m % 2) + w, NB + i, u == 0)
                if not last_one:
                    pe_.wait_ge(st_fwd, 8 * i + 8)
                    pe_.wait_ge(st_bwd, 8 * i + 8)
                    s5_matrices(i + 1)
                pe_.wait_ge(m_laid, i + 1)
                pe_.wait_ge(f_ready, i + 1)
                pe_.wait_ge(fixed, START + i + 1)
                for r in range(4):
                    if r < 2:
                        if last_one:
                            pe_.wait_ge(st_fwd, 8 * i + 8)
                            pe_.wait_ge(st_bwd, 8 * i + 8)
                        else:
                            pe_.wait_ge(e_evac, START + 4 * i + 8)
                            pe_.wait_ge(l_half, i + 2)
                            pe_.wait_ge(l_evac, START + i + 2)
                    else:
                        pe_.wait_ge(z_done, START + 4 * i + r - 1)
                    for n in range(2):
                        g = 2 * r + n
                        o = ps[:, 6 + r % 2, n * NC:(n + 1) * NC]
                        pe_.matmul(o, m_sb[:, g], u_sb[:, g], start=True, stop=False)
                        for ri in range(2):
                            last = pe_.matmul(o, f_sb[:, ri, g].rearrange("p h j -> p (h j)"), x_sb[:, ri, g, 1:NC + 1], start=False, stop=ri == 1)
                    last.then_inc(y_ready, 1)

            with pe_.Fori(0, NB - 1) as i:
                beside_vg(i, False)
            beside_vg(NB - 1, True)
            for m in range(2):
                pe_.wait_ge(c_done[m], START + 2 * NB)
            pe_.wait_ge(z_done, START + 4 * NB)
            pe_.wait_ge(pool_consts, 3)
            with pe_.Fori(0, NB) as b:
                it = 2 * NB + b
                use = USE_BLK + PER_BLK * b
                pe_.wait_ge(rows_added, START + 2 * NT * b)
                for u in range(GLU_UNITS):
                    pe_.wait_ge(split_done[u], START + use + 1)
                    wh = w_hi[:, u, :].rearrange("p (k m) -> p k m", k=CT)
                    wl = w_lo[:, u, :].rearrange("p (k m) -> p k m", k=CT)
                    for mm in range(2):
                        m = 2 * u + mm
                        cols = slice(mm * P, (mm + 1) * P)
                        for k in range(CT):
                            if m == 0:
                                pe_.wait_ge(zlo_done, CT * b + k + 1)
                            last = split_product(ps[:, m, :], (wh[:, k, cols], wl[:, k, cols]), t_hi[:, CT + k, :],
                                                 t_lo[:, CT + k, :], True, k == 0, k == CT - 1)
                    last.then_inc(used[u], 1)
                pe_.wait_ge(conv_done, b + 1)
                for k in range(CT):
                    last = pe_.matmul(ps[:, 4, :], mean_w[:], cv[:, k, :], start=k == 0, stop=k == CT - 1)
                last.then_inc(mean_ready, 1)
                for k in range(CT):
                    pe_.wait_ge(sq_done, CT * b + k + 1)
                    last = pe_.matmul(ps[:, 5, :], mean_w[:], sq[:, k, :], start=k == 0, stop=k == CT - 1)
                last.then_inc(var_ready, 1)

                def rows_product(units, at, act_of, ready, done):
                    total = sum(len(x_) for x_ in units)
                    n0 = 0
                    for group in units:
                        for tt_ in range(NT):
                            for j, k in enumerate(group):
                                u = at + k
                                slot = u % RING
                                if tt_ == 0:
                                    pe_.wait_ge(split_done[slot], START + use + u // RING + 1)
                                    ready(k)
                                toks = slice(tt_ * P, (tt_ + 1) * P)
                                hi_, lo_ = act_of(k)
                                for a in range(2):
                                    cols = slice(a * TB, (a + 1) * TB)
                                    last = split_product(ps[:, 2 * tt_ + a, :],
                                                         (w_hi[:, slot, cols], w_lo[:, slot, cols]),
                                                         hi_[:, toks], lo_[:, toks], False, n0 + j == 0,
                                                         n0 + j == total - 1)
                                if tt_ == NT - 1:
                                    last.then_inc(used[slot], 1)
                            if group is units[-1] and tt_ < NT - 1:
                                last.then_inc(done, 1)
                        n0 += len(group)

                def mixed_in(k):
                    if k < CT:
                        pe_.wait_ge(c_split, CT * b + k + 1)
                    else:
                        pe_.wait_ge(s_split, CT * b + k - CT + 1)
                    if k == 0:
                        pe_.wait_ge(gate_done, CT * b + CT)
                        pe_.wait_ge(lstd_ready, b + 1)

                rows_product([[k] for k in range(KD - 2)] + [[KD - 2, KD - 1]], GLU_UNITS,
                             lambda k: (t_hi[:, k, :], t_lo[:, k, :]), mixed_in, mixed_ready)
                pe_.wait_ge(rows_added, START + 2 * NT * b + NT)
                transpose_rows(it, xn)
                at = GLU_UNITS + KD
                with pe_.Fori(0, FT // 2) as t:
                    pe_.wait_ge(lo_done, START + KD * (it + 1))
                    for w in range(2):
                        pe_.wait_ge(hid_done[w], START + FT // 2 * b + t)
                        for a in range(2):
                            u = at + 2 * w + a
                            project(u % RING, use + u // RING + t, 2 * w + a, it, False)
                at += 2 * FT
                for w in range(2):
                    pe_.wait_ge(hid_done[w], START + FT // 2 * (b + 1))
                rows_product([[k] for k in range(FT - 2)] + [[FT - 2, FT - 1]], at,
                             lambda k: (hid_hi[:, k, :], hid_lo[:, k, :]), lambda k: None, down_tile)


_INS = ["x", "mix_norm_pre", "mix_norm_post", "w_in", "conv_dw_w", "conv_dw_b", "conv_ln_g", "conv_ln_b",
        "ssm_a_re", "ssm_a_im", "ssm_log_dt", "ssm_b_re", "ssm_b_im", "ssm_c_re", "ssm_c_im", "ssm_d",
        "ssm_glu_w", "ssm_glu_b", "w_out", "ffn_norm_pre", "ffn_norm_post", "ffn_w_gate", "ffn_w_up",
        "ffn_w_down"]


def kernel(**inputs):
    import numpy as _np
    import concourse.bacc as _bacc
    from concourse import mybir as _mybir
    from concourse.bass_utils import run_bass_kernel_spmd as _run

    nc = _bacc.Bacc("TRN2", target_bir_lowering=False, num_devices=1, dynamic_dma_scratch_size=1024)
    arrays, args = {}, []
    for name in _INS:
        a = _np.ascontiguousarray(inputs[name])
        arrays[f"in_{name}_dram"] = a
        args.append(nc.dram_tensor(f"in_{name}_dram", a.shape, _mybir.dt.from_np(a.dtype), kind="ExternalInput").ap())
    shape = inputs["x"].shape
    args.append(nc.dram_tensor("out_dram", shape, _mybir.dt.float32, kind="ExternalOutput").ap())
    hybrid_encoder(nc, *args)
    r = _run(nc, [arrays], core_ids=[0])
    return r.results[0]["out_dram"]
```

```python
import math
from contextlib import ExitStack

import concourse.bass as bass
from concourse import mybir

F32 = mybir.dt.float32
F32R = mybir.dt.float32r
I32 = mybir.dt.int32
ALU = mybir.AluOpType
ACT = mybir.ActivationFunctionType

P = 128
TB = 512
EPS = 1e-6
N_CONSTS = 19
HALF, HSIN, HABS, HCOS = 6, 7, 8, 18
START, START_DMA = 1, 16
SQ0 = 32
RING = 4
CH = 8
SUP = 16
GQ = 8
MAGIC = 12582912.0


def hybrid_encoder(nc, x, mix_norm_pre, mix_norm_post, w_in, conv_dw_w, conv_dw_b, conv_ln_g,
                   conv_ln_b, ssm_a_re, ssm_a_im, ssm_log_dt, ssm_b_re, ssm_b_im, ssm_c_re,
                   ssm_c_im, ssm_d, ssm_glu_w, ssm_glu_b, w_out, ffn_norm_pre, ffn_norm_post,
                   ffn_w_gate, ffn_w_up, ffn_w_down, out):
    _, T, D = x.shape
    KD = D // P
    NB = T // TB
    NT = TB // P
    CW = conv_dw_w.shape[2]
    CT = CW // P
    TAPS = conv_dw_w.shape[1]
    HALO = TAPS // 2
    CPAD = T + 2 * HALO
    CIN = TB + 2 * HALO
    _, _, G, NP_, H = ssm_b_re.shape
    NC = T // CH
    ND = NC // SUP
    CB = TB // CH
    FT = ffn_w_gate.shape[2] // P
    assert CH * H == P and 2 * NP_ == P and G == 4 * GQ and NB == 4 and KD == 8

    UNITS_U, UNITS_VG = CT, 2 * CT
    GLU_UNITS = 2
    USE_VG = NB * UNITS_U // RING
    USE_BLK = USE_VG + NB * UNITS_VG // RING
    UNITS_BLK = GLU_UNITS + KD + 2 * FT + FT
    PER_BLK = UNITS_BLK // RING
    WOUT_AT, FFN_AT = GLU_UNITS, GLU_UNITS + KD
    WOUT_ROWS = (*range(CT, KD), *range(CT))
    GLU_AT = FFN_AT + 2 * FT
    PE_TAPS = 10
    DVE_TAPS = TAPS - PE_TAPS
    CONV_BANKS = (2, 3, 6, 7)
    CONV_TURNS, MEAN_AT, DEV_AT, SQ_AT = 6, 7, 8, 9
    CONV_TAPS = (TAPS - 1) // CONV_TURNS
    assert UNITS_BLK % RING == 0 and UNITS_U == RING and CONV_TAPS * CONV_TURNS == TAPS - 1

    def scratch(name, shape):
        return nc.dram_tensor(name, shape, F32, kind="Internal").ap()

    u_d = scratch("u_scratch", [G, H, CH, NC])
    z_d = scratch("z_scratch", [G, H, CH, NC])
    c_d = scratch("c_scratch", [CT, P, CPAD])
    t_d = scratch("t_scratch", [NB, H, 2 * CH, GQ * H])

    with ExitStack() as ctx:
        def sb(name, shape, dt=F32, scope=ctx):
            return scope.enter_context(nc.sbuf_tensor(name, shape, dt))

        def sem(name):
            return ctx.enter_context(nc.semaphore(name))

        def sems(name, n):
            return [sem(f"{name}{i}") for i in range(n)]

        ident = sb("ident", [P, P])
        mean_w = sb("mean_w", [P, P])
        xb = sb("xb", [P, NT, D])
        raw = sb("raw", [P, RING, D])
        w_hi = sb("w_hi", [P, RING, D], F32R)
        w_lo = sb("w_lo", [P, RING, D], F32R)
        t_hi = sb("t_hi", [P, KD, TB], F32R)
        t_lo = sb("t_lo", [P, KD, TB], F32R)
        g_mix = sb("g_mix", [P, KD])
        g_ffn = sb("g_ffn", [P, KD])
        ln_g = sb("ln_g", [P, CT])
        ln_b = sb("ln_b", [P, CT])
        glu_b = sb("glu_b", [P, CT])
        conv_b = sb("conv_b", [P, CT])
        conv_w = sb("conv_w", [P, CT, TAPS])
        ssq = sb("ssq", [P, 3, NT])
        std = sb("std", [P, 3, NT])
        rstd = sb("rstd", [P, 3, NT])
        epsc = sb("epsc", [P, 1])
        halfpi = sb("halfpi", [P, 1])

        pscope = ExitStack()
        psb = lambda name, shape, dt=F32: sb(name, shape, dt, pscope)
        shared = psb("shared", [P, D])
        sig_st = psb("sig_st", [P, 2, TB])
        c_st = psb("c_st", [P, 2, TB])
        e_sb = psb("e_sb", [P, 2, GQ, P])
        gg = psb("gg", [P, 2, GQ, H, CH])
        bbq = psb("bbq", [P, 2, GQ, H])
        ccq = psb("ccq", [P, 2, GQ, 2, H])
        f_sb = psb("f_sb", [P, 2, GQ, H, CH])
        bb = psb("bb", [P, 2, G, H])
        cc = psb("cc", [P, 3, G, H])
        pe = psb("pe", [P, 2, CH, G])
        pf = psb("pf", [P, 2, CH, G])
        dd = psb("dd", [H, G, H])
        lf = psb("lf", [P, 2, GQ, H])
        l0 = psb("l0", [H, GQ, H])
        qr_t = psb("qr_t", [P, SUP + 3, G])
        qi_t = psb("qi_t", [P, SUP + 3, 2, G])
        pt = psb("pt", [P, GQ, H, CH])
        lscope = ExitStack()
        lsb = lambda name, shape, dt=F32: sb(name, shape, dt, lscope)
        u_sb = lsb("u_sb", [P, GQ, NC])
        m_sb = lsb("m_sb", [P, GQ, CH * H])
        s_sb = lsb("s_sb", [P, 2, GQ, NC])
        x_sb = lsb("x_sb", [P, 2, GQ, NC + 2])
        bnd = lsb("bnd", [P, 2, GQ, ND])
        fx1 = lsb("fx1", [P, 4, SUP, ND - 1])
        fx2 = lsb("fx2", [P, 4, SUP, ND - 1])
        sc1, sc2 = (t[:].rearrange("p a b c -> p (a b c)")[:, 0:2 * GQ * ND]
                    .rearrange("p (a g d) -> p a g d", a=2, g=GQ) for t in (fx1, fx2))
        sq_junk = shared[:]
        m_in = shared[:].rearrange("p (j n) -> p j n", j=CH)
        z_st = shared[:].rearrange("p (a g c) -> p a g c", a=2, g=2)
        lscope.close()
        rscope = ExitStack()
        rsb = lambda name, shape, dt=F32: sb(name, shape, dt, rscope)
        u_st = rsb("u_st", [P, CT, TB])
        zeros = rsb("zeros", [P, CT, HALO])
        cw_raw = rsb("cw_raw", [TAPS, CW])
        prm = rsb("prm", [G, 3, 2, NP_])
        ldt_raw = rsb("ldt_raw", [G, 2])
        c_raw = rsb("c_raw", [P, 2, 4, 2, NP_])
        b_in = rsb("b_in", [P, 2, G, H])
        lam = rsb("lam", [P, 3, G])
        pv = rsb("pv", [P, 24, G])
        pvi = rsb("pvi", [P, G], I32)
        pw = rsb("pw", [P, 2, CH + 1, G])
        g1 = rsb("g1", [P, G * H])
        g2 = rsb("g2", [P, G * H])
        rscope.close()
        pscope.close()

        fscope = ExitStack()
        fsb = lambda name, shape, dt=F32: sb(name, shape, dt, fscope)
        act_t = fsb("act_t", [P, 2, TB])
        gp_mix = fsb("gp_mix", [P, D])
        gp_ffn = fsb("gp_ffn", [P, D])
        cin = fsb("cin", [P, CT, CIN + 2])
        cv = fsb("cv", [P, CT, TB])
        sg = fsb("sg", [P, CT, TB])
        hscope = ExitStack()
        hid_hi = sb("hid_hi", [P, FT, TB], F32R, hscope)
        hid_lo = sb("hid_lo", [P, FT, TB], F32R, hscope)
        hscope.close()
        mscope = ExitStack()
        msb = lambda name, shape, dt=F32: sb(name, shape, dt, mscope)
        z_first = msb("z_first", [P, CT, TB])
        xn = msb("xn", [P, NT, D])
        diag = msb("diag", [P, PE_TAPS, CT, P])
        mscope.close()
        fscope.close()
        sg_rows = sg[:].rearrange("p (r k) n -> p r (k n)", r=2)
        junk, tmp = sg_rows[:, 0], sg_rows[:, 1]
        ln_std, ln_rstd = act_t[:, 0], act_t[:, 1]
        z_next = cin[:, :, 0:TB]

        ps = ctx.enter_context(nc.psum_tensor("ps", [P, 8, TB], F32))

        raw_landed = sems("raw_landed", RING)
        whi_done = sems("whi_done", RING)
        split_done = sems("split_done", RING)
        used = sems("used", RING)
        consts_in = sem("consts_in")
        s5_in = sem("s5_in")
        gp_in = sem("gp_in")
        pads_out = sem("pads_out")
        ident_zero = sem("ident_zero")
        ident_ready = sem("ident_ready")
        pool_consts = sem("pool_consts")
        zeros_ready = sem("zeros_ready")
        x_landed = sems("x_landed", NT)
        squares = sem("squares")
        std_ready = sem("std_ready")
        rstd_ready = sem("rstd_ready")
        rows_ready = sem("rows_ready")
        tp_ready = sem("tp_ready")
        hi_done = sem("hi_done")
        lo_done = sem("lo_done")
        u_evac = sems("u_evac", CT)
        u_stored = sems("u_stored", CT)
        dve = sem("dve_chain")
        act_chain = sem("act_chain")
        prm_t = sem("prm_t")
        prm_in = sem("prm_in")
        angle_ready = sem("angle_ready")
        trig_ready = sem("trig_ready")
        et_ready = sem("et_ready")
        e_evac = sem("e_evac")
        l_ready = sem("l_ready")
        l_evac = sem("l_evac")
        l_half = sem("l_half")
        disc_ready = sem("disc_ready")
        pool_p = sem("pool_products")
        pool_pause = sem("pool_pause")
        gg_ready = sem("gg_ready")
        f_ready = sem("f_ready")
        cq_ready = sem("cq_ready")
        t_stored = sem("t_stored")
        m_landed = sem("m_landed")
        u_landed = sem("u_landed")
        m_laid = sem("m_laid")
        st_ready = sem("st_ready")
        st_fwd = sem("st_fwd")
        st_bwd = sem("st_bwd")
        fixed = sem("fixed")
        sig_done = sem("sig_done")
        c_done = sems("c_done", 2)
        c_stored = sems("c_stored", 2)
        y_ready = sem("y_ready")
        z_done = sem("z_done")
        z_stored = sems("z_stored", 2)
        cin_landed = sem("cin_landed")
        conv_done = sem("conv_done")
        z_landed = sem("z_landed")
        zhi_done = sem("zhi_done")
        zlo_done = sem("zlo_done")
        gate_done = sem("gate_done")
        s_split = sem("s_split")
        mean_ready = sem("mean_ready")
        dev_done = sem("dev_done")
        sq_done = sem("sq_done")
        var_ready = sem("var_ready")
        lstd_ready = sem("lstd_ready")
        norm_done = sem("norm_done")
        silu_done = sem("silu_done")
        c_split = sem("c_split")
        mixed_ready = sem("mixed_ready")
        silu_h = sem("silu_h")
        hid_done = sems("hid_done", 2)
        out_stored = sem("out_stored")
        conv_chain = sems("conv_chain", CT)
        ln_chain = sem("ln_chain")
        chi_done = sem("chi_done")
        shi_done = sem("shi_done")
        s_done = sem("s_done")
        tmp_made = sem("tmp_made")
        diag_ready = sem("diag_ready")
        conv_pe = sem("conv_pe")
        mix_std = sem("mix_std")
        x1_std = sem("x1_std")
        ffn_std = sem("ffn_std")
        rows_added = sem("rows_added")
        hid_made = sems("hid_made", 2)
        hid_hi_done = sems("hid_hi_done", 2)
        down_tile = sem("down_tile")

        block = ctx.enter_context(nc.Block())


        @block.sync
        def _(sp):
            def load(slot, n, src):
                sp.wait_ge(split_done[slot], START + n)
                sp.dma_start(raw[:, slot, :].rearrange("p (k m) -> p k m", k=src.shape[1]), src)\
                    .then_inc(raw_landed[slot], 16)

            w_in_v = w_in[0].rearrange("(k p) n -> p k n", p=P)
            with sp.Fori(0, NB) as i:
                for m in range(CT):
                    load(m, i, w_in_v[:, :, 2 * CW + m * P:2 * CW + (m + 1) * P])
            with sp.Fori(0, NB) as i:
                for m in range(CT):
                    for v in range(2):
                        u = 2 * m + v
                        load(u % RING, USE_VG + 2 * i + u // RING,
                             w_in_v[:, :, v * CW + m * P:v * CW + (m + 1) * P])
            glu_v = ssm_glu_w[0].rearrange("(k p) n -> p k n", p=P)
            w_out_v = w_out[0].rearrange("(k p) (a n) -> p k a n", p=P, a=1)
            gate_v = ffn_w_gate[0].rearrange("(k p) n -> p k n", p=P)
            up_v = ffn_w_up[0].rearrange("(k p) n -> p k n", p=P)
            down_v = ffn_w_down[0].rearrange("(k p) (a n) -> p k a n", p=P, a=1)
            def load_glu(use, at):
                for u in range(GLU_UNITS):
                    load((at + u) % RING, use + (at + u) // RING, glu_v[:, :, u * 2 * P:(u + 1) * 2 * P])

            def block_units(b, last):
                use = USE_BLK + PER_BLK * b
                for k in range(KD):
                    u = WOUT_AT + k
                    load(u % RING, use + u // RING, w_out_v[:, WOUT_ROWS[k]])
                with sp.Fori(0, FT // 2) as t:
                    for v in range(4):
                        src = (gate_v, up_v)[v % 2]
                        load((FFN_AT + v) % RING, use + (FFN_AT + v) // RING + t,
                             src[:, :, bass.ds((2 * t + v // 2) * P, P)])
                at = GLU_AT
                if not last:
                    load_glu(use, at)
                    at += GLU_UNITS
                for k in range(FT):
                    load((at + k) % RING, use + (at + k) // RING, down_v[:, k])

            load_glu(USE_BLK, 0)
            with sp.Fori(0, NB - 1) as b:
                block_units(b, False)
            block_units(NB - 1, True)

        @block.gpsimd
        def _(pool):
            for s in (*split_done, pool_p):
                pool.sem_inc(s, START)
            pool.memset(ident[:], 0.0).then_inc(ident_zero, 1)
            pool.wait_ge(ident_zero, 1)
            pool.affine_select(out=ident[:], in_=ident[:], compare_op=ALU.not_equal, fill=1.0, base=0,
                               pattern=[[-1, P]], channel_multiplier=1).then_inc(ident_ready, 1)
            pool.memset(zeros[:], 0.0).then_inc(zeros_ready, 1)
            pool.memset(mean_w[:], 1.0 / CW).then_inc(pool_consts, 1)
            pool.memset(epsc[:], EPS).then_inc(pool_consts, 1)
            pool.memset(halfpi[:], math.pi / 2).then_inc(pool_consts, 1)

            def split_lo(slot, n):
                pool.wait_ge(whi_done[slot], n + 1)
                pool.tensor_tensor(w_lo[:, slot, :], raw[:, slot, :], w_hi[:, slot, :].bitcast(F32),
                                   ALU.subtract).then_inc(split_done[slot], 1)

            shape = [P, GQ, H, CH]

            def product(part, q, out, powers, coeffs, im, made):
                pa = lambda ri: powers[:, ri, :, q].rearrange("p j g -> p g j").unsqueeze(2).broadcast_to(shape)
                co = lambda c: coeffs[:, c, q, :].unsqueeze(3).broadcast_to(shape)
                ri, k = divmod(part, 3)
                if k == 0:
                    pool.wait_ge(pool_p, START + made)
                    pool.nop().then_inc(pool_pause, 1)
                    pool.tensor_tensor(out[:, ri], pa(0), co((0, im)[ri]), ALU.mult).then_inc(pool_p, 1)
                elif k == 1:
                    pool.wait_ge(pool_p, START + made)
                    pool.nop().then_inc(pool_pause, 1)
                    pool.tensor_tensor(pt[:], pa(1), co((1, 0)[ri]), ALU.mult).then_inc(pool_p, 1)
                else:
                    pool.wait_ge(pool_p, START + made)
                    pool.nop().then_inc(pool_pause, 1)
                    pool.tensor_tensor(out[:, ri], out[:, ri], pt[:], (ALU.subtract, ALU.add)[ri] if im == 1
                                       else ALU.subtract).then_inc(pool_p, 1)

            quarter = lambda q: bass.ds(GQ * q, GQ)

            def gg_part(part, q, made):
                product(part, quarter(q), gg, pe, bb, 1, made + part)
                if part == 5:
                    pool.wait_ge(pool_p, START + made + 6)
                    pool.sem_inc(gg_ready, 1)

            def f_part(part, q, last):
                if part == 0:
                    pool.wait_ge(y_ready, START + 4 * q)
                made = 12 * q + (6 if last else 12)
                product(part, quarter(q), f_sb, pf, cc, 2, made + part)
                if part == 5:
                    pool.wait_ge(pool_p, START + made + 6)
                    pool.sem_inc(f_ready, 1)

            with pool.Fori(0, NB) as n:
                for slot in range(RING):
                    split_lo(slot, n)
            pool.wait_ge(disc_ready, 1)
            for part in range(6):
                gg_part(part, 0, 0)

            def beside_vg(i, last):
                for u in range(2 * RING):
                    split_lo(u % RING, USE_VG + 2 * i + u // RING)
                    if u < 3 and not last:
                        if u == 0:
                            pool.wait_ge(l_ready, START + i + 1)
                        gg_part(2 * u, i + 1, 12 * i + 6)
                        gg_part(2 * u + 1, i + 1, 12 * i + 6)
                    elif 3 <= u < 6:
                        f_part(2 * u - 6, i, last)
                        f_part(2 * u - 5, i, last)

            with pool.Fori(0, NB - 1) as i:
                beside_vg(i, False)
            beside_vg(NB - 1, True)
            with pool.Fori(USE_BLK, USE_BLK + NB * PER_BLK) as n:
                for slot in range(RING):
                    split_lo(slot, n)

        W_IN_X = x[0].rearrange("(b t p) d -> p b t d", t=NT, p=P)
        W_OUT_X = out[0].rearrange("(b t p) d -> p b t d", t=NT, p=P)

        @block.scalar
        def _(act):
            for s in (*u_evac, e_evac, squares, z_done):
                act.sem_inc(s, START)
            for s in (*u_stored, *c_stored, *z_stored, out_stored):
                act.sem_inc(s, START_DMA)
            loads = [(prm[:, 0], ssm_a_re[0].rearrange("d g p -> g d p")),
                     (prm[:, 1], ssm_a_im[0].rearrange("d g p -> g d p")),
                     (ldt_raw[:], ssm_log_dt[0].rearrange("d g -> g d")),
                     (cw_raw[:], conv_dw_w[0])]
            for ri, c_in in enumerate((ssm_c_re, ssm_c_im)):
                for d in range(2):
                    loads.append((c_raw[:, ri, :, d, :],
                                  c_in[0, d].rearrange("(o g) h p -> (g h) o p", o=4)))
            for ri, b_x in enumerate((ssm_b_re, ssm_b_im)):
                for d in range(2):
                    loads.append((b_in[d * NP_:(d + 1) * NP_, ri], b_x[0, d].rearrange("g p h -> p g h")))
            for dst, src in ((g_mix, mix_norm_pre), (g_ffn, ffn_norm_pre), (ln_g, conv_ln_g),
                             (ln_b, conv_ln_b), (glu_b, ssm_glu_b), (conv_b, conv_dw_b)):
                loads.append((dst[:], src[0].rearrange("(k p) -> p k", p=P)))
            loads.append((dd[:].rearrange("p g h -> p (g h)"), ssm_d[0].partition_broadcast(H)))
            assert len(loads) == N_CONSTS
            for tt in range(NT):
                act.dma_start(xb[:, tt, :], W_IN_X[:, 0, tt, :]).then_inc(x_landed[tt], 16)
            for dst, src in loads:
                act.dma_start(dst, src, allow_slow_non_contiguous=True).then_inc(consts_in, 16)
            act.wait_ge(zeros_ready, 1)
            for at in (0, HALO + T):
                act.dma_start(c_d[:, :, at:at + HALO].rearrange("c p t -> p c t"), zeros[:])\
                    .then_inc(pads_out, 16)

            def split_hi(slot, n):
                act.wait_ge(raw_landed[slot], 16 * (n + 1))
                act.wait_ge(used[slot], START + n)
                act.activation(w_hi[:, slot, :], raw[:, slot, :], ACT.Copy).then_inc(whi_done[slot], 1)

            def row_stats(it):
                for tt in range(NT):
                    act.wait_ge(x_landed[tt], 16 * it + 16)
                    if tt:
                        act.wait_ge(squares, START + 4 * it + tt)
                    else:
                        act.wait_ge(squares, START + 4 * it)
                    act.activation(sq_junk[:], xb[:, tt, :], ACT.Square, accum_out=ssq[:, 0, tt:tt + 1])\
                        .then_inc(squares, 1)
                act.wait_ge(squares, START + 4 * it + 4)
                act.activation(std[:, 0, :], ssq[:, 0, :], ACT.Sqrt, bias=epsc[:, 0:1], scale=1.0 / D)\
                    .then_inc(std_ready, 1)

            def evacuate_hi(it, gain, banks=2):
                for k in range(KD):
                    act.wait_ge(tp_ready, KD * it + k + 1)
                    act.activation(t_hi[:, k, :], ps[:, 4 + k % banks, :], ACT.Copy, scale=gain[:, k:k + 1])\
                        .then_inc(hi_done, 1)

            def load_rows(it, nxt):
                for tt in range(NT):
                    act.dma_start(xb[:, tt, :], W_IN_X[:, nxt, tt, :]).then_inc(x_landed[tt], 16)

            act.wait_ge(pool_consts, 3)
            row_stats(0)
            def project_u(i):
                act.wait_ge(used[RING - 1], START + i)
                evacuate_hi(i, g_mix, 4)
                load_rows(i + 1, (i + 1) % NB)

            def evacuate_u(i, m):
                act.wait_ge(used[m], START + i + 1)
                act.wait_ge(u_stored[m], START_DMA + 16 * i)
                act.activation(u_st[:, m, :].rearrange("p (j c) -> p j c", j=CH),
                               ps[:, m, :].rearrange("p (c j) -> p j c", j=CH), ACT.Copy).then_inc(u_evac[m], 1)
                act.wait_ge(u_evac[m], START + i + 1)
                act.dma_start(
                    u_d[m * GQ:(m + 1) * GQ, :, :, bass.ds(CB * i, CB)].rearrange("g h j c -> (g h) j c"),
                    u_st[:, m, :].rearrange("p (j c) -> p j c", j=CH)).then_inc(u_stored[m], 16)
                split_hi(m, i + 1)

            act.wait_ge(consts_in, 16 * N_CONSTS)
            for u in range(RING):
                split_hi(u, 0)
            project_u(0)
            evacuate_u(0, 0)
            evacuate_u(0, 1)
            row_stats(1)
            evacuate_u(0, 2)
            evacuate_u(0, 3)
            act.wait_ge(angle_ready, 1)
            act.activation(pv[:, HSIN], pv[:, HALF], ACT.Sin).then_inc(trig_ready, 1)
            act.activation(pv[:, HABS], pv[:, HALF], ACT.Abs).then_inc(act_chain, 1)
            act.wait_ge(act_chain, 1)
            act.activation(pv[:, HCOS], pv[:, HABS], ACT.Sin, bias=halfpi[:, 0:1], scale=-1.0)\
                .then_inc(trig_ready, 1)

            with act.Fori(1, NB) as i:
                project_u(i)
                evacuate_u(i, 0)
                evacuate_u(i, 1)
                row_stats(i + 1)
                evacuate_u(i, 2)
                evacuate_u(i, 3)

            def evacuate_e(q):
                for r in range(4):
                    act.wait_ge(et_ready, 4 * q + r + 1)
                    act.activation(e_sb[:, r // 2, 4 * (r % 2):4 * (r % 2) + 4, :],
                                   ps[:, 6, :].rearrange("p (g q) -> p g q", g=4), ACT.Copy).then_inc(e_evac, 1)

            def store_responses(q):
                act.wait_ge(l_half, q + 1)
                act.wait_ge(l_evac, START + q + 1)
                for f in range(2):
                    act.dma_start(t_d[q, :, f * CH:(f + 1) * CH], lf[:, f].rearrange("p g h -> p (g h)"))\
                        .then_inc(t_stored, 16)

            def store_lag0(q):
                act.wait_ge(t_stored, 48 * q + 32)
                act.dma_start(t_d[q, :, CH - 1], l0[:].rearrange("p g n -> p (g n)")).then_inc(t_stored, 16)

            evacuate_e(0)

            cin_src = lambda b: c_d[:, :, bass.ds(TB * b, CIN)].rearrange("c p t -> p c t")

            def load_u(i):
                act.dma_start(u_sb[:], u_d[bass.ds(GQ * i, GQ)].rearrange("g h j c -> (h j) g c"))\
                    .then_inc(u_landed, 16)

            for m in range(CT):
                act.wait_ge(u_stored[m], START_DMA + 16 * NB)
            load_u(0)
            store_responses(0)
            store_lag0(0)

            def beside_vg(i, last):
                act.wait_ge(fixed, START + i)
                for r in range(4):
                    for ri in range(2):
                        act.wait_ge(st_ready, 8 * i + 2 * r + ri + 1)
                        act.activation(s_sb[0:NP_, ri, 2 * r:2 * r + 2, :],
                                       ps[0:NP_, 6 + ri, :].rearrange("p (g c) -> p g c", g=2), ACT.Copy)\
                            .then_inc(st_fwd, 1)
                evacuate_hi(NB + i, g_mix)
                load_rows(NB + i + 1, (i + 1) % NB)
                if last:
                    act.wait_ge(pads_out, 32)
                    act.wait_ge(l_half, NB)
                    for n in range(2):
                        act.wait_ge(c_stored[n], START_DMA + 16 * 4)
                    act.dma_start(cin[:, :, 0:CIN], cin_src(0)).then_inc(cin_landed, 16)
                act.wait_ge(t_stored, 48 * (i + 1))
                for n in range(2):
                    act.wait_ge(z_stored[n], START_DMA + 32 * i)
                for j in range(CH):
                    act.dma_start(m_in[:, j], t_d[i, :, CH - 1 - j:2 * CH - 1 - j].rearrange("h j n -> h j n"))\
                        .then_inc(m_landed, 16)

                def store_c(m):
                    act.wait_ge(c_done[m % 2], START + 2 * i + m // 2 + 1)
                    act.dma_start(c_d[m, :, bass.ds(TB * i + HALO, TB)], c_st[:, m % 2, :])\
                        .then_inc(c_stored[m % 2], 16)

                for m in range(CT):
                    gate = 2 * m + 1
                    act.wait_ge(used[gate % RING], START + USE_VG + 2 * i + gate // RING + 1)
                    act.wait_ge(c_done[m % 2], START + 2 * i + m // 2)
                    act.activation(sig_st[:, m % 2, :], ps[:, 2 * (m % 2) + 1, :], ACT.Sigmoid)\
                        .then_inc(sig_done, 1)
                    if m == 1 and not last:
                        evacuate_e(i + 1)
                    for u in (2 * (m % 2), 2 * (m % 2) + 1):
                        split_hi(u, USE_VG + 2 * i + 1 + m // 2)
                    if m:
                        store_c(m - 1)
                    else:
                        act.wait_ge(m_landed, 16 * CH * (i + 1))
                        act.activation(m_sb[:].rearrange("p g (h j) -> p g h j", j=CH),
                                       m_in[:].rearrange("p j (g h) -> p g h j", g=GQ), ACT.Copy).then_inc(m_laid, 1)
                    if m == 1 and not last:
                        row_stats(NB + i + 1)
                    if m == 2 and not last:
                        store_responses(i + 1)
                if not last:
                    store_lag0(i + 1)
                for r in range(4):
                    act.wait_ge(y_ready, START + 4 * i + r + 1)
                    if r == 3 and not last:
                        load_u(i + 1)
                    act.wait_ge(z_stored[r % 2], START_DMA + 16 * (2 * i + r // 2))
                    act.activation(z_st[:, r % 2], ps[:, 6 + r % 2, :].rearrange("p (g c) -> p g c", g=2),
                                   ACT.Gelu_apprx_tanh).then_inc(z_done, 1)
                    act.wait_ge(z_done, START + 4 * i + r + 1)
                    act.dma_start(z_d[bass.ds(GQ * i + 2 * r, 2)].rearrange("g h j c -> (h j) g c"),
                                  z_st[:, r % 2]).then_inc(z_stored[r % 2], 16)
                store_c(CT - 1)

            with act.Fori(0, NB - 1) as i:
                beside_vg(i, False)
            beside_vg(NB - 1, True)

            act.wait_ge(fixed, START + NB)

            def diagonals(taps):
                for j in taps:
                    for c in range(CT):
                        act.activation(diag[:, j, c], ident[:], ACT.Copy,
                                       scale=conv_w[:, c, DVE_TAPS + j:DVE_TAPS + j + 1]).then_inc(diag_ready, 1)

            diagonals(range(0, PE_TAPS // 2))
            for n in range(2):
                act.wait_ge(c_stored[n], START_DMA + 16 * 2 * NB)
                act.wait_ge(z_stored[n], START_DMA + 16 * 2 * NB)
            def load_z(n, z):
                for k in range(CT):
                    act.dma_start(z[:, k, :].rearrange("p (j c) -> p j c", j=CH),
                                  z_d[k * GQ:(k + 1) * GQ, :, :, bass.ds(CB * n, CB)]
                                  .rearrange("g h j c -> (g h) j c")).then_inc(z_landed, 16)

            load_z(0, z_first)
            act.dma_start(gp_mix[:], mix_norm_post[0].partition_broadcast(P)).then_inc(gp_in, 16)
            act.dma_start(gp_ffn[:], ffn_norm_post[0].partition_broadcast(P)).then_inc(gp_in, 16)

            def unit_hi(b, u):
                split_hi(u % RING, USE_BLK + PER_BLK * b + u // RING)

            def leading_z(n, z):
                act.wait_ge(z_landed, 16 * CT * (n + 1))
                for k in range(CT):
                    act.activation(t_hi[:, CT + k, :], z[:, k, :], ACT.Copy).then_inc(zhi_done, 1)

            def square_deviations(n):
                for k in range(CT):
                    act.wait_ge(dev_done, CT * n + k + 1)
                    act.activation(sg[:, k, :], cv[:, k, :], ACT.Square).then_inc(sq_done, 1)

            def gates(b, n, at):
                for k in range(CT):
                    u = at + k // 2
                    act.wait_ge(used[u % RING], START + USE_BLK + PER_BLK * b + u // RING + 1)
                    act.activation(sg[:, k, :], ps[:, (0, 1, 4, 5)[k], :], ACT.Sigmoid, bias=glu_b[:, k:k + 1])\
                        .then_inc(gate_done, 1)
                    if k % 2:
                        unit_hi(b, u + RING)

            def deviation_std(n):
                act.wait_ge(var_ready, n + 1)
                act.activation(ln_std, ps[:, 7, :], ACT.Sqrt, bias=epsc[:, 0:1]).then_inc(lstd_ready, 1)

            def silu_conv(n):
                for k in range(CT):
                    act.wait_ge(norm_done, CT * n + k + 1)
                    act.activation(cv[:, k, :], cv[:, k, :], ACT.Silu, scale=ln_g[:, k:k + 1],
                                   bias=ln_b[:, k:k + 1]).then_inc(silu_done, 1)

            diagonals(range(PE_TAPS // 2, PE_TAPS))
            leading_z(0, z_first)
            gates(0, 0, 0)
            act.wait_ge(s_split, CT)
            square_deviations(0)
            deviation_std(0)
            silu_conv(0)
            bank2 = lambda tt: ps[:, 2 * tt:2 * tt + 2, :].rearrange("p a n -> p (a n)")

            def block_act(b, last):
                it = 2 * NB + b
                sq = [0]
                act.wait_ge(conv_done, b + 1)
                act.wait_ge(s_done, CT * (b + 1))
                if not last:
                    act.dma_start(cin[:, :, 0:CIN], cin_src(b + 1)).then_inc(cin_landed, 16)

                def tile_std(which, tt, rows, ready):
                    act.wait_ge(squares, START + SQ0 + 12 * b + sq[0])
                    act.activation(junk, rows, ACT.Square, accum_out=ssq[:, which, tt:tt + 1]).then_inc(squares, 1)
                    sq[0] += 1
                    act.wait_ge(squares, START + SQ0 + 12 * b + sq[0])
                    act.activation(std[:, which, tt:tt + 1], ssq[:, which, tt:tt + 1], ACT.Sqrt, bias=epsc[:, 0:1],
                                   scale=1.0 / D).then_inc(ready, 1)

                def product_std(which, tt, tile_ready, last_unit, ready):
                    if tt < NT - 1:
                        act.wait_ge(tile_ready, (NT - 1) * b + tt + 1)
                    else:
                        act.wait_ge(used[last_unit % RING], START + USE_BLK + PER_BLK * b + last_unit // RING + 1)
                    tile_std(which, tt, bank2(tt), ready)

                for u in range(WOUT_AT + RING, FFN_AT + 1):
                    unit_hi(b, u)
                for tt in range(NT + 1):
                    if tt < NT:
                        product_std(0, tt, mixed_ready, FFN_AT - 1, mix_std)
                    if tt == NT:
                        for u in (FFN_AT + 1, FFN_AT + 2):
                            unit_hi(b, u)
                    if tt:
                        act.wait_ge(rows_added, START + 2 * NT * b + tt)
                        tile_std(1, tt - 1, xb[:, tt - 1, :], x1_std)
                evacuate_hi(it, g_ffn, 4)
                unit_hi(b, FFN_AT + 3)

                def silu_pairs(t0, t1):
                    with act.Fori(t0, t1) as t:
                        for v in range(2):
                            up = FFN_AT + 2 * v + 1
                            act.wait_ge(used[up % RING], START + USE_BLK + PER_BLK * b + up // RING + t + 1)
                            act.wait_ge(hid_done[v], START + FT // 2 * b + t)
                            act.activation(act_t[:, v, :], ps[:, 2 * v, :], ACT.Silu).then_inc(silu_h, 1)
                            for u in (up + 3, up + 4):
                                split_hi(u % RING, USE_BLK + PER_BLK * b + u // RING + t)

                if last:
                    silu_pairs(0, FT // 2)
                    down_at = GLU_AT
                    first = down_at + 4
                else:
                    silu_pairs(0, MEAN_AT)
                    act.wait_ge(conv_done, b + 2)
                    load_z(b + 1, z_next)
                    silu_pairs(MEAN_AT, SQ_AT)
                    square_deviations(b + 1)
                    silu_pairs(SQ_AT, FT // 2)
                    leading_z(b + 1, z_next)
                    act.wait_ge(hid_done[0], START + FT // 2 * (b + 1))
                    deviation_std(b + 1)
                    gates(b, b + 1, GLU_AT)
                    silu_conv(b + 1)
                    down_at = GLU_AT + GLU_UNITS
                    first = down_at + 4
                for u in range(first, down_at + FT + (0 if last else 2)):
                    unit_hi(b, u)
                act.wait_ge(s_split, CT * (b + (1 if last else 2)))
                for tt in range(NT):
                    product_std(2, tt, down_tile, down_at + FT - 1, ffn_std)
                if not last:
                    for u in (2, 3):
                        unit_hi(b, down_at + FT + u)
                for tt in range(NT):
                    act.wait_ge(rows_added, START + 2 * NT * b + NT + tt + 1)
                    act.dma_start(W_OUT_X[:, b, tt, :], xb[:, tt, :]).then_inc(out_stored, 16)
                if not last:
                    act.wait_ge(out_stored, START_DMA + 16 * NT * (b + 1))
                    load_rows(it + 1, b + 1)

            with act.Fori(0, NB - 1) as b:
                block_act(b, False)
            block_act(NB - 1, True)
            act.wait_ge(out_stored, START_DMA + 16 * NT * NB)

        @block.vector
        def _(v):
            for s in (lo_done, l_evac, fixed, *c_done, *hid_done, rows_added):
                v.sem_inc(s, START)
            v.sem_inc(tmp_made, NT)
            made = [0]

            def link(ins):
                made[0] += 1
                ins.then_inc(dve, 1)
                v.wait_ge(dve, made[0])

            def tt(o, a, b, op):
                link(v.tensor_tensor(o, a, b, op))

            def ts(o, a, s1, s2=None, op0=ALU.mult, op1=None):
                if op1 is None:
                    link(v.tensor_scalar(o, a, s1, None, op0))
                else:
                    link(v.tensor_scalar(o, a, s1, s2, op0, op1))

            def stt(o, a, s1, b, op0, op1):
                link(v.scalar_tensor_tensor(out=o, in0=a, scalar=s1, in1=b, op0=op0, op1=op1))

            def cmul(out_re, out_im, ar, ai, br, bi, shape, o=0):
                n = math.prod(shape[1:])
                pat = {2: "p (a) -> p a", 3: "p (a b) -> p a b", 4: "p (a b c) -> p a b c"}[len(shape)]
                sizes = dict(zip("abc", shape[1:]))
                t1 = g1[:, 0:n].rearrange(pat, **sizes)
                t2 = g2[:, 0:n].rearrange(pat, **sizes)
                tt(t1, ar, br, ALU.mult)
                tt(t2, ai, bi, ALU.mult)
                tt(out_re, t1, t2, ALU.subtract)
                tt(t1, ar, bi, ALU.mult)
                tt(t2, ai, br, ALU.mult)
                tt(out_im, t1, t2, ALU.add)

            v.wait_ge(consts_in, 16 * N_CONSTS)
            link(v.tensor_copy(prm[:, 2], ldt_raw[:].unsqueeze(2).broadcast_to([G, 2, NP_])))
            v.nop().then_inc(prm_in, 1)
            def expm1(out, out_pow, t):
                ts(t, t, 88.0, -87.0, ALU.min, ALU.max)
                kk, r, pol = pv[:, 20], pv[:, 21], pv[:, 22]
                ts(kk, t, 1.0 / math.log(2.0), MAGIC, ALU.mult, ALU.add)
                ts(kk, kk, MAGIC, None, ALU.subtract)
                stt(r, kk, -0.693359375, t, ALU.mult, ALU.add)
                stt(r, kk, 2.12194440e-4, r, ALU.mult, ALU.add)
                ts(pol, r, 1.0 / 5040)
                for c in (1.0 / 720, 1.0 / 120, 1.0 / 24, 1.0 / 6, 0.5, 1.0):
                    stt(pol, pol, c, r, ALU.add, ALU.mult)
                ts(pvi[:], kk, 127.0, None, ALU.add)
                link(v.tensor_scalar(pvi[:], pvi[:], 23, None, ALU.logical_shift_left))
                link(v.tensor_copy(out_pow, pvi[:].bitcast(F32)))
                tt(pol, pol, out_pow, ALU.mult)
                stt(out, out_pow, -1.0, pol, ALU.add, ALU.add)

            dt_, xr, th, em, pow2, kk, hs, c1, sn, ar1, ai, den, qr, qi, t1, ar = (pv[:, n] for n in
                (0, 1, 2, 3, 4, 5, HSIN, 9, 10, 11, 12, 13, 14, 15, 16, 17))
            lr, li, ldt = lam[:, 0], lam[:, 1], lam[:, 2]
            def scale_rows(it, k):
                v.wait_ge(std_ready, k)
                v.reciprocal(rstd[:, 0, :], std[:, 0, :]).then_inc(rstd_ready, 1)
                v.wait_ge(rstd_ready, k)
                for n in range(NT):
                    v.tensor_scalar(xb[:, n, :], xb[:, n, :], rstd[:, 0, n:n + 1], None, ALU.mult)\
                        .then_inc(rows_ready, 1)

            def evacuate_lo(it, gain, banks=2):
                for k in range(KD):
                    v.wait_ge(hi_done, KD * it + k + 1)
                    v.scalar_tensor_tensor(out=t_lo[:, k, :], in0=ps[:, 4 + k % banks, :], scalar=gain[:, k:k + 1],
                                           in1=t_hi[:, k, :].bitcast(F32), op0=ALU.mult, op1=ALU.subtract)\
                        .then_inc(lo_done, 1)

            def discretise_1():
                expm1(em, pow2, ldt)
                ts(dt_, em, 1.0, None, ALU.add)
                tt(dt_, pv[:, 22], pow2, ALU.add)
                tt(xr, lr, dt_, ALU.mult)
                tt(th, li, dt_, ALU.mult)
                expm1(em, pow2, xr)
                ts(kk, th, 1.0 / (2 * math.pi), MAGIC, ALU.mult, ALU.add)
                ts(kk, kk, MAGIC, None, ALU.subtract)
                for part in (6.28125, 0.0019350051879882812, 3.019915981956752e-07):
                    stt(th, kk, -part, th, ALU.mult, ALU.add)
                ts(pv[:, HALF], th, 0.5)
                link(v.tensor_scalar(pv[:, HALF], pv[:, HALF], 1.5707964, -1.5707964, ALU.min, ALU.max))
                v.nop().then_inc(angle_ready, 1)
            def discretise_2():
                v.wait_ge(trig_ready, 2)
                stt(c1, hs, -2.0, hs, ALU.mult, ALU.mult)
                stt(sn, hs, 2.0, pv[:, HCOS], ALU.mult, ALU.mult)
                tt(ar1, em, c1, ALU.mult)
                tt(ar1, ar1, em, ALU.add)
                tt(ar1, ar1, c1, ALU.add)
                stt(ai, em, 1.0, sn, ALU.add, ALU.mult)
                ts(ar, ar1, 1.0, None, ALU.add)
                tt(den, lr, lr, ALU.mult)
                tt(t1, li, li, ALU.mult)
                tt(den, den, t1, ALU.add)
                link(v.reciprocal(den, den))
                tt(qr, ar1, lr, ALU.mult)
                tt(t1, ai, li, ALU.mult)
                tt(qr, qr, t1, ALU.add)
                tt(qr, qr, den, ALU.mult)
                tt(qi, ai, lr, ALU.mult)
                tt(t1, ar1, li, ALU.mult)
                tt(qi, qi, t1, ALU.subtract)
                tt(qi, qi, den, ALU.mult)
                over_h = lambda a: a.unsqueeze(2).broadcast_to([P, G, H])
                cmul(bb[:, 0], bb[:, 1], over_h(qr), over_h(qi), b_in[:, 0], b_in[:, 1], [P, G, H])
            def discretise_3():
                link(v.memset(pw[:, 0, 0], 1.0))
                link(v.memset(pw[:, 1, 0], 0.0))
                link(v.tensor_copy(pw[:, 0, 1], ar))
                link(v.tensor_copy(pw[:, 1, 1], ai))
                n = 1
                while n < CH:
                    last = lambda ri: pw[:, ri, n:n + 1].broadcast_to([P, n, G])
                    cmul(pw[:, 0, n + 1:2 * n + 1], pw[:, 1, n + 1:2 * n + 1], pw[:, 0, 1:n + 1],
                         pw[:, 1, 1:n + 1], last(0), last(1), [P, n, G])
                    n *= 2
                for ri in range(2):
                    link(v.tensor_copy(pe[0:NP_, ri], pw[0:NP_, ri, CH - 1::-1]))
                    link(v.tensor_copy(pe[NP_:P, ri], pw[NP_:P, ri, 1:CH + 1]))
                    link(v.tensor_copy(pf[0:NP_, ri], pw[0:NP_, ri, 1:CH + 1]))
                    link(v.tensor_copy(pf[NP_:P, ri], pw[NP_:P, ri, CH - 1::-1]))
                q_re, q_im = qr_t, qi_t[:, :, 1]
                link(v.tensor_copy(q_re[:, 0], pw[:, 0, CH]))
                link(v.tensor_copy(q_im[:, 0], pw[:, 1, CH]))
                n = 1
                while n < SUP:
                    last = lambda a: a[:, n - 1:n].broadcast_to([P, n, G])
                    cmul(q_re[:, n:2 * n], q_im[:, n:2 * n], q_re[:, 0:n], q_im[:, 0:n], last(q_re), last(q_im),
                         [P, n, G])
                    n *= 2
                for n in range(SUP, SUP + 3):
                    cmul(q_re[:, n], q_im[:, n], q_re[:, n - 1], q_im[:, n - 1], q_re[:, n - 1], q_im[:, n - 1],
                         [P, G])
                ts(qi_t[:, :, 0], q_im, -1.0)
                tt(dd[:], dd[:], ident[0:H, 0:H].unsqueeze(1).broadcast_to([H, G, H]), ALU.mult)
                v.sem_inc(disc_ready, 1)

            def small_matrices(q, step):
                qg = bass.ds(GQ * q, GQ)
                for half, d in ((slice(0, NP_), 0), (slice(NP_, P), 1)):
                    step(v.tensor_copy(ccq[half, 0, :, d], cc[half, 0, qg]))
                    step(v.tensor_copy(ccq[half, 1, :, d], cc[half, 2, qg]))
                step(v.tensor_copy(bbq[:], bb[:, :, qg, :]))
                v.sem_inc(cq_ready, 1)

            def add_d(q):
                v.wait_ge(l_ready, START + q + 1)
                if not isinstance(q, int):
                    v.wait_ge(t_stored, 48 * q)
                v.tensor_copy(lf[:], ps[:, 7, 0:2 * GQ * H].rearrange("p (g f h) -> p f g h", g=GQ, f=2))\
                    .then_inc(l_half, 1)
                v.tensor_tensor(l0[:], ps[0:H, 7, 2 * GQ * H:3 * GQ * H].rearrange("p (g h) -> p g h", g=GQ),
                                dd[:, bass.ds(GQ * q, GQ), :], ALU.add).then_inc(l_evac, 1)

            link(v.memset(ccq[:], 0.0))
            scale_rows(0, 1)
            v.wait_ge(pool_consts, 3)
            v.wait_ge(prm_t, 1)
            link(v.tensor_copy(lam[:], ps[:, 0, 0:3 * G].rearrange("p (a g) -> p a g", a=3)))
            for ri in range(2):
                link(v.tensor_copy(cc[:, ri], ps[:, 1 + ri, :].rearrange("p (g h) -> p g h", g=G)))
            link(v.tensor_copy(conv_w[:], ps[:, 3, 0:CT * TAPS].rearrange("p (c k) -> p c k", c=CT)))
            ts(cc[:, 2], cc[:, 1], -1.0)
            pieces = (discretise_1, discretise_2, discretise_3, lambda: small_matrices(0, link))
            for i in range(NB):
                evacuate_lo(i, g_mix, 4)
                pieces[i]()
                scale_rows(i + 1, i + 2)
            v.wait_ge(gg_ready, 1)
            v.wait_ge(pads_out, 32)
            v.wait_ge(prm_t, 1)
            add_d(0)
            for edge in (slice(0, 2), slice(NC, NC + 2)):
                link(v.memset(x_sb[:, :, :, edge], 0.0))

            before2 = made[0]
            STEPS2 = 4 * (SUP - 1) + 1 + 16 + 4 + 4 * 5 + 5

            def beside_vg(i, last):
                count = [0]

                def step(ins, wait=True):
                    count[0] += 1
                    ins.then_inc(dve, 1)
                    if wait:
                        v.wait_ge(dve, before2 + STEPS2 * i + count[0])

                qg = bass.ds(GQ * i, GQ)
                for r in range(4):
                    for ri in range(2):
                        v.wait_ge(st_ready, 8 * i + 2 * r + ri + 1)
                        v.tensor_copy(s_sb[NP_:P, ri, 2 * r:2 * r + 2, ::-1],
                                      ps[NP_:P, 6 + ri, :].rearrange("p (g c) -> p g c", g=2))\
                            .then_inc(st_bwd, 1)
                v.wait_ge(st_fwd, 8 * i + 8)
                v.wait_ge(st_bwd, 8 * i + 8)
                sv = s_sb[:].rearrange("p r g (d e) -> p r g d e", e=SUP)

                def local(e):
                    prev = sv[:, :, :, :, e - 1]
                    shape = [P, 2, GQ, ND]
                    step(v.tensor_tensor(sc1[:], prev, qr_t[:, 0:1, qg].unsqueeze(3).broadcast_to(shape), ALU.mult),
                         False)
                    step(v.tensor_tensor(sc2[:], prev[:, ::-1],
                                         qi_t[:, 0, :, qg].unsqueeze(3).broadcast_to(shape), ALU.mult))
                    step(v.tensor_tensor(sc1[:], sc1[:], sc2[:], ALU.add))
                    step(v.tensor_tensor(sv[:, :, :, :, e], sv[:, :, :, :, e], sc1[:], ALU.add))

                def super_scan():
                    step(v.tensor_copy(bnd[:], sv[:, :, :, :, SUP - 1]))
                    for lev in range(4):
                        sh = 1 << lev
                        w = ND - sh
                        shape = [P, 2, GQ, w]
                        prev = bnd[:, :, :, 0:w]
                        pr = qr_t[:, SUP - 1 + lev:SUP + lev, qg].unsqueeze(3).broadcast_to(shape)
                        pi = qi_t[:, SUP - 1 + lev, :, qg].unsqueeze(3).broadcast_to(shape)
                        step(v.tensor_tensor(sc1[:, :, :, 0:w], prev, pr, ALU.mult), False)
                        step(v.tensor_tensor(sc2[:, :, :, 0:w], prev[:, ::-1], pi, ALU.mult))
                        step(v.tensor_tensor(sc1[:, :, :, 0:w], sc1[:, :, :, 0:w], sc2[:, :, :, 0:w], ALU.add))
                        step(v.tensor_tensor(bnd[:, :, :, sh:], bnd[:, :, :, sh:], sc1[:, :, :, 0:w], ALU.add))

                def fix_up(half):
                    v.wait_ge(y_ready, START + 4 * i)
                    for ri in range(0 if half else 2):
                        step(v.tensor_copy(x_sb[0:NP_, ri, :, 2:2 + SUP], s_sb[0:NP_, ri, :, 0:SUP]), False)
                        step(v.tensor_copy(x_sb[NP_:P, ri, :, NC - 1:NC - 1 - SUP:-1], s_sb[NP_:P, ri, :, 0:SUP]),
                             False)
                    for g0 in (4 * half,):
                        shape = [P, 4, SUP, ND - 1]
                        qs = bass.ds(GQ * i + g0, 4)
                        for ri in range(2):
                            over = lambda t: t.rearrange("p e g -> p g e").unsqueeze(3).broadcast_to(shape)
                            b_ = lambda r: bnd[:, r, g0:g0 + 4, 0:ND - 1].unsqueeze(2).broadcast_to(shape)
                            step(v.tensor_tensor(fx1[:], b_(ri), over(qr_t[:, 0:SUP, qs]), ALU.mult), False)
                            step(v.tensor_tensor(fx2[:], b_(1 - ri), over(qi_t[:, 0:SUP, ri, qs]), ALU.mult))
                            step(v.tensor_tensor(fx1[:], fx1[:], fx2[:], ALU.add))
                            view = lambda t: t.rearrange("p g (d e) -> p g e d", e=SUP)
                            step(v.tensor_tensor(view(x_sb[0:NP_, ri, g0:g0 + 4, 2 + SUP:2 + NC]),
                                                 view(s_sb[0:NP_, ri, g0:g0 + 4, SUP:NC]), fx1[0:NP_], ALU.add),
                                 False)
                            step(v.tensor_tensor(view(x_sb[NP_:P, ri, g0:g0 + 4, NC - 1 - SUP::-1]),
                                                 view(s_sb[NP_:P, ri, g0:g0 + 4, SUP:NC]), fx1[NP_:P], ALU.add))
                    if half:
                        v.nop().then_inc(fixed, 1)

                pieces = (lambda: [local(1), local(2), evacuate_lo(NB + i, g_mix), *(local(e) for e in range(3, 9))],
                          lambda: [*(local(e) for e in range(9, SUP)), super_scan()],
                          lambda: fix_up(0), lambda: fix_up(1))
                for m in range(CT):
                    pieces[m]()
                    if m == 2 and not last:
                        add_d(i + 1)
                    v.wait_ge(sig_done, CT * i + m + 1)
                    v.wait_ge(c_stored[m % 2], START_DMA + 16 * (2 * i + m // 2))
                    v.tensor_tensor(c_st[:, m % 2, :], ps[:, 2 * (m % 2), :], sig_st[:, m % 2, :], ALU.mult)\
                        .then_inc(c_done[m % 2], 1)
                    if m == 0 and not last:
                        v.wait_ge(l_ready, START + i + 1)
                        small_matrices(i + 1, step)
                if not last:
                    scale_rows(NB + i + 1, NB + i + 2)
                assert count[0] == STEPS2 - (5 if last else 0), count[0]

            with v.Fori(0, NB - 1) as i:
                beside_vg(i, False)
            beside_vg(NB - 1, True)

            def conv_start():
                for c in range(CT):
                    v.tensor_scalar(cv[:, c, :], cin[:, c, 0:TB], conv_w[:, c, 0:1], conv_b[:, c:c + 1],
                                    ALU.mult, ALU.add).then_inc(conv_chain[c], 1)

            def conv_tap(k, n):
                for c in range(CT):
                    v.wait_ge(conv_chain[c], n)
                    v.scalar_tensor_tensor(out=cv[:, c, :], in0=cin[:, c, bass.ds(k, TB)],
                                           scalar=conv_w[:, c, bass.ds(k, 1)], in1=cv[:, c, :],
                                           op0=ALU.mult, op1=ALU.add).then_inc(conv_chain[c], 1)

            def low_z(n, z):
                for k in range(CT):
                    v.wait_ge(zhi_done, CT * n + k + 1)
                    v.tensor_tensor(t_lo[:, CT + k, :], z[:, k, :], t_hi[:, CT + k, :].bitcast(F32),
                                    ALU.subtract).then_inc(zlo_done, 1)

            def deviations(n):
                v.wait_ge(mean_ready, n + 1)
                for k in range(CT):
                    v.tensor_tensor(cv[:, k, :], cv[:, k, :], ps[:, 6, :], ALU.subtract).then_inc(dev_done, 1)

            def normalise(n):
                v.wait_ge(lstd_ready, n + 1)
                v.reciprocal(ln_rstd, ln_std).then_inc(ln_chain, 1)
                v.wait_ge(ln_chain, n + 1)
                v.wait_ge(sq_done, CT * n + CT)
                v.wait_ge(dev_done, CT * n + CT)
                for k in range(CT):
                    v.tensor_tensor(cv[:, k, :], cv[:, k, :], ln_rstd, ALU.mult).then_inc(norm_done, 1)

            def conv_parts(n):
                for k in range(CT):
                    v.wait_ge(silu_done, CT * n + k + 1)
                    v.tensor_copy(t_hi[:, k, :], cv[:, k, :]).then_inc(chi_done, 1)
                for k in range(CT):
                    v.wait_ge(chi_done, CT * n + k + 1)
                    v.tensor_tensor(t_lo[:, k, :], cv[:, k, :], t_hi[:, k, :].bitcast(F32), ALU.subtract)\
                        .then_inc(c_split, 1)

            def s5_parts(b, n, at, z):
                natural = lambda t: t.rearrange("p (c j) -> p j c", j=CH)
                steps = lambda t: t.rearrange("p (j c) -> p j c", j=CH)
                for k in range(CT):
                    v.wait_ge(gate_done, CT * n + k + 1)
                    v.tensor_tensor(sg[:, k, :], sg[:, k, :], z[:, k, :], ALU.mult).then_inc(s_done, 1)
                u = at + 1
                v.wait_ge(used[u % RING], START + USE_BLK + PER_BLK * b + u // RING + 1)
                for k in range(CT):
                    v.wait_ge(s_done, CT * n + k + 1)
                    v.tensor_copy(natural(t_hi[:, CT + k, :]), steps(sg[:, k, :])).then_inc(shi_done, 1)
                for k in range(CT):
                    v.wait_ge(shi_done, CT * n + k + 1)
                    v.tensor_tensor(natural(t_lo[:, CT + k, :]), steps(sg[:, k, :]),
                                    natural(t_hi[:, CT + k, :].bitcast(F32)), ALU.subtract)\
                        .then_inc(s_split, 1)

            v.wait_ge(cin_landed, 16)
            conv_start()
            with v.Fori(1, 13) as k:
                conv_tap(k, k)
            low_z(0, z_first)
            with v.Fori(13, 17) as k:
                conv_tap(k, k)
            s5_parts(0, 0, 0, z_first)
            with v.Fori(17, DVE_TAPS) as k:
                conv_tap(k, k)
            v.wait_ge(conv_pe, 1)
            for c in range(CT):
                v.wait_ge(conv_chain[c], DVE_TAPS)
                v.tensor_tensor(cv[:, c, :], cv[:, c, :], ps[:, CONV_BANKS[c], :], ALU.add)\
                    .then_inc(conv_chain[c], 1)
            for c in range(CT):
                v.wait_ge(conv_chain[c], DVE_TAPS + 1)
                v.sem_inc(conv_chain[c], PE_TAPS - 1)
            v.nop().then_inc(conv_done, 1)
            deviations(0)
            normalise(0)
            conv_parts(0)
            v.wait_ge(gp_in, 32)
            bank2 = lambda n: ps[:, 2 * n:2 * n + 2, :].rearrange("p a n -> p (a n)")

            def block_dve(b, last):
                it = 2 * NB + b
                made3 = [2 * NB]

                def invert(which, n, ready):
                    v.wait_ge(ready, NT * b + n + 1)
                    v.reciprocal(rstd[:, which, n:n + 1], std[:, which, n:n + 1]).then_inc(rstd_ready, 1)
                    made3[0] += 1
                    v.wait_ge(rstd_ready, made3[0] + 12 * b)

                def residual(which, n, gain, ready):
                    invert(which, n, ready)
                    at = NT * (which // 2) + n
                    v.wait_ge(rows_added, START + 2 * NT * b + at)
                    v.scalar_tensor_tensor(out=tmp, in0=bank2(n), scalar=rstd[:, which, n:n + 1],
                                           in1=gain[:], op0=ALU.mult, op1=ALU.mult).then_inc(tmp_made, 1)
                    v.wait_ge(tmp_made, NT + 2 * NT * b + at + 1)
                    if which == 0:
                        v.wait_ge(x_landed[n], 16 * (it + 1))
                    v.tensor_tensor(xb[:, n, :], xb[:, n, :], tmp, ALU.add).then_inc(rows_added, 1)

                for n in range(NT + 1):
                    if n < NT:
                        residual(0, n, gp_mix, mix_std)
                    if n:
                        invert(1, n - 1, x1_std)
                        v.tensor_scalar(xn[:, n - 1, :], xb[:, n - 1, :], rstd[:, 1, n - 1:n], None, ALU.mult)\
                            .then_inc(rows_ready, 1)
                evacuate_lo(it, g_ffn, 4)

                def hidden(m, w, n):
                    v.wait_ge(silu_h, FT * b + m + 1)
                    v.tensor_tensor(act_t[:, w, :], act_t[:, w, :], ps[:, 2 * w + 1, :], ALU.mult)\
                        .then_inc(hid_made[w], 1)
                    v.wait_ge(hid_made[w], n + 1)
                    v.tensor_copy(hid_hi[:, bass.ds(m, 1), :].rearrange("p a n -> p (a n)"), act_t[:, w, :])\
                        .then_inc(hid_hi_done[w], 1)
                    v.wait_ge(hid_hi_done[w], n + 1)
                    v.tensor_tensor(hid_lo[:, bass.ds(m, 1), :].rearrange("p a n -> p (a n)"), act_t[:, w, :],
                                    hid_hi[:, bass.ds(m, 1), :].bitcast(F32).rearrange("p a n -> p (a n)"),
                                    ALU.subtract).then_inc(hid_done[w], 1)

                def hidden_pairs(t0, t1, conv):
                    with v.Fori(t0, t1) as t:
                        for w in range(2):
                            hidden(2 * t + w, w, FT // 2 * b + t)
                            if conv:
                                for k in ((1, 2), (3, 4, 5))[w]:
                                    conv_tap(CONV_TAPS * t + k, TAPS * (b + 1) + CONV_TAPS * t + k)

                if last:
                    hidden_pairs(0, FT // 2, False)
                else:
                    v.wait_ge(cin_landed, 16 * (b + 2))
                    conv_start()
                    hidden_pairs(0, CONV_TURNS, True)
                    for c in range(CT):
                        v.wait_ge(conv_chain[c], TAPS * (b + 2))
                    v.nop().then_inc(conv_done, 1)
                    hidden_pairs(CONV_TURNS, DEV_AT, False)
                    deviations(b + 1)
                    hidden_pairs(DEV_AT, FT // 2, False)
                    low_z(b + 1, z_next)
                    v.wait_ge(hid_done[1], START + FT // 2 * (b + 1))
                    normalise(b + 1)
                    s5_parts(b, b + 1, GLU_AT, z_next)
                    conv_parts(b + 1)
                for n in range(NT):
                    residual(2, n, gp_ffn, ffn_std)

            with v.Fori(0, NB - 1) as b:
                block_dve(b, False)
            block_dve(NB - 1, True)

        @block.tensor
        def _(pe_):
            for s in (*used, l_ready, y_ready):
                pe_.sem_inc(s, START)
            def split_product(o, slot_w, act_hi, act_lo, weights_first, start, stop):
                whi, wlo = slot_w
                if weights_first:
                    parts = ((whi, act_hi), (whi, act_lo), (wlo, act_hi))
                else:
                    parts = ((act_hi, whi), (act_hi, wlo), (act_lo, whi))
                for n, (l, r) in enumerate(parts):
                    last = pe_.matmul(o, l, r, start=start and n == 0, stop=stop and n == 2)
                return last

            pe_.wait_ge(ident_ready, 1)
            pe_.wait_ge(prm_in, 1)
            for n in range(3):
                pe_.transpose(ps[:, 0, n * G:(n + 1) * G], prm[:, n].rearrange("g d p -> g (d p)"),
                              ident[0:G, 0:G])
            for ri in range(2):
                for o in range(4):
                    pe_.transpose(ps[:, 1 + ri, o * P:(o + 1) * P],
                                  c_raw[:, ri, o].rearrange("q d p -> q (d p)"), ident[:])
            for c in range(CT):
                last = pe_.transpose(ps[:, 3, c * TAPS:(c + 1) * TAPS], cw_raw[:, c * P:(c + 1) * P],
                                     ident[0:TAPS, 0:TAPS])
            last.then_inc(prm_t, 1)

            def transpose_rows(it, rows, banks=2, part=range(KD)):
                pe_.wait_ge(rows_ready, NT * (it + 1))
                for k in part:
                    if k < banks:
                        pe_.wait_ge(lo_done, START + KD * it)
                    else:
                        pe_.wait_ge(lo_done, START + KD * it + k - banks + 1)
                    for n in range(NT):
                        last = pe_.transpose(ps[:, 4 + k % banks, n * P:(n + 1) * P], rows[:, n, k * P:(k + 1) * P],
                                             ident[:])
                    last.then_inc(tp_ready, 1)

            def project(slot, n, bank, it, first):
                pe_.wait_ge(split_done[slot], START + n + 1)
                wh = w_hi[:, slot, :].rearrange("p (k m) -> p k m", k=KD)
                wl = w_lo[:, slot, :].rearrange("p (k m) -> p k m", k=KD)
                for k in range(KD):
                    if first:
                        pe_.wait_ge(lo_done, START + KD * it + k + 1)
                    last = split_product(ps[:, bank, :], (wh[:, k], wl[:, k]), t_hi[:, k, :], t_lo[:, k, :], True,
                                         k == 0, k == KD - 1)
                return last.then_inc(used[slot], 1)

            with pe_.Fori(0, NB) as i:
                transpose_rows(i, xb, 4)
                for m in range(CT):
                    pe_.wait_ge(u_evac[m], START + i)
                    project(m, i, m, i, m == 0)

            def s5_matrices(q):
                pe_.wait_ge(gg_ready, q + 1)
                for r in range(4):
                    pe_.wait_ge(e_evac, START + 4 * q + r)
                    for n in range(4):
                        last = pe_.transpose(ps[:, 6, n * P:(n + 1) * P],
                                             gg[:, r // 2, 4 * (r % 2) + n].rearrange("p h j -> p (h j)"), ident[:])
                    last.then_inc(et_ready, 1)
                pe_.wait_ge(l_evac, START + q)
                if not isinstance(q, int):
                    pe_.wait_ge(l_half, q)
                pe_.wait_ge(cq_ready, q + 1)
                flat = lambda t: t.rearrange("p a b -> p (a b)")
                for g in range(GQ):
                    at = 2 * H * g
                    for ri in range(2):
                        pe_.matmul(ps[:, 7, at:at + 2 * H], flat(gg[:, ri, g]), flat(ccq[:, ri, g]), start=ri == 0,
                                   stop=ri == 1)
                    at = 2 * H * GQ + H * g
                    for ri in range(2):
                        last = pe_.matmul(ps[0:H, 7, at:at + H], bbq[:, ri, g],
                                          cc[:, 2 * ri, bass.ds(GQ * q + g, 1)].rearrange("p a h -> p (a h)"),
                                          start=ri == 0, stop=ri == 1)
                last.then_inc(l_ready, 1)

            s5_matrices(0)

            def value_gate(i, u):
                m, w = divmod(u, 2)
                if w == 0:
                    pe_.wait_ge(c_done[m % 2], START + 2 * i + m // 2)
                project(u % RING, USE_VG + 2 * i + u // RING, 2 * (m % 2) + w, NB + i, u == 0)

            def beside_vg(i, last_one):
                transpose_rows(NB + i, xb, part=range(2))
                pe_.wait_ge(u_landed, 16 * (i + 1))
                for r in range(4):
                    for ri in range(2):
                        if r == 0:
                            pe_.wait_ge(z_done, START + 4 * i)
                            pe_.wait_ge(e_evac, START + 4 * i + 4)
                            pe_.wait_ge(l_half, i + 1)
                            pe_.wait_ge(l_evac, START + i + 1)
                        else:
                            pe_.wait_ge(st_fwd, 8 * i + 2 * (r - 1) + ri + 1)
                            pe_.wait_ge(st_bwd, 8 * i + 2 * (r - 1) + ri + 1)
                        for n in range(2):
                            last = pe_.matmul(ps[:, 6 + ri, n * NC:(n + 1) * NC], e_sb[:, ri, 2 * r + n],
                                              u_sb[:, 2 * r + n], start=True, stop=True)
                        last.then_inc(st_ready, 1)
                transpose_rows(NB + i, xb, part=range(2, KD))
                for u in range(2 * CT):
                    if u == 4 and not last_one:
                        pe_.wait_ge(st_fwd, 8 * i + 8)
                        pe_.wait_ge(st_bwd, 8 * i + 8)
                        s5_matrices(i + 1)
                    value_gate(i, u)
                pe_.wait_ge(m_laid, i + 1)
                pe_.wait_ge(f_ready, i + 1)
                pe_.wait_ge(fixed, START + i + 1)
                for r in range(4):
                    if r < 2:
                        if last_one:
                            pe_.wait_ge(st_fwd, 8 * i + 8)
                            pe_.wait_ge(st_bwd, 8 * i + 8)
                        else:
                            pe_.wait_ge(e_evac, START + 4 * i + 8)
                            pe_.wait_ge(l_half, i + 2)
                            pe_.wait_ge(l_evac, START + i + 2)
                    else:
                        pe_.wait_ge(z_done, START + 4 * i + r - 1)
                    for n in range(2):
                        g = 2 * r + n
                        o = ps[:, 6 + r % 2, n * NC:(n + 1) * NC]
                        pe_.matmul(o, m_sb[:, g], u_sb[:, g], start=True, stop=False)
                        for ri in range(2):
                            last = pe_.matmul(o, f_sb[:, ri, g].rearrange("p h j -> p (h j)"),
                                               x_sb[:, ri, g, 1:NC + 1], start=False, stop=ri == 1)
                    last.then_inc(y_ready, 1)

            with pe_.Fori(0, NB - 1) as i:
                beside_vg(i, False)
            beside_vg(NB - 1, True)
            for m in range(2):
                pe_.wait_ge(c_done[m], START + 2 * NB)
            pe_.wait_ge(z_done, START + 4 * NB)
            pe_.wait_ge(pool_consts, 3)

            def glu(b, n, at):
                for w in range(GLU_UNITS):
                    u = at + w
                    slot = u % RING
                    pe_.wait_ge(split_done[slot], START + USE_BLK + PER_BLK * b + u // RING + 1)
                    wh = w_hi[:, slot, :].rearrange("p (k m) -> p k m", k=CT)
                    wl = w_lo[:, slot, :].rearrange("p (k m) -> p k m", k=CT)
                    for mm in range(2):
                        cols = slice(mm * P, (mm + 1) * P)
                        for k in range(CT):
                            if w == 0 and mm == 0:
                                pe_.wait_ge(zlo_done, CT * n + k + 1)
                            last = split_product(ps[:, 4 * w + mm, :], (wh[:, k, cols], wl[:, k, cols]),
                                                 t_hi[:, CT + k, :], t_lo[:, CT + k, :], True, k == 0, k == CT - 1)
                    last.then_inc(used[slot], 1)

            def channel_mean(n):
                pe_.wait_ge(conv_done, n + 1)
                for k in range(CT):
                    last = pe_.matmul(ps[:, 6, :], mean_w[:], cv[:, k, :], start=k == 0, stop=k == CT - 1)
                last.then_inc(mean_ready, 1)

            def channel_variance(n):
                for k in range(CT):
                    pe_.wait_ge(sq_done, CT * n + k + 1)
                    last = pe_.matmul(ps[:, 7, :], mean_w[:], sg[:, k, :], start=k == 0, stop=k == CT - 1)
                last.then_inc(var_ready, 1)

            pe_.wait_ge(cin_landed, 16)
            for j in range(PE_TAPS):
                if j == PE_TAPS // 2:
                    glu(0, 0, 0)
                pe_.wait_ge(diag_ready, CT * (j + 1))
                k = DVE_TAPS + j
                for c in range(CT):
                    last = pe_.matmul(ps[:, CONV_BANKS[c], :], diag[:, j, c], cin[:, c, k:k + TB], start=j == 0,
                                      stop=j == PE_TAPS - 1)
            last.then_inc(conv_pe, 1)
            channel_mean(0)
            channel_variance(0)

            def block_pe(b, last_one):
                it = 2 * NB + b
                use = USE_BLK + PER_BLK * b

                def rows_product(units, at, act_of, ready, free, done):
                    total = sum(len(x_) for x_ in units)
                    n0 = 0
                    for group in units:
                        for tt_ in range(NT):
                            if n0 == 0:
                                free(tt_)
                            for j, k in enumerate(group):
                                u = at + k
                                slot = u % RING
                                if tt_ == 0:
                                    pe_.wait_ge(split_done[slot], START + use + u // RING + 1)
                                    ready(k)
                                toks = slice(tt_ * P, (tt_ + 1) * P)
                                hi_, lo_ = act_of(k)
                                for a in range(2):
                                    cols = slice(a * TB, (a + 1) * TB)
                                    last = split_product(ps[:, 2 * tt_ + a, :],
                                                         (w_hi[:, slot, cols], w_lo[:, slot, cols]),
                                                         hi_[:, toks], lo_[:, toks], False, n0 + j == 0,
                                                         n0 + j == total - 1)
                                if tt_ == NT - 1:
                                    last.then_inc(used[slot], 1)
                            if group is units[-1] and tt_ < NT - 1:
                                last.then_inc(done, 1)
                        n0 += len(group)

                def mixed_in(n):
                    k = WOUT_ROWS[n]
                    if k < CT:
                        pe_.wait_ge(c_split, CT * b + k + 1)
                    else:
                        pe_.wait_ge(s_split, CT * b + k - CT + 1)

                def mixed_free(tt_):
                    pe_.wait_ge(tmp_made, 2 * NT * b + tt_ + 1)
                    if tt_ == NT - 1:
                        pe_.wait_ge(lstd_ready, b + 1)

                ends = lambda n, e: [[0, 1], *([k] for k in range(2, n - e)), [*range(n - e, n)]]
                rows_product(ends(KD, 3), WOUT_AT, lambda k: (t_hi[:, WOUT_ROWS[k], :], t_lo[:, WOUT_ROWS[k], :]),
                             mixed_in, mixed_free, mixed_ready)
                transpose_rows(it, xn, 4)

                def gate_up(t0, t1):
                    with pe_.Fori(t0, t1) as t:
                        pe_.wait_ge(lo_done, START + KD * (it + 1))
                        for w in range(2):
                            pe_.wait_ge(hid_done[w], START + FT // 2 * b + t)
                            for a in range(2):
                                u = FFN_AT + 2 * w + a
                                project(u % RING, use + u // RING + t, 2 * w + a, it, False)

                if last_one:
                    gate_up(0, FT // 2)
                    down_at = GLU_AT
                else:
                    gate_up(0, MEAN_AT)
                    channel_mean(b + 1)
                    gate_up(MEAN_AT, FT // 2)
                    channel_variance(b + 1)
                    pe_.wait_ge(hid_done[0], START + FT // 2 * (b + 1))
                    glu(b, b + 1, GLU_AT)
                    down_at = GLU_AT + GLU_UNITS

                def down_free(tt_):
                    if tt_ == 0:
                        for w in range(2):
                            pe_.wait_ge(hid_done[w], START + FT // 2 * (b + 1))
                    if not last_one and tt_ != 1:
                        pe_.wait_ge(*{0: (gate_done, CT * (b + 1) + 2), 2: (gate_done, CT * (b + 2)),
                                      3: (lstd_ready, b + 2)}[tt_])

                rows_product(ends(FT, 2), down_at, lambda k: (hid_hi[:, k, :], hid_lo[:, k, :]), lambda k: None,
                             down_free, down_tile)

            with pe_.Fori(0, NB - 1) as b:
                block_pe(b, False)
            block_pe(NB - 1, True)


_INS = ["x", "mix_norm_pre", "mix_norm_post", "w_in", "conv_dw_w", "conv_dw_b", "conv_ln_g", "conv_ln_b",
        "ssm_a_re", "ssm_a_im", "ssm_log_dt", "ssm_b_re", "ssm_b_im", "ssm_c_re", "ssm_c_im", "ssm_d",
        "ssm_glu_w", "ssm_glu_b", "w_out", "ffn_norm_pre", "ffn_norm_post", "ffn_w_gate", "ffn_w_up",
        "ffn_w_down"]


def kernel(**inputs):
    import numpy as _np
    import concourse.bacc as _bacc
    from concourse import mybir as _mybir
    from concourse.bass_utils import run_bass_kernel_spmd as _run

    nc = _bacc.Bacc("TRN2", target_bir_lowering=False, num_devices=1, dynamic_dma_scratch_size=1024)
    arrays, args = {}, []
    for name in _INS:
        a = _np.ascontiguousarray(inputs[name])
        arrays[f"in_{name}_dram"] = a
        args.append(nc.dram_tensor(f"in_{name}_dram", a.shape, _mybir.dt.from_np(a.dtype), kind="ExternalInput").ap())
    shape = inputs["x"].shape
    args.append(nc.dram_tensor("out_dram", shape, _mybir.dt.float32, kind="ExternalOutput").ap())
    hybrid_encoder(nc, *args)
    r = _run(nc, [arrays], core_ids=[0])
    return r.results[0]["out_dram"]
```
